# Optimizing a Trainium2 kernel written in Bass

```python
import math
import jax, jax.numpy as jnp
from jax import lax
import numpy as np

D_MODEL = 2048
BATCH = 1
SEQ = 256
DEPTH = 1

SSM_WIDTH = D_MODEL // 2
SSM_GROUP = 16
SSM_GROUPS = SSM_WIDTH // SSM_GROUP
SSM_STATE = 64
ATTN_WIDTH = D_MODEL // 2
ATTN_HEADS = 8
ATTN_HEAD_DIM = ATTN_WIDTH // ATTN_HEADS // 2
ROPE_THETA = 10000.0
Q_BLOCK = 128
IN_WIDTH = SSM_WIDTH + 3 * ATTN_WIDTH + 2 * D_MODEL
N_GROUPS = 4
EXPERTS_PER_GROUP = 8
N_EXPERTS = N_GROUPS * EXPERTS_PER_GROUP
TOP_K = 2
D_FF_EXPERT = D_MODEL // 4
MOE_BLOCK = 128
NORM_EPS = 1e-6
SUBLN_EPS = 1e-5

kernel_name = "hybrid_s5_diffattn_hmoe_block"

def rms_norm(x, w, eps=NORM_EPS):
    xf = x.astype(jnp.float32)
    y = xf * lax.rsqrt(jnp.mean(xf * xf, axis=-1, keepdims=True) + eps)
    return (y * w.astype(jnp.float32)).astype(x.dtype)

def lambda_init_fn(layer_idx):
    return 0.8 - 0.6 * math.exp(-0.3 * layer_idx)

def s5_branch(u, lam_re, lam_im, log_dt, b_re, b_im, c_re, c_im, d_skip, glu_w, glu_b):
    bsz, seq = u.shape[0], u.shape[1]
    f32 = jnp.float32
    uf = u.astype(f32).reshape(bsz, seq, SSM_GROUPS, SSM_GROUP)
    lr = lam_re.astype(f32)
    li = lam_im.astype(f32)
    dt = jnp.exp(log_dt.astype(f32))[:, None]
    mag = jnp.exp(lr * dt)
    abar_re = mag * jnp.cos(li * dt)
    abar_im = mag * jnp.sin(li * dt)
    nr = abar_re - 1.0
    ni = abar_im
    den = lr * lr + li * li
    f_re = (nr * lr + ni * li) / den
    f_im = (ni * lr - nr * li) / den
    br = b_re.astype(f32)
    bi = b_im.astype(f32)
    bbar_re = f_re[..., None] * br - f_im[..., None] * bi
    bbar_im = f_re[..., None] * bi + f_im[..., None] * br
    bu_re = jnp.einsum('bsgm,gpm->bsgp', uf, bbar_re)
    bu_im = jnp.einsum('bsgm,gpm->bsgp', uf, bbar_im)
    a_re = jnp.broadcast_to(abar_re, bu_re.shape)
    a_im = jnp.broadcast_to(abar_im, bu_im.shape)

    def combine(e1, e2):
        a1r, a1i, b1r, b1i = e1
        a2r, a2i, b2r, b2i = e2
        return (a2r * a1r - a2i * a1i,
                a2r * a1i + a2i * a1r,
                a2r * b1r - a2i * b1i + b2r,
                a2r * b1i + a2i * b1r + b2i)

    _, _, x_re, x_im = lax.associative_scan(combine, (a_re, a_im, bu_re, bu_im), axis=1)
    y = (jnp.einsum('bsgp,gmp->bsgm', x_re, c_re.astype(f32))
         - jnp.einsum('bsgp,gmp->bsgm', x_im, c_im.astype(f32)))
    y = y.reshape(bsz, seq, SSM_WIDTH) + d_skip.astype(f32) * uf.reshape(bsz, seq, SSM_WIDTH)
    y = jax.nn.gelu(y)
    y = y * jax.nn.sigmoid(y @ glu_w.astype(f32) + glu_b.astype(f32))
    return y.astype(u.dtype)

def rope_cos_sin(positions, dim):
    inv_freq = 1.0 / (ROPE_THETA ** (jnp.arange(0, dim, 2, dtype=jnp.float32) / dim))
    ang = positions.astype(jnp.float32)[..., None] * inv_freq
    return jnp.cos(ang)[:, :, None, None, :], jnp.sin(ang)[:, :, None, None, :]

def apply_rope(t, cos, sin):
    half = t.shape[-1] // 2
    t1, t2 = t[..., :half], t[..., half:]
    return jnp.concatenate([t1 * cos - t2 * sin, t2 * cos + t1 * sin], axis=-1)

def diff_attention(q, k, v, positions, lam_q1, lam_k1, lam_q2, lam_k2, subln_w, lambda_init):
    bsz, seq = q.shape[0], q.shape[1]
    f32 = jnp.float32
    hd = ATTN_HEAD_DIM
    cos, sin = rope_cos_sin(positions, hd)
    qf = apply_rope(q.astype(f32).reshape(bsz, seq, ATTN_HEADS, 2, hd), cos, sin)
    kf = apply_rope(k.astype(f32).reshape(bsz, seq, ATTN_HEADS, 2, hd), cos, sin)
    vf = v.astype(f32).reshape(bsz, seq, ATTN_HEADS, 2 * hd)
    lam = (jnp.exp(jnp.sum(lam_q1.astype(f32) * lam_k1.astype(f32)))
           - jnp.exp(jnp.sum(lam_q2.astype(f32) * lam_k2.astype(f32))) + lambda_init)
    n_blk = seq // Q_BLOCK
    q_blocks = jnp.moveaxis(qf.reshape(bsz, n_blk, Q_BLOCK, ATTN_HEADS, 2, hd), 1, 0)
    key_pos = jnp.arange(seq)
    scale = hd ** -0.5

    def block(args):
        qb, bi = args
        s = jnp.einsum('bqhcd,bkhcd->bhcqk', qb, kf) * scale
        q_pos = bi * Q_BLOCK + jnp.arange(Q_BLOCK)
        mask = key_pos[None, :] <= q_pos[:, None]
        s = jnp.where(mask, s, -jnp.inf)
        p = jax.nn.softmax(s, axis=-1)
        a = p[:, :, 0] - lam * p[:, :, 1]
        return jnp.einsum('bhqk,bkhe->bqhe', a, vf)

    o = lax.map(block, (q_blocks, jnp.arange(n_blk)))
    o = jnp.moveaxis(o, 0, 1).reshape(bsz, seq, ATTN_HEADS, 2 * hd)
    o = o * lax.rsqrt(jnp.mean(o * o, axis=-1, keepdims=True) + SUBLN_EPS)
    o = o * subln_w.astype(f32) * (1.0 - lambda_init)
    return o.reshape(bsz, seq, ATTN_WIDTH).astype(q.dtype)

def hierarchical_moe(h, router_group_w, router_expert_w, w_gate, w_up, w_down):
    bsz, seq, dm = h.shape
    n_tok = bsz * seq
    f32 = jnp.float32
    hf = h.reshape(n_tok, dm)
    hf32 = hf.astype(f32)
    g_logits = hf32 @ router_group_w.astype(f32)
    g_prob = jax.nn.softmax(g_logits, axis=-1)
    g_val, g_idx = lax.top_k(g_prob, 1)
    e_logits = (hf32 @ router_expert_w.astype(f32)).reshape(n_tok, N_GROUPS, EXPERTS_PER_GROUP)
    e_sel = jnp.take_along_axis(e_logits, g_idx[:, :, None], axis=1)[:, 0]
    e_val, e_idx = lax.top_k(e_sel, TOP_K)
    gate = jax.nn.softmax(e_val, axis=-1) * g_val
    expert_id = g_idx * EXPERTS_PER_GROUP + e_idx

    n_slots = n_tok * TOP_K
    e_flat = expert_id.reshape(n_slots)
    tok_flat = jnp.repeat(jnp.arange(n_tok, dtype=jnp.int32), TOP_K)
    w_flat = gate.reshape(n_slots)
    order = jnp.argsort(e_flat)
    sorted_e = e_flat[order]
    counts = jnp.bincount(e_flat, length=N_EXPERTS)
    starts = jnp.cumsum(counts) - counts
    padded = ((counts + MOE_BLOCK - 1) // MOE_BLOCK) * MOE_BLOCK
    padded_ends = jnp.cumsum(padded)
    padded_starts = padded_ends - padded
    dest = padded_starts[sorted_e] + (jnp.arange(n_slots) - starts[sorted_e])
    buf_len = n_slots + N_EXPERTS * MOE_BLOCK
    n_blocks = buf_len // MOE_BLOCK
    buf_tok = jnp.zeros((buf_len,), jnp.int32).at[dest].set(tok_flat[order])
    buf_w = jnp.zeros((buf_len,), f32).at[dest].set(w_flat[order])
    block_start = jnp.arange(n_blocks) * MOE_BLOCK
    block_e = jnp.clip(jnp.searchsorted(padded_ends, block_start, side='right'), 0, N_EXPERTS - 1)

    def expert_block(args):
        tok, e = args
        xb = hf[tok]
        a = jax.nn.silu(xb @ w_gate[e]) * (xb @ w_up[e])
        return a @ w_down[e]

    ys = lax.map(expert_block, (buf_tok.reshape(n_blocks, MOE_BLOCK), block_e))
    ys = ys.reshape(buf_len, dm)
    out = jnp.zeros((n_tok, dm), hf.dtype).at[buf_tok].add(ys * buf_w[:, None].astype(ys.dtype))
    return out.reshape(bsz, seq, dm)

def setup_inputs(seed: int = 0) -> dict:
    key = jax.random.key(seed)
    ks = jax.random.split(key, 32)
    f32 = jnp.float32
    L, D, G, P, M = DEPTH, D_MODEL, SSM_GROUPS, SSM_STATE, SSM_GROUP
    nrm = lambda k, shape, s: jax.random.normal(k, shape, f32) * s
    x = jax.random.normal(ks[0], (BATCH, SEQ, D), f32)
    positions = jnp.broadcast_to(jnp.arange(SEQ, dtype=jnp.int32), (BATCH, SEQ))
    n_idx = jnp.arange(P, dtype=f32)[None, None, :]
    return {
        "x": x,
        "positions": positions,
        "norm1_w": 1.0 + nrm(ks[1], (L, D), 0.02),
        "w_in": nrm(ks[2], (L, D, IN_WIDTH), D ** -0.5),
        "ssm_lambda_re": -0.5 + nrm(ks[3], (L, G, P), 0.01),
        "ssm_lambda_im": jnp.pi * n_idx + nrm(ks[4], (L, G, P), 0.01),
        "ssm_log_dt": jax.random.uniform(ks[5], (L, G), f32, math.log(1e-3), math.log(1e-1)),
        "ssm_b_re": nrm(ks[6], (L, G, P, M), (2 * M) ** -0.5),
        "ssm_b_im": nrm(ks[7], (L, G, P, M), (2 * M) ** -0.5),
        "ssm_c_re": nrm(ks[8], (L, G, M, P), P ** -0.5),
        "ssm_c_im": nrm(ks[9], (L, G, M, P), P ** -0.5),
        "ssm_d": nrm(ks[10], (L, SSM_WIDTH), 0.5),
        "ssm_glu_w": nrm(ks[11], (L, SSM_WIDTH, SSM_WIDTH), SSM_WIDTH ** -0.5),
        "ssm_glu_b": nrm(ks[12], (L, SSM_WIDTH), 0.01),
        "attn_lambda_q1": nrm(ks[13], (L, ATTN_HEAD_DIM), 0.1),
        "attn_lambda_k1": nrm(ks[14], (L, ATTN_HEAD_DIM), 0.1),
        "attn_lambda_q2": nrm(ks[15], (L, ATTN_HEAD_DIM), 0.1),
        "attn_lambda_k2": nrm(ks[16], (L, ATTN_HEAD_DIM), 0.1),
        "attn_subln_w": 1.0 + nrm(ks[17], (L, 2 * ATTN_HEAD_DIM), 0.02),
        "w_proj_ssm": nrm(ks[18], (L, SSM_WIDTH, D), SSM_WIDTH ** -0.5),
        "w_proj_attn": nrm(ks[19], (L, ATTN_WIDTH, D), ATTN_WIDTH ** -0.5),
        "w_out": nrm(ks[20], (L, D, D), D ** -0.5),
        "norm2_w": 1.0 + nrm(ks[21], (L, D), 0.02),
        "router_group_w": nrm(ks[22], (L, D, N_GROUPS), D ** -0.5),
        "router_expert_w": nrm(ks[23], (L, D, N_EXPERTS), D ** -0.5),
        "expert_w_gate": nrm(ks[24], (L, N_EXPERTS, D, D_FF_EXPERT), D ** -0.5),
        "expert_w_up": nrm(ks[25], (L, N_EXPERTS, D, D_FF_EXPERT), D ** -0.5),
        "expert_w_down": nrm(ks[26], (L, N_EXPERTS, D_FF_EXPERT, D), D_FF_EXPERT ** -0.5),
        "final_norm_w": 1.0 + nrm(ks[27], (D,), 0.02),
    }

def reference(x, positions, norm1_w, w_in, ssm_lambda_re, ssm_lambda_im, ssm_log_dt,
              ssm_b_re, ssm_b_im, ssm_c_re, ssm_c_im, ssm_d, ssm_glu_w, ssm_glu_b,
              attn_lambda_q1, attn_lambda_k1, attn_lambda_q2, attn_lambda_k2, attn_subln_w,
              w_proj_ssm, w_proj_attn, w_out, norm2_w, router_group_w, router_expert_w,
              expert_w_gate, expert_w_up, expert_w_down, final_norm_w):
    o_q = SSM_WIDTH
    o_k = o_q + ATTN_WIDTH
    o_v = o_k + ATTN_WIDTH
    o_gs = o_v + ATTN_WIDTH
    o_ga = o_gs + D_MODEL
    for l in range(DEPTH):
        h = rms_norm(x, norm1_w[l])
        z = h @ w_in[l]
        u = z[..., :o_q]
        q = z[..., o_q:o_k]
        k = z[..., o_k:o_v]
        v = z[..., o_v:o_gs]
        g_ssm = jax.nn.sigmoid(z[..., o_gs:o_ga])
        g_attn = jax.nn.sigmoid(z[..., o_ga:])
        y_ssm = s5_branch(u, ssm_lambda_re[l], ssm_lambda_im[l], ssm_log_dt[l],
                          ssm_b_re[l], ssm_b_im[l], ssm_c_re[l], ssm_c_im[l],
                          ssm_d[l], ssm_glu_w[l], ssm_glu_b[l])
        y_attn = diff_attention(q, k, v, positions, attn_lambda_q1[l], attn_lambda_k1[l],
                                attn_lambda_q2[l], attn_lambda_k2[l], attn_subln_w[l],
                                lambda_init_fn(l))
        merged = g_ssm * (y_ssm @ w_proj_ssm[l]) + g_attn * (y_attn @ w_proj_attn[l])
        x = x + merged @ w_out[l]
        h2 = rms_norm(x, norm2_w[l])
        x = x + hierarchical_moe(h2, router_group_w[l], router_expert_w[l],
                                 expert_w_gate[l], expert_w_up[l], expert_w_down[l])
    return rms_norm(x, final_norm_w)


_drawn_inputs = setup_inputs


def setup_inputs(seed=0):
    import zlib

    import numpy as np

    out = dict(_drawn_inputs(seed))
    spreads = {}
    factors = {'ssm_lambda_re': 64.0,
     'ssm_lambda_im': 10.016,
     'ssm_b_im': 15.195,
     'ssm_c_re': 14.925,
     'ssm_glu_b': 64.0,
     'attn_subln_w': 3.46,
     'final_norm_w': 7.997,
     'ssm_log_dt': 4.303,
     'ssm_b_re': 7.966,
     'ssm_c_im': 6.75,
     'ssm_glu_w': 5.145,
     'norm2_w': 3.405}
    for name, (base, spread) in spreads.items():
        noise = np.random.default_rng([zlib.crc32(name.encode()), seed]).standard_normal(out[name].shape)
        drawn = base * np.exp(spread * noise) if base else spread * noise
        out[name] = __import__('jax').numpy.asarray(drawn.astype(out[name].dtype))
    for name, factor in factors.items():
        out[name] = (out[name] * factor).astype(out[name].dtype)
    return out
```

```python
from contextlib import ExitStack

import concourse.bass as bass
from concourse import mybir

F32 = mybir.dt.float32
I32 = mybir.dt.int32
U32 = mybir.dt.uint32
ALU = mybir.AluOpType
ACT = mybir.ActivationFunctionType
AX = mybir.AxisListType

P = 128
D = 2048
T = 256
TT = T // P
KT = D // P
W = 1024
WK = W // P
BLK = 512
CH = 8
CHF = CH * BLK
SLOTS = 6
DENSE_SLOTS = 3
G, SP_, SM = 64, 64, 16
PR = G // 2
L = 8
NJ = T // L
NQ = 4
QP = PR // NQ
H, HD = 8, 64
NG, EPG, NE = 4, 8, 32
F = 512
FK = F // P
CAP = 32
MAXI = 48
NORM_EPS, SUBLN_EPS = 1e-6, 1e-5
LAMBDA_INIT = 0.2
SCALE = HD ** -0.5
NEG = -1.0e30
ROUND = 12582912.0
INV_2PI = 0.15915494309189535
C1 = 6.28125
C2 = 0.0019350051879882812
C3 = 3.0199157663412e-07
PI = 3.1415925
GELU_C = 0.044715
GELU_S = 1.5957691216057308


def bc(ap, axis, n):
    a = ap.unsqueeze(axis)
    s = list(a.shape)
    s[axis] = n
    return a.to_broadcast(s)


class Steps:

    def __init__(self, eng, sem):
        self.eng, self.sem, self.n = eng, sem, 0

    def __call__(self, ins):
        ins.then_inc(self.sem, 1)
        self.n += 1
        self.eng.wait_ge(self.sem, self.n)


def hybrid_block(nc, a, out, upto=99, dbg=None):
    ctx = ExitStack()
    with ctx:
        def sb(name, shape, dt=F32):
            return ctx.enter_context(nc.sbuf_tensor(name, shape, dt))

        def sem(name):
            return ctx.enter_context(nc.semaphore(name))

        ring = sb("ring", [P, DENSE_SLOTS * CHF])
        s3 = sb("s3", [P, CHF])
        r45 = sb("r45", [P, 2 * CHF])
        xa = sb("xa", [P, TT * D])
        ht = sb("ht", [P, KT * T])
        z = sb("z", [P, TT * 4096])
        st = sb("st", [P, (NJ + 1) * 2 * PR])
        ypk = sb("ypk", [P, 2048])
        sml = sb("sml", [P, 2048])
        par = sb("par", [P, 1056])
        bcw = sb("bcw", [P, 2048])
        rw = sb("rw", [P, KT * (NG + NE)])
        wp = sb("wp", [P, G * SM])
        ident = sb("ident", [P, P])
        mask = sb("mask", [P, 2 * P])
        ang = sb("ang", [P, 4 * 96])
        pb = [ctx.enter_context(nc.psum_tensor(f"pb{i}", [P, BLK], F32)) for i in range(8)]

        def slot(c):
            t, c = (ring, c) if c < DENSE_SLOTS else (s3, 0) if c == 3 else (r45, c - 4)
            return t[:, c * CHF:(c + 1) * CHF]

        x_t = xa[:].rearrange("p (t d) -> p t d", t=TT)
        h_t = z[:, 0:TT * D].rearrange("p (t d) -> p t d", t=TT)
        hT = ht[:].rearrange("p (k t) -> p k t", k=KT)
        z_t = z[:].rearrange("p (t c) -> p t c", t=TT)
        bp = xa[:, 0:2048].rearrange("p (c q i m) -> p c q i m", c=2, q=QP, i=L)
        tq = xa[:, 2048:4096].rearrange("p (i x) -> p i x", i=L)
        up = xa[:, 2048:4096].rearrange("p (g i m) -> p g i m", g=16, i=L)
        bt = r45[:, 0:2048].rearrange("p (q c x) -> p q c x", q=QP, c=2)
        cbd = r45[:, 2048:4096].rearrange("p (c q h m) -> p c q h m", c=2, q=PR, h=2)
        sbd = r45[:, 0:4096].rearrange("p (c h q j) -> p c h q j", c=2, h=2, q=PR)
        ut = r45[:, 4096:6144].rearrange("p (g f j) -> p g f j", g=16, f=4)
        tmp = r45[:, 6144:8192].rearrange("p (a x) -> p a x", a=2)
        braw = sml[:, 0:1024].rearrange("p (c g q m) -> p c g q m", c=2, g=4, q=8)
        ct = sml[:, 1024:2048].rearrange("p (c g q m) -> p c g q m", c=2, g=4, q=8)
        cn = ypk[:, 0:1024].rearrange("p (c g x) -> p c g x", c=2, g=4)
        yp = ypk[:].rearrange("p (i x) -> p i x", i=L)
        st_j = st[:].rearrange("p (j c q) -> p j c q", c=2, q=PR)
        yg = st[:, 0:2048].rearrange("p (t c) -> p t c", t=TT)
        yT = ypk[:].rearrange("p (k t) -> p k t", k=WK)
        oT = sml[:].rearrange("p (k t) -> p k t", k=WK)
        o = [0]

        def pv(n):
            o[0] += n
            return par[:, o[0] - n:o[0]]

        lam3 = pv(96)
        lr, li, ldt = lam3[:, 0:32], lam3[:, 32:64], lam3[:, 64:96]
        dt_, mag, nr, den, fr, fi, pt = pv(32), pv(32), pv(32), pv(32), pv(32), pv(32), pv(64)
        apw = pv(4 * 64).rearrange("p (k c q) -> p k c q", k=4, c=2)
        a8 = pv(128)
        w1c, w2c = pv(16), pv(16)
        ss = pv(8)
        lamv = pv(8)
        assert o[0] <= 1056
        p32 = ypk[0:32, 1408:1792]
        dt32 = ypk[0:32, 1792:1794]
        invf = sb("invf", [P, 32])
        posi = sb("posi", [P, TT], I32)
        posf = sb("posf", [P, TT])
        lamw = ypk[:, 1024:1344]
        subw = sb("subw", [P, P])
        qk = z_t[:, :, W:3 * W]
        qkT = r45[:, 0:4096].rearrange("p (h t) -> p h t", h=2 * H)
        rt = ypk[:].rearrange("p (a h d) -> p a h d", a=4, h=2 * H)
        sm_ = r45[:, 4096:5120].rearrange("p (c x) -> p c x", c=2)
        ex = r45[:, 5120:6144].rearrange("p (c x) -> p c x", c=2)
        am = r45[:, 6144:6656]
        aT = r45[:, 6656:7168]
        sc8 = r45[:, 7168:7232]
        oa = xa[:, 0:2048].rearrange("p (t c) -> p t c", t=TT)
        osq = xa[:, 2048:4096].rearrange("p (t c) -> p t c", t=TT)
        gs_t = s3[:].rearrange("p (t c) -> p t c", t=TT)
        ga_t = z_t[:, :, W:3 * W]

        h2 = h_t
        gu = z[:, 4096:5120].rearrange("p (c f) -> p c f", c=2)
        ys = z[:, 5120:7168].rearrange("p (n d) -> p n d", n=4)
        xg = z[:, 7168:7680]
        aTe = z[:, 7680:7808].rearrange("p (k s) -> p k s", k=FK)
        sge = z[:, 7808:7936]
        lg = z[:, 7936:8008].rearrange("p (t e) -> p t e", t=TT)
        lt = yT[:, 0, 0:P]
        ones = yT[:, 0, P:2 * P]
        iota = yT[:, 1, 0:P].rearrange("p (a s) -> p a s", a=4)
        q32 = yT[:, 1, P:P + 32]
        thr = yT[:, 1, P + 32:P + 40]
        i48 = oT[0:1, :, :].rearrange("p k t -> p (k t)")[:, 0:MAXI * NE].rearrange("p (i e) -> p i e", i=MAXI)
        cmp48 = bcw[0:1, 0:MAXI * NE].rearrange("p (i e) -> p i e", i=MAXI)
        rs = st[:, 0:1600]
        xT = ht[:, 0:512].rearrange("p (j n s) -> p j n s", j=4, n=4)
        sel = ht[:, 512:576].rearrange("p (t s) -> p t s", t=TT)
        swr = ht[:, 576:832].rearrange("p (t a s) -> p t a s", t=TT, a=4)
        swt = ht[:, 832:1088]
        swa = ht[:, 1088:1344].rearrange("p (t a s) -> p t a s", t=TT, a=4)
        sela = ht[:, 1344:1408].rearrange("p (t s) -> p t s", t=TT)
        rem = ang[:, 0:4].rearrange("p (t k) -> p t k", t=TT)
        gw = ang[:, 4:8].rearrange("p (t k) -> p t k", t=TT)
        tabf = ang[0:1, 96:96 + 1 + MAXI]
        tab = ang[0:1, 160:160 + 1 + MAXI].bitcast(I32)
        rwv = rw[:].rearrange("p (k e) -> p k e", k=KT)

        S = {n: sem(n) for n in (
            "x_in norms_in lam_in dt_in b_in c_in consts_in bc_in rw_in ident_ok mask_ok st0_ok "
            "ss_done root_done h_done dve act pool pe_params "
            "v_ready v_free a_ready a_free hT_ok chunk_used blk_ready blk_free out_free dt_spread "
            "dt_done mag_done arg_done sin_done lamx_in_done apow_done bp_ok bp_used bt_ok ct_ok cbd_ok "
            "uqkv_done up_ok uj_in ut_ok wp_ok s_used tq_zero tq_in tq_used ca_ok ca_used sbd_ok yp_ok yp_in "
            "gel_in gel_sig gelu_ok qk_rot qkT_ok nmx_ok ex_ok am_ok aT_ok aT_used o_ok osq_ok ort_ok oa_ok gates_ok "
            "glu_pre glu_sig y2_ok yT_ok oT_ok y2T_ok mrg_ok mT_ok x_again x2_ok scan cbd_zero sbd_zero "
            "lsum_ok lexp_ok mT_ps xfree ss2_done root2_done h2_ok h2T_ok lg_ps gex_in gex_ok pex_ok m_ok cnt_ps tab_ok iota_ok fw_in "
            "sel_ok xg_ps xg_sb xt_ps xt_sb gate_ps gate_sb up_ps up_sb sum_ps sig_ok swr_ok swt_ps swt_sb at_ok dn_ps dn_sb "
            "si_ok istep sc_ps sc_free item_chunk moe_ok fss_done froot_done out_ok out_in").split()}
        full = [sem(f"slot{i}_full") for i in range(SLOTS)]

        block = ctx.enter_context(nc.Block())

        PE_A = (5, 7, 9, 11)
        PE_C = (17, 18, 19, 20)
        PE_QK = 21
        PE_ROUND = 22

        def blocks_of(wap, kt_total):
            return wap.rearrange("(p k) n -> p k n", k=kt_total)

        win = blocks_of(a["w_in"][0], KT)
        glu = blocks_of(a["ssm_glu_w"][0], WK)
        wps = blocks_of(a["w_proj_ssm"][0], WK)
        wpa = blocks_of(a["w_proj_attn"][0], WK)
        wout = blocks_of(a["w_out"][0], KT)
        x_d = a["x"][0].rearrange("(t p) d -> p t d", p=P)
        out_d = out[0].rearrange("(t p) d -> p t d", p=P)

        def chunk3(c):
            return slot(c).rearrange("p (k n) -> p k n", k=CH)

        dense = []
        for n in range(2):
            dense.append(glu[:, :, n * BLK:(n + 1) * BLK])
        for n in range(4):
            dense.append(wps[:, :, n * BLK:(n + 1) * BLK])
            dense.append(wpa[:, :, n * BLK:(n + 1) * BLK])
        for n in range(4):
            for c in range(2):
                dense.append(wout[:, c * CH:(c + 1) * CH, n * BLK:(n + 1) * BLK])
        N_WIN = 32
        N_DENSE = N_WIN + len(dense)
        EXP_SLOT = (4, 5, 3, 2, 0, 1)
        FILLS = [len(range(s, N_DENSE, DENSE_SLOTS)) for s in range(DENSE_SLOTS)] + [0, 0, 0]

        @block.sync
        def _(sp):
            for t in range(TT):
                sp.dma_start(x_t[:, t, :], x_d[:, t, :]).then_inc(S["x_in"], 16)

            for k in range(N_DENSE):
                if k >= DENSE_SLOTS:
                    sp.wait_ge(S["chunk_used"], k - DENSE_SLOTS + 1)
                if k < N_WIN:
                    b, c = k // 2, k % 2
                    src = win[:, c * CH:(c + 1) * CH, b * BLK:(b + 1) * BLK]
                else:
                    src = dense[k - N_WIN]
                sp.dma_start(chunk3(k % DENSE_SLOTS), src).then_inc(full[k % DENSE_SLOTS], 16)
                if k == 42:
                    sp.wait_ge(S["xfree"], 1)
                    for t in range(TT):
                        sp.dma_start(x_t[:, t, :], x_d[:, t, :]).then_inc(S["x_again"], 16)

            def expert_chunks(e):
                for name in ("expert_w_gate", "expert_w_up"):
                    w = a[name][0, e].rearrange("e (p k) n -> p (e k) n", k=KT)
                    for c in range(2):
                        yield w[:, c * CH:(c + 1) * CH, :], "k"
                w = a["expert_w_down"][0, e].rearrange("e (p k) n -> p (e k) n", k=FK)
                for c in range(2):
                    yield w[:, 2 * c:2 * c + 2, :], "d"

            def fill(c, src, kind):
                s_ = EXP_SLOT[c]
                dst = chunk3(s_) if kind == "k" else slot(s_).rearrange("p (k n) -> p k n", k=2)
                sp.dma_start(dst, src).then_inc(full[s_], 16)

            for c, (src, kind) in enumerate(expert_chunks(bass.ds(0, 1))):
                if c == 0:
                    sp.wait_ge(S["y2_ok"], 1)
                if c == 2:
                    sp.wait_ge(S["mT_ps"], 1)
                if c >= 3:
                    sp.wait_ge(S["chunk_used"], N_DENSE - 5 + c)
                fill(c, src, kind)
            sp.wait_ge(S["tab_ok"], 1)
            n_items = sp.value_load(tab[:, 0:1], min_val=1, max_val=MAXI)
            with sp.If(n_items > 1):
                with sp.Fori(1, n_items) as i:
                    e = sp.value_load(tab[:, bass.ds(i + 1, 1)], min_val=0, max_val=NE - 1)
                    for c, (src, kind) in enumerate(expert_chunks(bass.ds(e, 1))):
                        sp.wait_ge(S["item_chunk"], i * 6 + c - 5)
                        fill(c, src, kind)
            for t in range(TT):
                sp.wait_ge(S["out_ok"], t + 1)
                sp.dma_start(out_d[:, t, :], x_t[:, t, :]).then_inc(S["out_in"], 16)
            sp.wait_ge(S["out_in"], 16 * TT)

        @block.scalar
        def _(act):
            steps = Steps(act, S["act"])
            act.dma_start(w1c, a["norm1_w"][0].rearrange("(p k) -> p k", k=KT)).then_inc(S["norms_in"], 16)
            act.dma_start(w2c, a["norm2_w"][0].rearrange("(p k) -> p k", k=KT)).then_inc(S["norms_in"], 16)
            for n, name in enumerate(("ssm_lambda_re", "ssm_lambda_im")):
                src = a[name][0].rearrange("(g q r h) p -> q g r (h p)", g=4, q=NQ, h=2)
                for q in range(NQ):
                    act.dma_start(p32[q * 8:(q + 1) * 8, n * P:(n + 1) * P], src[q]).then_inc(S["lam_in"], 16)
            src = a["ssm_log_dt"][0].rearrange("(g q r h) -> q g r h", g=4, q=NQ, h=2)
            for q in range(NQ):
                act.dma_start(dt32[q * 8:(q + 1) * 8, :], src[q]).then_inc(S["dt_in"], 16)
            act.dma_start(invf[:], a["inv_freq"].partition_broadcast(P)).then_inc(S["consts_in"], 16)
            with nc.allow_non_contiguous_dma(reason="256 positions, one per partition"):
                act.dma_start(posi[:], a["positions"][0].rearrange("(t p) -> p t", p=P)).then_inc(S["consts_in"], 16)
            for n, name in enumerate(("q1", "k1", "q2", "k2")):
                act.dma_start(lamw[:, n * 64:(n + 1) * 64],
                              a[f"attn_lambda_{name}"][0].partition_broadcast(P)).then_inc(S["consts_in"], 16)
            act.dma_start(subw[:], a["attn_subln_w"][0].partition_broadcast(P)).then_inc(S["consts_in"], 16)
            act.wait_ge(S["x_in"], 32)
            for t in range(TT):
                act.activation(h_t[:, t, :], x_t[:, t, :], ACT.Square, accum_out=ss[:, t:t + 1]).then_inc(S["ss_done"], 1)
            act.wait_ge(S["root_done"], 1)
            act.activation(ss[:, 4:6], ss[:, 2:4], ACT.Sqrt).then_inc(S["ss_done"], 1)
            act.wait_ge(S["pe_params"], 1)
            act.activation(dt_, ldt, ACT.Exp).then_inc(S["dt_done"], 1)
            act.wait_ge(S["arg_done"], 1)
            act.activation(mag, nr, ACT.Exp).then_inc(S["mag_done"], 1)
            act.wait_ge(S["lsum_ok"], 1)
            act.activation(lamv[:, 2:4], lamv[:, 0:2], ACT.Exp).then_inc(S["lexp_ok"], 1)
            act.wait_ge(S["arg_done"], 2)
            act.activation(ang[:, 192:288], ang[:, 96:192], ACT.Sin).then_inc(S["sin_done"], 1)
            act.activation(ang[:, 288:384], ang[:, 96:192], ACT.Sin, scale=0.5).then_inc(S["sin_done"], 1)

            aj = [0]

            def a_job(out_, cols, func=ACT.Copy):
                n = aj[0]
                aj[0] += 1
                act.wait_ge(S["a_ready"], n + 1)
                act.activation(out_, pb[6 + n % 2][:, 0:cols] if len(out_.shape) == 2 else out_x(out_, n, cols),
                               func).then_inc(S["a_free"], 1)

            def out_x(out_, n, cols):
                v = pb[6 + n % 2][:, 0:cols]
                if len(out_.shape) == 3:
                    return v.rearrange("p (a b) -> p a b", a=out_.shape[1])
                return v.rearrange("p (a b c) -> p a b c", a=out_.shape[1], b=out_.shape[2])

            for c in range(2):
                a_job(ct[:, c].rearrange("p g q m -> p (g q m)"), BLK)

            def block_out(b):
                for t in range(TT):
                    act.wait_ge(S["blk_ready"], 2 * b + t + 1)
                    if b < 8:
                        dst = z_t[:, t, b * BLK:(b + 1) * BLK]
                    elif b < 12:
                        dst = gs_t[:, t, (b - 8) * BLK:(b - 7) * BLK]
                    else:
                        dst = ga_t[:, t, (b - 12) * BLK:(b - 11) * BLK]
                    act.activation(dst, pb[2 * (b % 2) + t][:], ACT.Copy if b < 8 else ACT.Sigmoid).then_inc(S["blk_free"], 1)

            def u_out():
                for n in range(4):
                    a_job(ut[:, 4 * n:4 * n + 4].rearrange("p g f j -> p (g f j)"), BLK)

            def stage_a(q):
                for h in range(4):
                    if q and h == 0:
                        act.wait_ge(S["s_used"], q)
                    a_job(bt[:, 2 * h:2 * h + 2].rearrange("p q c x -> p (q c x)"), BLK)

            def stage_c(q):
                if q == 0:
                    act.wait_ge(S["qk_rot"], 1)
                n = aj[0]
                act.wait_ge(S["a_ready"], n + 1)
                aj[0] += 1
                act.activation(yp.rearrange("p i (g m) -> p g i m", g=16)[:, 4 * q:4 * q + 4],
                               pb[6 + n % 2][:].rearrange("p (g i m) -> p g i m", g=4, i=L),
                               ACT.Copy).then_inc(S["a_free"], 1)

            def exps(r):
                nh, K = (4, P) if r < 2 else (2, 2 * P)
                act.wait_ge(S["nmx_ok"], r + 1)
                if r:
                    act.wait_ge(S["am_ok"], r)
                for c in range(2):
                    for h in range(nh):
                        act.activation(ex[:, c, h * K:(h + 1) * K], sm_[:, c, h * K:(h + 1) * K], ACT.Exp,
                                       bias=sc8[:, 8 + c * 4 + h:9 + c * 4 + h], scale=SCALE,
                                       accum_out=sc8[:, 16 + c * 4 + h:17 + c * 4 + h]).then_inc(S["ex_ok"], 1)

            def round_out(r):
                nh = 4 if r < 2 else 2
                a_job(aT, BLK)
                t = 0 if r < 2 else 1
                h0 = 4 * r if r < 2 else 2 * (r - 2)
                a_job(oa[:, t, h0 * P:(h0 + nh) * P], nh * P)

            for c in range(N_WIN):
                r = c - PE_ROUND
                if 0 <= r < 6:
                    exps(r)
                if c % 2:
                    block_out(c // 2)
                if c == PE_A[0]:
                    u_out()
                if c in PE_A:
                    stage_a(PE_A.index(c))
                if c in PE_C:
                    stage_c(PE_C.index(c))
                if c == PE_QK:
                    for n in range(8):
                        a_job(qkT[:, 2 * n:2 * n + 2].rearrange("p h t -> p (h t)"), BLK)
                if 0 <= r < 6:
                    round_out(r)
                if c == PE_ROUND + 6:
                    act.wait_ge(S["osq_ok"], 1)
                    act.activation(sc8[:, 40:56], sc8[:, 24:40], ACT.Sqrt).then_inc(S["ort_ok"], 1)
                    act.wait_ge(S["gel_in"], 1)
                    act.activation(r45[:, 2048:4096], r45[:, 0:2048], ACT.Sigmoid, scale=GELU_S).then_inc(S["gel_sig"], 1)
            for n in range(4):
                a_job(oT[:, 2 * n:2 * n + 2].rearrange("p k t -> p (k t)"), BLK)
            for n in range(4):
                if n == 0:
                    act.wait_ge(S["yp_in"], 16 * 8)
                a_job(yT[:, 2 * n:2 * n + 2].rearrange("p k t -> p (k t)"), BLK)
            act.wait_ge(S["glu_pre"], 1)
            act.activation(r45[:, 0:2048], r45[:, 0:2048], ACT.Sigmoid).then_inc(S["glu_sig"], 1)
            for n in range(4):
                a_job(yT[:, 2 * n:2 * n + 2].rearrange("p k t -> p (k t)"), BLK)
            for n in range(8):
                a_job(hT[:, 2 * n:2 * n + 2].rearrange("p k t -> p (k t)"), BLK)
            act.wait_ge(S["x2_ok"], 1)
            for t in range(TT):
                act.activation(h2[:, t, :], x_t[:, t, :], ACT.Square, accum_out=ss[:, t:t + 1]).then_inc(S["ss2_done"], 1)
            act.wait_ge(S["root2_done"], 1)
            act.activation(ss[:, 4:6], ss[:, 2:4], ACT.Sqrt).then_inc(S["ss2_done"], 1)
            act.wait_ge(S["gex_in"], 1)
            act.activation(rs[:, 64:74], rs[:, 48:58], ACT.Exp).then_inc(S["gex_ok"], 1)
            act.wait_ge(S["xg_ps"], 1)
            act.activation(xg, pb[0][:], ACT.Copy).then_inc(S["xg_sb"], 1)
            act.wait_ge(S["tab_ok"], 1)
            n_items = act.value_load(tab[:, 0:1], min_val=1, max_val=MAXI)
            act.sem_inc(S["gate_sb"], 1)
            with act.Fori(0, n_items) as i:
                act.wait_ge(S["gate_ps"], i + 1)
                act.activation(gu[:, 0], pb[2][:], ACT.Copy).then_inc(S["gate_sb"], 1)
                act.wait_ge(S["xt_ps"], i + 1)
                act.wait_ge(S["xg_ps"], i + 2)
                act.activation(xg, pb[0][:], ACT.Copy).then_inc(S["xg_sb"], 1)
                act.wait_ge(S["sum_ps"], i + 1)
                act.activation(sge, pb[4][:, 0:P], ACT.Sigmoid).then_inc(S["sig_ok"], 1)
                act.wait_ge(S["sc_ps"], i * 8 + 1)
                for n in range(4):
                    act.wait_ge(S["dn_ps"], i * 4 + n + 1)
                    act.activation(ys[:, n], pb[5 + n % 2][:], ACT.Copy).then_inc(S["dn_sb"], 1)
            act.wait_ge(S["moe_ok"], 1)
            for t in range(TT):
                act.activation(h2[:, t, :], x_t[:, t, :], ACT.Square, accum_out=ss[:, t:t + 1]).then_inc(S["fss_done"], 1)
            act.wait_ge(S["froot_done"], 1)
            act.activation(ss[:, 4:6], ss[:, 2:4], ACT.Sqrt).then_inc(S["fss_done"], 1)

        @block.gpsimd
        def _(pool):
            steps = Steps(pool, S["pool"])
            steps(pool.memset(ident[:], 0.0))
            pool.affine_select(out=ident[:], in_=ident[:], compare_op=ALU.not_equal, fill=1.0, base=0,
                               pattern=[[-1, P]], channel_multiplier=1).then_inc(S["ident_ok"], 1)
            for n, name in enumerate(("ssm_c_re", "ssm_c_im")):
                for g in range(4):
                    s_ = a[name][0, 16 * g:16 * g + 16].rearrange("(q h) m p -> h q m p", h=2)
                    for h in range(2):
                        pool.dma_start(cn[:, n, g, h * 64:(h + 1) * 64], s_[h]).then_inc(S["c_in"], 16)
            for n, name in enumerate(("ssm_b_re", "ssm_b_im")):
                pool.dma_start(braw[:, n].rearrange("p g q m -> p (g q) m"),
                              a[name][0].rearrange("(q h) p m -> (h p) q m", h=2)).then_inc(S["b_in"], 16)
            pool.dma_start(bcw[:, 0:W], a["ssm_d"][0].partition_broadcast(P)).then_inc(S["bc_in"], 16)
            pool.dma_start(bcw[:, W:2 * W], a["ssm_glu_b"][0].partition_broadcast(P)).then_inc(S["bc_in"], 16)
            pool.dma_start(rwv[:, :, 0:NG], a["router_group_w"][0].rearrange("(p k) e -> p k e", k=KT)).then_inc(S["rw_in"], 16)
            pool.dma_start(rwv[:, :, NG:NG + NE], a["router_expert_w"][0].rearrange("(p k) e -> p k e", k=KT)).then_inc(S["rw_in"], 16)
            steps(pool.memset(mask[:], 0.0))
            pool.affine_select(out=mask[:, P:2 * P], in_=mask[:, P:2 * P], compare_op=ALU.is_ge, fill=NEG, base=0,
                               pattern=[[-1, P]], channel_multiplier=1).then_inc(S["mask_ok"], 1)
            pool.memset(r45[:, 2048:4096], 0.0).then_inc(S["cbd_zero"], 1)
            pool.memset(st_j[:, 0], 0.0).then_inc(S["st0_ok"], 1)
            pool.wait_ge(S["blk_free"], 4)
            pool.wait_ge(S["a_free"], 2)
            pool.wait_ge(S["lsum_ok"], 1)
            for f in range(4):
                for t in range(TT):
                    pool.dma_start(yp[32 * f + 16 * t:32 * f + 16 * t + 16],
                                   z_t[:, t, f * 256:(f + 1) * 256]).then_inc(S["uj_in"], 16)
            pool.wait_ge(S["uj_in"], 16 * 8)
            pool.wait_ge(S["h_done"], 2)
            pool.tensor_copy(up, yp.rearrange("p i (g m) -> p g i m", g=16)).then_inc(S["up_ok"], 1)
            pool.wait_ge(S["ut_ok"], 1)
            pool.memset(xa[:, 2048:4096], 0.0).then_inc(S["tq_zero"], 1)
            pool.wait_ge(S["tq_zero"], 1)
            pool.wait_ge(S["wp_ok"], NQ)
            for q in range(NQ):
                if q:
                    pool.wait_ge(S["tq_used"], q)
                for i in range(L):
                    pool.dma_start(tq[0:SM * (i + 1), i, :],
                                   wp[SM * (L - 1 - i):P, q * 256:(q + 1) * 256]).then_inc(S["tq_in"], 16)
            pool.wait_ge(S["yp_ok"], 1)
            for f in range(4):
                for t in range(TT):
                    pool.dma_start(yg[:, t, f * 256:(f + 1) * 256],
                                   yp[32 * f + 16 * t:32 * f + 16 * t + 16]).then_inc(S["yp_in"], 16)
            pool.wait_ge(S["x2_ok"], 1)
            steps(pool.memset(yT[:, 0], 1.0))
            pool.affine_select(out=lt, in_=lt, compare_op=ALU.is_gt, fill=0.0, base=0,
                               pattern=[[1, P]], channel_multiplier=-1)
            pool.iota(iota, pattern=[[0, 4], [1, CAP]], base=0, channel_multiplier=0, allow_small_or_imprecise_dtypes=True)
            pool.iota(thr, pattern=[[CAP, 8]], base=0, channel_multiplier=0, allow_small_or_imprecise_dtypes=True)
            steps(pool.iota(i48, pattern=[[1, MAXI], [0, NE]], base=0, channel_multiplier=0, allow_small_or_imprecise_dtypes=True))
            pool.sem_inc(S["iota_ok"], 1)
            pool.wait_ge(S["tab_ok"], 1)
            pool.dma_start(bcw[:], a["final_norm_w"].partition_broadcast(P)).then_inc(S["fw_in"], 16)
            pool.wait_ge(S["fw_in"], 16)

        @block.vector
        def _(v):
            steps = Steps(v, S["dve"])
            vj = [0]

            def v_bank():
                n = vj[0]
                vj[0] += 1
                v.wait_ge(S["v_ready"], n + 1)
                return pb[4 + n % 2]

            v.wait_ge(S["dt_in"], 64)
            v.tensor_copy(p32[:, 2 * P:3 * P].rearrange("p (h s) -> p h s", h=2), bc(dt32, 2, 64)).then_inc(S["dt_spread"], 1)
            v.wait_ge(S["ss_done"], 2)
            v.tensor_scalar(ss[:, 2:4], ss[:, 0:2], 1.0 / D, NORM_EPS, ALU.mult, ALU.add).then_inc(S["root_done"], 1)
            v.wait_ge(S["ss_done"], 3)
            steps(v.reciprocal(ss[:, 6:8], ss[:, 4:6]))
            for t in range(TT):
                ins = v.tensor_scalar(h_t[:, t, :], x_t[:, t, :], ss[:, 6 + t:7 + t], None, ALU.mult)
                ins.then_inc(S["h_done"], 1) if t == 0 else ins.then_inc(S["h_done"], 1)
            bank = v_bank()
            v.tensor_copy(lam3, bank[:, 0:96]).then_inc(S["v_free"], 1)
            v.wait_ge(S["v_free"], 1)
            v.sem_inc(S["pe_params"], 1)
            v.wait_ge(S["norms_in"], 32)
            for n in range(8):
                bank = v_bank()
                v.tensor_tensor(hT[:, 2 * n:2 * n + 2], bank[:].rearrange("p (k t) -> p k t", k=2),
                                bc(w1c[:, 2 * n:2 * n + 2], 2, T), ALU.mult).then_inc(S["v_free"], 1)
            v.wait_ge(S["v_free"], 9)
            v.sem_inc(S["hT_ok"], 1)
            v.wait_ge(S["dt_done"], 1)
            steps(v.tensor_tensor(nr, lr, dt_, ALU.mult))
            v.sem_inc(S["arg_done"], 1)
            v.tensor_tensor(ang[:, 0:32], li, dt_, ALU.mult)
            v.wait_ge(S["consts_in"], 16 * 7)
            steps(v.tensor_copy(posf[:], posi[:]))
            for t in range(TT):
                steps(v.tensor_scalar(ang[:, 32 + 32 * t:64 + 32 * t], invf[:], posf[:, t:t + 1], None, ALU.mult))
            for n in range(2):
                steps(v.tensor_tensor(lamw[:, 256:320], lamw[:, n * 128:n * 128 + 64], lamw[:, n * 128 + 64:n * 128 + 128], ALU.mult))
                steps(v.tensor_reduce(lamv[:, n:n + 1], lamw[:, 256:320], AX.X, ALU.add))
            v.sem_inc(S["lsum_ok"], 1)
            kf, r_ = ang[:, 192:288], ang[:, 96:192]
            steps(v.tensor_scalar(kf, ang[:, 0:96], INV_2PI, ROUND, ALU.mult, ALU.add))
            steps(v.tensor_scalar(kf, kf, ROUND, None, ALU.subtract))
            steps(v.scalar_tensor_tensor(r_, kf, -C1, ang[:, 0:96], ALU.mult, ALU.add))
            steps(v.scalar_tensor_tensor(r_, kf, -C2, r_, ALU.mult, ALU.add))
            steps(v.scalar_tensor_tensor(r_, kf, -C3, r_, ALU.mult, ALU.add))
            steps(v.tensor_scalar(r_, r_, PI, -PI, ALU.min, ALU.max))
            v.sem_inc(S["arg_done"], 1)
            v.wait_ge(S["lexp_ok"], 1)
            steps(v.tensor_tensor(lamv[:, 4:5], lamv[:, 3:4], lamv[:, 2:3], ALU.subtract))
            steps(v.tensor_scalar(lamv[:, 5:6], lamv[:, 4:5], LAMBDA_INIT, None, ALU.subtract))
            v.wait_ge(S["sin_done"], 2)
            steps(v.tensor_tensor(ang[:, 0:96], ang[:, 288:384], ang[:, 288:384], ALU.mult))
            steps(v.tensor_scalar(ang[:, 0:96], ang[:, 0:96], -2.0, 1.0, ALU.mult, ALU.add))
            v.wait_ge(S["mag_done"], 1)
            A1 = apw[:, 0]
            v.tensor_tensor(A1[:, 0], mag, ang[:, 0:32], ALU.mult)
            steps(v.tensor_tensor(A1[:, 1], mag, ang[:, 192:224], ALU.mult))
            v.tensor_scalar(nr, A1[:, 0], 1.0, None, ALU.subtract)
            v.tensor_tensor(pt[:, 0:32], lr, lr, ALU.mult)
            steps(v.tensor_tensor(pt[:, 32:64], li, li, ALU.mult))
            steps(v.tensor_tensor(den, pt[:, 0:32], pt[:, 32:64], ALU.add))
            steps(v.reciprocal(den, den))
            v.tensor_tensor(pt[:, 0:32], nr, lr, ALU.mult)
            steps(v.tensor_tensor(pt[:, 32:64], A1[:, 1], li, ALU.mult))
            steps(v.tensor_tensor(fr, pt[:, 0:32], pt[:, 32:64], ALU.add))
            v.tensor_tensor(fr, fr, den, ALU.mult)
            v.tensor_tensor(pt[:, 0:32], A1[:, 1], lr, ALU.mult)
            steps(v.tensor_tensor(pt[:, 32:64], nr, li, ALU.mult))
            steps(v.tensor_tensor(fi, pt[:, 0:32], pt[:, 32:64], ALU.subtract))
            steps(v.tensor_tensor(fi, fi, den, ALU.mult))
            for k in range(3):
                Ak, An = apw[:, k], apw[:, k + 1]
                v.tensor_tensor(pt[:, 0:32], Ak[:, 0], Ak[:, 0], ALU.mult)
                v.tensor_tensor(pt[:, 32:64], Ak[:, 1], Ak[:, 1], ALU.mult)
                steps(v.tensor_tensor(An[:, 1], Ak[:, 0], Ak[:, 1], ALU.mult))
                v.tensor_tensor(An[:, 0], pt[:, 0:32], pt[:, 32:64], ALU.subtract)
                steps(v.tensor_scalar(An[:, 1], An[:, 1], 2.0, None, ALU.mult))
            v.tensor_copy(a8[:, 0:64].rearrange("p (c q) -> p c q", c=2), bc(apw[:, 3, 0], 1, 2))
            v.tensor_copy(a8[:, 64:96], apw[:, 3, 1])
            steps(v.tensor_scalar(a8[:, 96:128], apw[:, 3, 1], -1.0, None, ALU.mult))
            v.wait_ge(S["a_free"], 2)
            v.wait_ge(S["cbd_zero"], 1)
            for h in range(2):
                rows = slice(64 * h, 64 * h + 64)
                for c in range(2):
                    ins = v.tensor_scalar(cbd[rows, c, :, h, :], ct[rows, c].rearrange("p g q m -> p (g q) m"),
                                          1.0 - 2.0 * c, None, ALU.mult)
            steps(ins)
            v.sem_inc(S["cbd_ok"], 1)

            def quarter(t, q):
                return t[:, :, 2 * q:2 * q + 2, :]

            def cmul(o_re, o_im, i_re, i_im, m_re, m_im, t1, t2):
                v.tensor_tensor(t1, i_re, m_re, ALU.mult)
                steps(v.tensor_tensor(t2, i_im, m_im, ALU.mult))
                steps(v.tensor_tensor(o_re, t1, t2, ALU.subtract))
                v.tensor_tensor(t1, i_re, m_im, ALU.mult)
                steps(v.tensor_tensor(t2, i_im, m_re, ALU.mult))
                steps(v.tensor_tensor(o_im, t1, t2, ALU.add))

            def start_quarter(i, raw, m_re, m_im, q):
                def v4(x):
                    return x.rearrange("p (g r m) -> p g r m", g=4, r=2)

                def par_(x):
                    return bc(x[:, q * QP:(q + 1) * QP].rearrange("p (g r) -> p g r", g=4), 3, SM)

                t1, t2 = tmp[:, 0, 0:128], tmp[:, 1, 0:128]
                r_re, r_im = quarter(raw[:, 0], q), quarter(raw[:, 1], q)
                v.tensor_tensor(v4(t1), r_re, par_(m_re), ALU.mult)
                steps(v.tensor_tensor(v4(t2), r_im, par_(m_im), ALU.mult))
                t3 = t1.rearrange("p (q m) -> p q m", q=QP)
                t4 = t2.rearrange("p (q m) -> p q m", q=QP)
                steps(v.tensor_tensor(bp[:, 0, :, i, :], t3, t4, ALU.subtract))
                v.tensor_tensor(v4(t1), r_re, par_(m_im), ALU.mult)
                steps(v.tensor_tensor(v4(t2), r_im, par_(m_re), ALU.mult))
                steps(v.tensor_tensor(bp[:, 1, :, i, :], t3, t4, ALU.add))

            def raise_(dst, src, n, k, q):
                def x(t):
                    return t.rearrange("p q i m -> p q (i m)")
                sh = n * SM
                def w(t):
                    return t[:, 0:QP * sh].rearrange("p (q x) -> p q x", q=QP)
                cmul(x(bp[:, 0, :, dst:dst + n]), x(bp[:, 1, :, dst:dst + n]),
                     x(bp[:, 0, :, src:src + n]), x(bp[:, 1, :, src:src + n]),
                     bc(apw[:, k, 0, q * QP:(q + 1) * QP], 2, sh), bc(apw[:, k, 1, q * QP:(q + 1) * QP], 2, sh),
                     w(tmp[:, 0]), w(tmp[:, 1]))

            v.wait_ge(S["b_in"], 32)
            v.wait_ge(S["v_free"], 9)
            for q in range(NQ):
                if q:
                    v.wait_ge(S["bp_used"], q)
                start_quarter(7, braw, fr, fi, q)
                raise_(6, 7, 1, 0, q)
                raise_(4, 6, 2, 1, q)
                raise_(0, 4, 4, 2, q)
                v.sem_inc(S["bp_ok"], 1)
                bank = v_bank()
                ins = v.tensor_copy(wp[:, q * 256:(q + 1) * 256], bank[:, 0:256])
                ins.then_inc(S["v_free"], 1)
                v.wait_ge(S["v_free"], vj[0])
                v.sem_inc(S["wp_ok"], 1)
                for c in range(2):
                    bank = v_bank()
                    src = bank[:].rearrange("p (q h j) -> p q h j", q=QP, h=2)
                    for h in range(2):
                        rows = slice(64 * h, 64 * h + 64)
                        ins = v.tensor_copy(st_j[rows, 1:NJ + 1, c, q * QP:(q + 1) * QP].rearrange("p j q -> p q j"),
                                            src[rows, :, h, :])
                    ins.then_inc(S["v_free"], 1)
            v.wait_ge(S["v_free"], vj[0])
            v.wait_ge(S["st0_ok"], 1)
            t1 = tmp[:, 0, 0:64]
            t2 = tmp[:, 0, 64:128]
            SC = 5
            with v.Fori(0, NJ) as j:
                sj = st[:, bass.ds(j * 64, 64)]
                sn = st[:, bass.ds(j * 64 + 64, 64)]
                n_re = st[:, bass.ds(j * 64 + 64, 32)]
                n_im = st[:, bass.ds(j * 64 + 96, 32)]
                v.tensor_tensor(t1, sj, a8[:, 0:64], ALU.mult).then_inc(S["scan"], 1)
                v.tensor_tensor(t2, sj, a8[:, 64:128], ALU.mult).then_inc(S["scan"], 1)
                v.wait_ge(S["scan"], j * SC + 2)
                v.tensor_tensor(sn, sn, t1, ALU.add).then_inc(S["scan"], 1)
                v.wait_ge(S["scan"], j * SC + 3)
                v.tensor_tensor(n_re, n_re, t2[:, 32:64], ALU.add).then_inc(S["scan"], 1)
                v.tensor_tensor(n_im, n_im, t2[:, 0:32], ALU.add).then_inc(S["scan"], 1)
                v.wait_ge(S["scan"], j * SC + 5)
            v.wait_ge(S["s_used"], NQ)
            steps(v.memset(r45[:, 0:4096], 0.0))
            for h in range(2):
                rows = slice(64 * h, 64 * h + 64)
                for c in range(2):
                    ins = v.tensor_scalar(sbd[rows, c, h], st_j[rows, 0:NJ, c, :].rearrange("p j q -> p q j"),
                                          1.0 - 2.0 * c, None, ALU.mult)
            steps(ins)
            v.sem_inc(S["sbd_ok"], 1)
            v.wait_ge(S["up_ok"], 1)
            for part in range(2):
                v.wait_ge(S["blk_free"], 8 + 4 * part)
                for t in range(TT):
                    src = z_t[:, t, (part + 1) * W:(part + 2) * W].rearrange("p (h a d) -> p h a d", a=2, d=32)
                    cos = bc(ang[:, 32 + 32 * t:64 + 32 * t], 1, 2 * H)
                    sin = bc(ang[:, 224 + 32 * t:256 + 32 * t], 1, 2 * H)
                    v.tensor_tensor(rt[:, 0], src[:, :, 0], cos, ALU.mult)
                    v.tensor_tensor(rt[:, 1], src[:, :, 1], sin, ALU.mult)
                    v.tensor_tensor(rt[:, 2], src[:, :, 1], cos, ALU.mult)
                    steps(v.tensor_tensor(rt[:, 3], src[:, :, 0], sin, ALU.mult))
                    v.tensor_tensor(src[:, :, 0], rt[:, 0], rt[:, 1], ALU.subtract)
                    steps(v.tensor_tensor(src[:, :, 1], rt[:, 2], rt[:, 3], ALU.add))
            v.sem_inc(S["qk_rot"], 1)
            v.wait_ge(S["bp_used"], NQ)
            for q in range(NQ):
                if q:
                    v.wait_ge(S["ca_used"], q)
                start_quarter(0, ct, apw[:, 0, 0], apw[:, 0, 1], q)
                raise_(1, 0, 1, 0, q)
                raise_(2, 0, 2, 1, q)
                raise_(4, 0, 4, 2, q)
                v.sem_inc(S["ca_ok"], 1)
            v.wait_ge(S["ca_used"], NQ)
            v.wait_ge(S["mask_ok"], 1)
            exps = [0, 8, 16, 20, 24, 28, 32]
            amw = [33 + 2 * r for r in range(7)]
            for r in range(6):
                nh, K = (4, P) if r < 2 else (2, 2 * P)
                mk = mask[:, P:2 * P] if r < 2 else mask[:]
                if r:
                    v.wait_ge(S["ex_ok"], exps[r])
                for c in range(2):
                    bank = v_bank()
                    v.tensor_tensor(sm_[:, c].rearrange("p (h k) -> p h k", h=nh),
                                    bank[:].rearrange("p (h k) -> p h k", h=nh), bc(mk, 1, nh), ALU.add).then_inc(S["v_free"], 1)
                v.wait_ge(S["v_free"], vj[0])
                steps(v.tensor_reduce(sc8[:, 0:8].rearrange("p (c h) -> p c h", c=2)[:, :, 0:nh],
                                      sm_[:].rearrange("p c (h k) -> p c h k", h=nh), AX.X, ALU.max))
                nm = sc8[:, 8:16].rearrange("p (c h) -> p c h", c=2)[:, :, 0:nh]
                steps(v.tensor_scalar(nm, sc8[:, 0:8].rearrange("p (c h) -> p c h", c=2)[:, :, 0:nh], -SCALE, None, ALU.mult))
                v.sem_inc(S["nmx_ok"], 1)
                v.wait_ge(S["ex_ok"], exps[r + 1])
                sv = sc8[:, 16:24].rearrange("p (c h) -> p c h", c=2)[:, :, 0:nh]
                steps(v.reciprocal(sv, sv))
                steps(v.tensor_scalar(sv[:, 1], sv[:, 1], lamv[:, 5:6], None, ALU.mult))
                e4 = ex[:].rearrange("p c (h k) -> p c h k", h=nh)
                am3 = am.rearrange("p (h k) -> p h k", h=nh)
                if r:
                    v.wait_ge(S["a_free"], amw[r])
                v.tensor_tensor(am3, e4[:, 0], bc(sv[:, 0], 2, K), ALU.mult)
                steps(v.tensor_tensor(e4[:, 1], e4[:, 1], bc(sv[:, 1], 2, K), ALU.mult))
                steps(v.tensor_tensor(am3, am3, e4[:, 1], ALU.add))
                v.sem_inc(S["am_ok"], 1)
            v.wait_ge(S["a_free"], amw[6] + 1)
            oa4 = oa.rearrange("p t (h e) -> p t h e", h=H)
            steps(v.tensor_tensor(osq, oa, oa, ALU.mult))
            for t in range(TT):
                steps(v.tensor_reduce(sc8[:, 24 + 8 * t:32 + 8 * t], osq[:, t].rearrange("p (h e) -> p h e", h=H), AX.X, ALU.add))
            steps(v.tensor_scalar(sc8[:, 24:40], sc8[:, 24:40], 1.0 / P, SUBLN_EPS, ALU.mult, ALU.add))
            v.sem_inc(S["osq_ok"], 1)
            steps(v.tensor_scalar(subw[:], subw[:], 1.0 - LAMBDA_INIT, None, ALU.mult))
            v.wait_ge(S["ort_ok"], 1)
            steps(v.reciprocal(sc8[:, 40:56], sc8[:, 40:56]))
            for t in range(TT):
                steps(v.tensor_tensor(oa4[:, t], oa4[:, t], bc(sc8[:, 40 + 8 * t:48 + 8 * t], 2, P), ALU.mult))
                steps(v.tensor_tensor(oa4[:, t], oa4[:, t], bc(subw[:], 1, H), ALU.mult))
            v.sem_inc(S["oa_ok"], 1)
            g0 = r45[:, 0:2048].rearrange("p (t c) -> p t c", t=TT)
            g1 = r45[:, 2048:4096].rearrange("p (t c) -> p t c", t=TT)
            v.wait_ge(S["yp_in"], 16 * 8)
            v.wait_ge(S["bc_in"], 32)
            steps(v.tensor_tensor(g0, z_t[:, :, 0:W], bc(bcw[:, 0:W], 1, TT), ALU.mult))
            steps(v.tensor_tensor(yg, yg, g0, ALU.add))
            steps(v.tensor_tensor(g0, yg, yg, ALU.mult))
            steps(v.tensor_scalar(g0, g0, GELU_C, 1.0, ALU.mult, ALU.add))
            steps(v.tensor_tensor(g0, g0, yg, ALU.mult))
            v.sem_inc(S["gel_in"], 1)
            v.wait_ge(S["gel_sig"], 1)
            steps(v.tensor_tensor(yg, yg, g1, ALU.mult))
            v.sem_inc(S["gelu_ok"], 1)
            for n in range(2):
                for t in range(TT):
                    v.wait_ge(S["blk_ready"], 33 + 2 * n + t)
                    v.tensor_tensor(g0[:, t, n * BLK:(n + 1) * BLK], pb[2 * n + t][:],
                                    bcw[:, W + n * BLK:W + (n + 1) * BLK], ALU.add).then_inc(S["out_free"], 1)
            v.wait_ge(S["out_free"], 4)
            v.sem_inc(S["glu_pre"], 1)
            v.wait_ge(S["glu_sig"], 1)
            steps(v.tensor_tensor(yg, yg, g0, ALU.mult))
            v.sem_inc(S["y2_ok"], 1)
            for n in range(4):
                for t in range(TT):
                    gs = gs_t[:, t, n * BLK:(n + 1) * BLK]
                    v.wait_ge(S["blk_ready"], 37 + 4 * n + t)
                    steps(v.tensor_tensor(gs, gs, pb[t][:], ALU.mult))
                    v.sem_inc(S["out_free"], 1)
                for t in range(TT):
                    gs = gs_t[:, t, n * BLK:(n + 1) * BLK]
                    ga = ga_t[:, t, n * BLK:(n + 1) * BLK]
                    v.wait_ge(S["blk_ready"], 39 + 4 * n + t)
                    steps(v.tensor_tensor(ga, ga, pb[2 + t][:], ALU.mult))
                    v.sem_inc(S["out_free"], 1)
                    steps(v.tensor_tensor(gs, gs, ga, ALU.add))
            v.sem_inc(S["mrg_ok"], 1)
            v.wait_ge(S["x_again"], 32)
            for n in range(4):
                for t in range(TT):
                    v.wait_ge(S["blk_ready"], 53 + 2 * n + t)
                    xs = x_t[:, t, n * BLK:(n + 1) * BLK]
                    steps(v.tensor_tensor(xs, xs, pb[2 * (n % 2) + t][:], ALU.add))
                    v.sem_inc(S["out_free"], 1)
            v.sem_inc(S["x2_ok"], 1)
            v.wait_ge(S["ss2_done"], 2)
            steps(v.tensor_scalar(ss[:, 2:4], ss[:, 0:2], 1.0 / D, NORM_EPS, ALU.mult, ALU.add))
            v.sem_inc(S["root2_done"], 1)
            v.wait_ge(S["ss2_done"], 3)
            steps(v.reciprocal(ss[:, 6:8], ss[:, 4:6]))
            for t in range(TT):
                steps(v.tensor_scalar(h2[:, t, :], x_t[:, t, :], ss[:, 6 + t:7 + t], None, ALU.mult))
            v.sem_inc(S["h2_ok"], 1)
            for n in range(8):
                bank = v_bank()
                v.tensor_tensor(hT[:, 2 * n:2 * n + 2], bank[:].rearrange("p (k t) -> p k t", k=2),
                                bc(w2c[:, 2 * n:2 * n + 2], 2, T), ALU.mult).then_inc(S["v_free"], 1)
            v.wait_ge(S["v_free"], vj[0])
            v.sem_inc(S["h2T_ok"], 1)
            v.wait_ge(S["iota_ok"], 1)
            steps(v.tensor_reduce(q32, ident[:].rearrange("p (g s) -> p s g", g=4), AX.X, ALU.add))
            v.wait_ge(S["lg_ps"], 1)
            steps(v.tensor_copy(lg, pb[0][:, 0:128].rearrange("p (t e) -> p t e", t=TT)[:, :, 0:NG + NE]))
            g8 = rs[:, 0:16].rearrange("p (t e) -> p t e", t=TT)
            steps(v.memset(rs[:, 0:16], -3.0e38))
            steps(v.tensor_copy(g8[:, :, 0:NG], lg[:, :, 0:NG]))
            m8 = rs[:, 16:32].rearrange("p (t e) -> p t e", t=TT)
            x8 = rs[:, 32:48].bitcast(U32).rearrange("p (t e) -> p t e", t=TT)
            gidx = rs[:, 80:82]
            oh = rs[:, 84:92].rearrange("p (t g) -> p t g", t=TT)
            es = rs[:, 96:112].rearrange("p (t e) -> p t e", t=TT)
            pr = rs[:, 112:176].rearrange("p (t g e) -> p t g e", t=TT, g=NG)
            v8 = rs[:, 176:192].rearrange("p (t e) -> p t e", t=TT)
            y8 = rs[:, 192:208].bitcast(U32).rearrange("p (t e) -> p t e", t=TT)
            eid = rs[:, 208:212].rearrange("p (t k) -> p t k", t=TT)
            mk = rs[:, 212:340].rearrange("p (t k e) -> p t k e", t=TT, k=2)
            mm = rs[:, 340:404].rearrange("p (t e) -> p t e", t=TT)
            rk = rs[:, 404:500].rearrange("p (t e) -> p t e", t=3)
            nb = rs[:, 500:532]
            be = rs[:, 532:564]
            cm = rs[:, 564:820].rearrange("p (e j) -> p e j", j=8)
            pk = rs[:, 820:948].rearrange("p (t k e) -> p t k e", t=TT, k=2)
            for t in range(TT):
                steps(v.max(m8[:, t], g8[:, t]))
                steps(v.max_index(x8[:, t], m8[:, t], g8[:, t]))
            steps(v.tensor_copy(gidx, x8[:, :, 0]))
            for t in range(TT):
                steps(v.tensor_scalar(rs[:, 48 + 4 * t:52 + 4 * t], lg[:, t, 0:NG], m8[:, t, 0:1], None, ALU.subtract))
                steps(v.tensor_scalar(oh[:, t], iota[:, 0, 0:NG], gidx[:, t:t + 1], None, ALU.is_equal))
                steps(v.tensor_tensor(pr[:, t], lg[:, t, NG:NG + NE].rearrange("p (g e) -> p g e", g=NG), bc(oh[:, t], 2, EPG), ALU.mult))
                steps(v.tensor_reduce(es[:, t], pr[:, t].rearrange("p g e -> p e g"), AX.X, ALU.add))
                steps(v.max(v8[:, t], es[:, t]))
                steps(v.max_index(y8[:, t], v8[:, t], es[:, t]))
                steps(v.tensor_copy(eid[:, t], y8[:, t, 0:2]))
                steps(v.scalar_tensor_tensor(eid[:, t], gidx[:, t:t + 1].to_broadcast([P, 2]),
                                             float(EPG), eid[:, t], ALU.mult, ALU.add))
            steps(v.tensor_tensor(rs[:, 56:58], v8[:, :, 1], v8[:, :, 0], ALU.subtract))
            v.sem_inc(S["gex_in"], 1)
            for t in range(TT):
                for k in range(2):
                    steps(v.tensor_scalar(mk[:, t, k], iota[:, 0], eid[:, t, k:k + 1], None, ALU.is_equal))
            steps(v.tensor_tensor(mm, mk[:, :, 0], mk[:, :, 1], ALU.add))
            v.sem_inc(S["m_ok"], 1)
            v.wait_ge(S["gex_ok"], 1)
            steps(v.tensor_reduce(rs[:, 76:78], rs[:, 64:72].rearrange("p (t g) -> p t g", t=TT), AX.X, ALU.add))
            steps(v.tensor_scalar(rs[:, 78:80], rs[:, 72:74], 1.0, None, ALU.add))
            steps(v.tensor_tensor(rs[:, 76:78], rs[:, 76:78], rs[:, 78:80], ALU.mult))
            steps(v.reciprocal(gw[:, :, 0], rs[:, 76:78]))
            steps(v.tensor_tensor(gw[:, :, 1], gw[:, :, 0], rs[:, 72:74], ALU.mult))
            v.wait_ge(S["cnt_ps"], 1)
            steps(v.tensor_copy(rs[:, 404:500], pb[1][:, 0:96]))
            steps(v.tensor_tensor(cm, bc(rk[:, 2], 2, 8), bc(thr, 1, NE), ALU.is_gt))
            steps(v.tensor_reduce(nb, cm, AX.X, ALU.add))
            steps(v.tensor_scalar(nb[:, 0:1], nb[:, 0:1], 1.0, None, ALU.max))
            steps(v.tensor_tensor_scan(be, ones[:, 0:NE], nb, 0.0, ALU.mult, ALU.add))
            steps(v.tensor_tensor(cmp48, bc(be[0:1], 1, MAXI), i48, ALU.is_le))
            steps(v.tensor_reduce(tabf[:, 1:1 + MAXI], cmp48, AX.X, ALU.add))
            steps(v.tensor_copy(tabf[:, 0:1], be[0:1, NE - 1:NE]))
            steps(v.tensor_scalar(tabf[:, 1:1 + MAXI], tabf[:, 1:1 + MAXI], NE - 1.0, None, ALU.min))
            steps(v.tensor_copy(tab, tabf))
            v.sem_inc(S["tab_ok"], 1)
            steps(v.tensor_tensor(nb, be, nb, ALU.subtract))
            for t in range(TT):
                steps(v.scalar_tensor_tensor(rk[:, t], nb, float(CAP), rk[:, t], ALU.mult, ALU.add))
                steps(v.tensor_tensor(pk[:, t], mk[:, t], bc(rk[:, t], 1, 2), ALU.mult))
            for t in range(TT):
                steps(v.tensor_reduce(rem[:, t], pk[:, t], AX.X, ALU.add))
            istep = S["istep"]

            def selection():
                for t in range(TT):
                    v.tensor_scalar(sel[:, t], iota[:, 0], rem[:, t, 0:1], None, ALU.is_equal)
                    last = v.tensor_scalar(sela[:, t], iota[:, 0], rem[:, t, 1:2], None, ALU.is_equal)
                return last

            selection().then_inc(istep, 1)
            v.wait_ge(istep, 1)
            v.tensor_tensor(sel, sel, sela, ALU.add).then_inc(S["sel_ok"], 1)

            def xT_out():
                v.tensor_tensor(xT, pb[1][:].rearrange("p (j n s) -> p j n s", j=4, n=4),
                                bc(w2c.rearrange("p (n j) -> p j n", j=4), 3, CAP), ALU.mult).then_inc(S["xt_sb"], 1)

            v.wait_ge(S["xt_ps"], 1)
            xT_out()
            n_items = v.value_load(tab[:, 0:1], min_val=1, max_val=MAXI)
            v.sem_inc(S["up_sb"], 1)
            v.sem_inc(S["sc_free"], 1)
            with v.Fori(0, n_items) as i:
                v.wait_ge(S["swt_ps"], i + 1)
                v.wait_ge(S["sc_free"], i * 8 + 1)
                for t in range(TT):
                    v.tensor_scalar(swr[:, t], iota, rem[:, t, 0:1], gw[:, t, 0:1], ALU.is_equal, ALU.mult)
                    last = v.tensor_scalar(swa[:, t], iota, rem[:, t, 1:2], gw[:, t, 1:2], ALU.is_equal, ALU.mult)
                last.then_inc(istep, 1)
                v.wait_ge(istep, i * 3 + 2)
                v.tensor_tensor(swr, swr, swa, ALU.add).then_inc(S["swr_ok"], 1)
                v.tensor_scalar(rem, rem, float(CAP), None, ALU.subtract).then_inc(istep, 1)
                v.wait_ge(istep, i * 3 + 3)
                v.wait_ge(S["xg_ps"], i + 1)
                selection().then_inc(istep, 1)
                v.wait_ge(istep, i * 3 + 4)
                v.tensor_tensor(sel, sel, sela, ALU.add).then_inc(S["sel_ok"], 1)
                v.wait_ge(S["up_ps"], i + 1)
                v.tensor_copy(gu[:, 1], pb[3][:]).then_inc(S["up_sb"], 1)
                v.wait_ge(S["swt_ps"], i + 2)
                v.tensor_copy(swt, pb[5][:, 0:T]).then_inc(S["swt_sb"], 1)
                v.wait_ge(S["xt_ps"], i + 2)
                xT_out()
                v.wait_ge(S["sig_ok"], i + 1)
                aTf = aTe.rearrange("p k s -> p (k s)")
                v.tensor_tensor(sge, sge, pb[4][:, 0:P], ALU.mult).then_inc(S["si_ok"], 1)
                v.wait_ge(S["si_ok"], i + 1)
                v.tensor_tensor(aTf, sge, pb[4][:, P:2 * P], ALU.mult).then_inc(S["at_ok"], 1)
                for n in range(4):
                    for t in range(TT):
                        m = 2 * n + t
                        v.wait_ge(S["sc_ps"], i * 8 + m + 2)
                        xs = x_t[:, t, n * BLK:(n + 1) * BLK]
                        v.tensor_tensor(xs, xs, pb[(7, 1)[m % 2]][:], ALU.add).then_inc(S["sc_free"], 1)
            v.wait_ge(S["sc_free"], n_items * 8 + 1)
            v.sem_inc(S["moe_ok"], 1)
            v.wait_ge(S["fss_done"], 2)
            steps(v.tensor_scalar(ss[:, 2:4], ss[:, 0:2], 1.0 / D, NORM_EPS, ALU.mult, ALU.add))
            v.sem_inc(S["froot_done"], 1)
            v.wait_ge(S["fss_done"], 3)
            steps(v.reciprocal(ss[:, 6:8], ss[:, 4:6]))
            v.wait_ge(S["fw_in"], 16)
            for t in range(TT):
                v.scalar_tensor_tensor(x_t[:, t, :], x_t[:, t, :], ss[:, 6 + t:7 + t], bcw[:],
                                       ALU.mult, ALU.mult).then_inc(S["out_ok"], 1)

        @block.tensor
        def _(pe):
            vj, aj = [0], [0]

            def v_bank():
                n = vj[0]
                vj[0] += 1
                if n >= 2:
                    pe.wait_ge(S["v_free"], n - 1)
                return pb[4 + n % 2]

            def a_bank():
                n = aj[0]
                aj[0] += 1
                if n >= 2:
                    pe.wait_ge(S["a_free"], n - 1)
                return pb[6 + n % 2]

            pe.wait_ge(S["ident_ok"], 1)
            pe.wait_ge(S["lam_in"], 16 * 8)
            pe.wait_ge(S["dt_spread"], 1)
            bank = v_bank()
            for n in range(3):
                ins = pe.transpose(bank[:, 32 * n:32 * n + 32], p32[:, n * P:(n + 1) * P], ident[0:32, 0:32])
            ins.then_inc(S["v_ready"], 1)
            pe.wait_ge(S["h_done"], 2)
            hs = h_t.rearrange("p t (d k) -> p t d k", k=KT)
            for n in range(8):
                bank = v_bank()
                for k in range(2):
                    for t in range(TT):
                        ins = pe.transpose(bank[:, (2 * k + t) * P:(2 * k + t + 1) * P], hs[:, t, :, 2 * n + k], ident[:])
                ins.then_inc(S["v_ready"], 1)
            pe.wait_ge(S["c_in"], 16 * 16)
            for c in range(2):
                bank = a_bank()
                for g in range(4):
                    ins = pe.transpose(bank[:, g * P:(g + 1) * P], cn[:, c, g, :], ident[:])
                ins.then_inc(S["a_ready"], 1)

            def w_in_chunk(k):
                b, c, s_ = k // 2, k % 2, k % DENSE_SLOTS
                b0 = 2 * (b % 2)
                if c == 0 and b >= 2:
                    pe.wait_ge(S["blk_free"], 2 * (b - 1))
                pe.wait_ge(full[s_], 16 * (k // DENSE_SLOTS + 1))
                wv = chunk3(s_)
                for kk in range(CH):
                    for t in range(TT):
                        ins = pe.matmul(pb[b0 + t][:], hT[:, c * CH + kk, t * P:(t + 1) * P], wv[:, kk, :],
                                        start=(c == 0 and kk == 0), stop=(c == 1 and kk == CH - 1))
                        if c == 1 and kk == CH - 1:
                            ins.then_inc(S["blk_ready"], 1)
                if c == 0:
                    ins.then_inc(S["chunk_used"], 1)
                else:
                    pe.wait_ge(S["blk_ready"], 2 * b + 2)
                    pe.sem_inc(S["chunk_used"], 1)

            def u_turn():
                pe.wait_ge(S["up_ok"], 1)
                for n in range(4):
                    bank = a_bank()
                    for g in range(4):
                        ins = pe.transpose(bank[:, g * P:(g + 1) * P], up[:, 4 * n + g].rearrange("p i m -> p (i m)"), ident[:])
                    ins.then_inc(S["a_ready"], 1)
                pe.wait_ge(S["a_ready"], aj[0])
                pe.sem_inc(S["ut_ok"], 1)
                pe.wait_ge(S["cbd_ok"], 1)

            def stage_a(q):
                pe.wait_ge(S["bp_ok"], q + 1)
                for n in range(4):
                    bank = a_bank()
                    for r in range(2):
                        for c in range(2):
                            ins = pe.transpose(bank[:, (2 * r + c) * P:(2 * r + c + 1) * P],
                                               bp[:, c, 2 * n + r].rearrange("p i m -> p (i m)"), ident[:])
                    ins.then_inc(S["a_ready"], 1)
                bank = v_bank()
                for r in range(QP):
                    nat = (r // 2) * 8 + 2 * q + r % 2
                    for c in range(2):
                        ins = pe.matmul(bank[:, r * 32:(r + 1) * 32], bp[:, c, r].rearrange("p i m -> p (i m)"),
                                        cbd[:, c, nat].rearrange("p h m -> p (h m)"), start=(c == 0), stop=(c == 1))
                ins.then_inc(S["v_ready"], 1)
                pe.wait_ge(S["v_ready"], vj[0])
                pe.sem_inc(S["bp_used"], 1)
                pe.wait_ge(S["a_free"], aj[0])
                for c in range(2):
                    bank = v_bank()
                    for r in range(QP):
                        g0_ = 4 * q + 2 * (r % 2)
                        ins = pe.matmul(bank[:, r * 64:(r + 1) * 64].rearrange("p (h j) -> p h j", h=2), bt[:, r, c, :],
                                        ut[:, g0_:g0_ + 2, r // 2, :], start=True, stop=True)
                    ins.then_inc(S["v_ready"], 1)
                pe.wait_ge(S["v_ready"], vj[0])
                pe.sem_inc(S["s_used"], 1)

            def stage_c(q):
                pe.wait_ge(S["sbd_ok"], 1)
                pe.wait_ge(S["tq_in"], 16 * L * (q + 1))
                pe.wait_ge(S["ca_ok"], q + 1)
                bank = a_bank()
                for gq in range(4):
                    r2, h = gq // 2, gq % 2
                    for part in range(3):
                        for f in range(4):
                            dst = bank[32 * f:32 * f + 32, gq * P:(gq + 1) * P]
                            r = 2 * f + r2
                            if part == 0:
                                rhs = tq[:, :, r * 32 + h * SM:r * 32 + h * SM + SM]
                                ins = pe.matmul(dst.rearrange("p (i m) -> p i m", i=L), ut[:, 4 * q + gq, f, :], rhs,
                                                start=True, stop=False)
                            else:
                                ins = pe.matmul(dst, sbd[:, part - 1, h, q * QP + r, :],
                                                bp[:, part - 1, r].rearrange("p i m -> p (i m)"),
                                                start=False, stop=(part == 2))
                ins.then_inc(S["a_ready"], 1)
                pe.wait_ge(S["a_ready"], aj[0])
                pe.sem_inc(S["ca_used"], 1)
                pe.sem_inc(S["tq_used"], 1)
                if q == NQ - 1:
                    pe.wait_ge(S["a_free"], aj[0])
                    pe.sem_inc(S["yp_ok"], 1)

            def qk_turn():
                pe.wait_ge(S["qk_rot"], 1)
                for n in range(8):
                    bank = a_bank()
                    for k in range(2):
                        for t in range(TT):
                            hh = 2 * n + k
                            ins = pe.transpose(bank[:, (2 * k + t) * P:(2 * k + t + 1) * P], qk[:, t, hh * P:(hh + 1) * P], ident[:])
                    ins.then_inc(S["a_ready"], 1)
                pe.wait_ge(S["a_free"], aj[0])

            def scores(r):
                nh, K = (4, P) if r < 2 else (2, 2 * P)
                t = 0 if r < 2 else 1
                h0 = 4 * r if r < 2 else 2 * (r - 2)
                for c in range(2):
                    bank = v_bank()
                    rows = slice(64 * c, 64 * c + 64)
                    for h in range(nh):
                        ins = pe.matmul(bank[:, h * K:(h + 1) * K], qkT[rows, h0 + h, t * P:(t + 1) * P],
                                        qkT[rows, H + h0 + h, 0:K], start=True, stop=True)
                    ins.then_inc(S["v_ready"], 1)

            def round_(r):
                nh, K = (4, P) if r < 2 else (2, 2 * P)
                h0 = 4 * r if r < 2 else 2 * (r - 2)
                if r < 5:
                    scores(r + 1)
                pe.wait_ge(S["am_ok"], r + 1)
                bank = a_bank()
                for n in range(4):
                    ins = pe.transpose(bank[:, n * P:(n + 1) * P], am[:, n * P:(n + 1) * P], ident[:])
                ins.then_inc(S["a_ready"], 1)
                pe.wait_ge(S["a_free"], aj[0])
                bank = a_bank()
                nk = K // P
                for h in range(nh):
                    for k in range(nk):
                        ins = pe.matmul(bank[:, h * P:(h + 1) * P], aT[:, (h * nk + k) * P:(h * nk + k + 1) * P],
                                        z_t[:, k, 3 * W + (h0 + h) * P:3 * W + (h0 + h + 1) * P],
                                        start=(k == 0), stop=(k == nk - 1))
                ins.then_inc(S["a_ready"], 1)

            def turn(src, nk):
                sv = src.rearrange("p t (c k) -> p t c k", k=nk)
                for n in range(nk // 2):
                    bank = a_bank()
                    for k in range(2):
                        for t in range(TT):
                            ins = pe.transpose(bank[:, (2 * k + t) * P:(2 * k + t + 1) * P], sv[:, t, :, 2 * n + k], ident[:])
                    ins.then_inc(S["a_ready"], 1)

            pe.wait_ge(S["hT_ok"], 1)
            for c in range(N_WIN):
                w_in_chunk(c)
                if c == PE_A[0]:
                    u_turn()
                if c in PE_A:
                    stage_a(PE_A.index(c))
                if c in PE_C:
                    stage_c(PE_C.index(c))
                if c == PE_QK:
                    qk_turn()
                    scores(0)
                if 0 <= c - PE_ROUND < 6:
                    round_(c - PE_ROUND)
            pe.wait_ge(S["oa_ok"], 1)
            turn(oa, WK)
            pe.wait_ge(S["a_ready"], aj[0])
            pe.sem_inc(S["xfree"], 1)
            pe.wait_ge(S["gelu_ok"], 1)
            turn(yg, WK)
            pe.wait_ge(S["a_free"], aj[0])
            k = N_WIN
            for n in range(2):
                pe.wait_ge(S["blk_free"], 30 + 2 * n)
                s = k % DENSE_SLOTS
                pe.wait_ge(full[s], 16 * (k // DENSE_SLOTS + 1))
                wv = chunk3(s)
                for kk in range(CH):
                    for t in range(TT):
                        ins = pe.matmul(pb[2 * n + t][:], yT[:, kk, t * P:(t + 1) * P], wv[:, kk, :],
                                        start=(kk == 0), stop=(kk == CH - 1))
                        if kk == CH - 1:
                            ins.then_inc(S["blk_ready"], 1)
                pe.wait_ge(S["blk_ready"], 32 + 2 * n + 2)
                pe.sem_inc(S["chunk_used"], 1)
                k += 1
            pe.wait_ge(S["y2_ok"], 1)
            turn(yg, WK)
            pe.wait_ge(S["a_free"], aj[0])
            br = 36
            for n in range(4):
                for src, b0 in ((yT, 0), (oT, 2)):
                    pe.wait_ge(S["out_free"], 4 if n == 0 else 4 + 4 * (n - 1) + b0 + 2)
                    s = k % DENSE_SLOTS
                    pe.wait_ge(full[s], 16 * (k // DENSE_SLOTS + 1))
                    wv = chunk3(s)
                    for kk in range(CH):
                        for t in range(TT):
                            ins = pe.matmul(pb[b0 + t][:], src[:, kk, t * P:(t + 1) * P], wv[:, kk, :],
                                            start=(kk == 0), stop=(kk == CH - 1))
                            if kk == CH - 1:
                                ins.then_inc(S["blk_ready"], 1)
                    br += 2
                    pe.wait_ge(S["blk_ready"], br)
                    pe.sem_inc(S["chunk_used"], 1)
                    k += 1
            pe.wait_ge(S["mrg_ok"], 1)
            turn(gs_t, KT)
            pe.wait_ge(S["a_ready"], aj[0])
            pe.sem_inc(S["mT_ps"], 1)
            pe.wait_ge(S["a_free"], aj[0])
            for n in range(4):
                b0 = 2 * (n % 2)
                pe.wait_ge(S["out_free"], 20 if n < 2 else 20 + 2 * (n - 1))
                for c in range(2):
                    s = k % DENSE_SLOTS
                    pe.wait_ge(full[s], 16 * (k // DENSE_SLOTS + 1))
                    wv = chunk3(s)
                    for kk in range(CH):
                        for t in range(TT):
                            ins = pe.matmul(pb[b0 + t][:], hT[:, c * CH + kk, t * P:(t + 1) * P], wv[:, kk, :],
                                            start=(c == 0 and kk == 0), stop=(c == 1 and kk == CH - 1))
                            if c == 1 and kk == CH - 1 and t == 0:
                                ins.then_inc(S["blk_ready"], 1)
                    if c == 0:
                        ins.then_inc(S["chunk_used"], 1)
                    else:
                        ins.then_inc(S["blk_ready"], 1)
                        pe.wait_ge(S["blk_ready"], 52 + 2 * n + 2)
                        pe.sem_inc(S["chunk_used"], 1)
                    k += 1
            pe.wait_ge(S["h2_ok"], 1)
            for n in range(8):
                bank = v_bank()
                for kk in range(2):
                    for t in range(TT):
                        ins = pe.transpose(bank[:, (2 * kk + t) * P:(2 * kk + t + 1) * P], hs[:, t, :, 2 * n + kk], ident[:])
                ins.then_inc(S["v_ready"], 1)
            pe.wait_ge(S["h2T_ok"], 1)
            pe.wait_ge(S["rw_in"], 32)
            for t in range(TT):
                for kk in range(KT):
                    ins = pe.matmul(pb[0][:, 64 * t:64 * t + NG + NE], hT[:, kk, t * P:(t + 1) * P], rwv[:, kk, :],
                                    start=(kk == 0), stop=(kk == KT - 1))
            ins.then_inc(S["lg_ps"], 1)
            pe.wait_ge(S["m_ok"], 1)
            mmr = rs[:, 340:404].rearrange("p (t e) -> p t e", t=TT)
            pe.matmul(pb[1][:, 0:32], lt, mmr[:, 0], start=True, stop=True)
            pe.matmul(pb[1][:, 32:64], ones, mmr[:, 0], start=True, stop=False)
            pe.matmul(pb[1][:, 32:64], lt, mmr[:, 1], start=False, stop=True)
            pe.matmul(pb[1][:, 64:96], ones, mmr[:, 0], start=True, stop=False)
            pe.matmul(pb[1][:, 64:96], ones, mmr[:, 1], start=False, stop=True).then_inc(S["cnt_ps"], 1)

            h2k = h2.rearrange("p t (d k) -> p t k d", k=KT)

            def gather():
                for t in range(TT):
                    for n in range(4):
                        ins = pe.matmul(pb[0][32 * n:32 * n + 32, :].rearrange("p (j d) -> p j d", j=4), sel[:, t],
                                        h2k[:, t, 4 * n:4 * n + 4, :], start=(t == 0), stop=(t == TT - 1))
                ins.then_inc(S["xg_ps"], 1)

            def gather_turn():
                for j in range(4):
                    ins = pe.transpose(pb[1][:, j * P:(j + 1) * P], xg[:, j * P:(j + 1) * P], ident[:])
                ins.then_inc(S["xt_ps"], 1)

            pe.wait_ge(S["sel_ok"], 1)
            gather()
            pe.wait_ge(S["xg_sb"], 1)
            gather_turn()
            n_items = pe.value_load(tab[:, 0:1], min_val=1, max_val=MAXI)
            pe.sem_inc(S["swt_ps"], 1)
            pe.sem_inc(S["sc_ps"], 1)
            with pe.Fori(0, n_items) as i:
                pe.wait_ge(S["xt_sb"], i + 1)
                for part in range(2):
                    pe.wait_ge(S[("gate_sb", "up_sb")[part]], i + 1)
                    for c in range(2):
                        s_ = EXP_SLOT[2 * part + c]
                        pe.wait_ge(full[s_], i * 16 + 16 * (FILLS[s_] + 1))
                        wv = chunk3(s_)
                        for kk in range(CH):
                            kt = c * CH + kk
                            g_ = kt % 4
                            ins = pe.matmul(pb[2 + part][32 * g_:32 * g_ + 32, :], xT[:, kt % 4, kt // 4, :], wv[:, kk, :],
                                            start=(kt < 4), stop=(kt >= KT - 4))
                        ins.then_inc(S["item_chunk"], 1)
                    pe.wait_ge(S["item_chunk"], i * 6 + 2 * part + 2)
                    pe.sem_inc(S[("gate_ps", "up_ps")[part]], 1)
                pe.wait_ge(S["sel_ok"], i + 2)
                gather()
                pe.wait_ge(S["gate_sb"], i + 2)
                pe.wait_ge(S["up_sb"], i + 2)
                for part in range(2):
                    gv = gu[:, part].rearrange("p (f k) -> p f k", k=FK)
                    for k in range(FK):
                        ins = pe.matmul(pb[4][:, part * P + k * CAP:part * P + (k + 1) * CAP], gv[:, :, k], q32,
                                        start=True, stop=True)
                ins.then_inc(S["sum_ps"], 1)
                pe.wait_ge(S["swr_ok"], i + 1)
                for t in range(TT):
                    ins = pe.transpose(pb[5][:, t * P:(t + 1) * P], swr[:, t].rearrange("p a s -> p (a s)"), ident[:])
                ins.then_inc(S["swt_ps"], 1)
                pe.wait_ge(S["xg_sb"], i + 2)
                pe.wait_ge(S["sc_free"], i * 8 + 1)
                gather_turn()
                for c in (4, 5):
                    s_ = EXP_SLOT[c]
                    pe.wait_ge(full[s_], i * 16 + 16 * (FILLS[s_] + 1))
                pe.wait_ge(S["at_ok"], i + 1)
                for n in range(4):
                    if n >= 2:
                        pe.wait_ge(S["dn_sb"], i * 4 + n - 1)
                    for k in range(FK):
                        wv = slot(EXP_SLOT[4 + k // 2]).rearrange("p (k n) -> p k n", k=2)
                        ins = pe.matmul(pb[5 + n % 2][32 * k:32 * k + 32, :], aTe[:, k, :], wv[:, k % 2, n * BLK:(n + 1) * BLK],
                                        start=True, stop=True)
                    ins.then_inc(S["dn_ps"], 1)
                pe.wait_ge(S["dn_ps"], i * 4 + 4)
                pe.sem_inc(S["item_chunk"], 2)
                pe.wait_ge(S["swt_sb"], i + 1)
                pe.wait_ge(S["xt_sb"], i + 2)
                for n in range(4):
                    pe.wait_ge(S["dn_sb"], i * 4 + n + 1)
                    for t in range(TT):
                        m = 2 * n + t
                        if m >= 2:
                            pe.wait_ge(S["sc_free"], i * 8 + m)
                        pe.matmul(pb[(7, 1)[m % 2]][:], swt[:, t * P:(t + 1) * P], ys[:, n], start=True, stop=True).then_inc(S["sc_ps"], 1)


def kernel(**inputs):
    import numpy as np
    import concourse.bacc as bacc
    from concourse.bass_utils import run_bass_kernel_spmd

    nc = bacc.Bacc("TRN2", target_bir_lowering=False, num_devices=1)
    arrays, aps = {}, {}
    given = {k: np.ascontiguousarray(x) for k, x in inputs.items()}
    given["inv_freq"] = (1.0 / (np.float32(10000.0) ** (np.arange(0, HD, 2, dtype=np.float32) / np.float32(HD)))).astype(np.float32)
    for name, x in given.items():
        arrays[f"in_{name}"] = x
        aps[name] = nc.dram_tensor(f"in_{name}", x.shape, mybir.dt.from_np(x.dtype), kind="ExternalInput").ap()
    out = nc.dram_tensor("out_0", (1, T, D), F32, kind="ExternalOutput").ap()
    hybrid_block(nc, aps, out)
    r = run_bass_kernel_spmd(nc, [arrays], core_ids=[0])
    return r.results[0]["out_0"]
```

```python
from contextlib import ExitStack

import concourse.bass as bass
from concourse import mybir

F32 = mybir.dt.float32
F32R = mybir.dt.float32r
I32 = mybir.dt.int32
U32 = mybir.dt.uint32
ALU = mybir.AluOpType
ACT = mybir.ActivationFunctionType
AX = mybir.AxisListType

P = 128
D = 2048
T = 256
TT = T // P
KT = D // P
W = 1024
WK = W // P
BLK = 512
CH = 8
CHF = CH * BLK
HK = CH // 2
HF = HK * BLK
SLOTS = 6
DENSE_SLOTS = 3
PK = 2
PF = PK * BLK
RAW, HIS = 6, 4
G, SP_, SM = 64, 64, 16
PR = G // 2
L = 8
NJ = T // L
NQ = 4
QP = PR // NQ
H, HD = 8, 64
NG, EPG, NE = 4, 8, 32
F = 512
FK = F // P
CAP = 32
MAXI = 48
NORM_EPS, SUBLN_EPS = 1e-6, 1e-5
LAMBDA_INIT = 0.2
SCALE = HD ** -0.5
NEG = -1.0e30
ROUND = 12582912.0
INV_2PI = 0.15915494309189535
C1 = 6.28125
C2 = 0.0019350051879882812
C3 = 3.0199157663412e-07
PI = 3.1415925
GELU_C = 0.044715
GELU_S = 1.5957691216057308


def bc(ap, axis, n):
    a = ap.unsqueeze(axis)
    s = list(a.shape)
    s[axis] = n
    return a.to_broadcast(s)


class Steps:

    def __init__(self, eng, sem):
        self.eng, self.sem, self.n = eng, sem, 0

    def __call__(self, ins):
        ins.then_inc(self.sem, 1)
        self.n += 1
        self.eng.wait_ge(self.sem, self.n)


def hybrid_block(nc, a, out, upto=99, dbg=None):
    ctx = ExitStack()
    with ctx:
        place = {}

        def sb(name, shape, dt=F32):
            t = ctx.enter_context(nc.sbuf_tensor(name, shape, dt))
            place[name] = nc.sbuf_base - 4 * shape[1]
            return t

        def short(name, size):
            return nc.alloc_sbuf_tensor_at(name + "_r", [P, size], F32R, offset=place[name])

        def sem(name):
            return ctx.enter_context(nc.semaphore(name))

        ring = sb("ring", [P, DENSE_SLOTS * CHF])
        s3 = sb("s3", [P, CHF])
        r45 = sb("r45", [P, 2 * CHF])
        xa = sb("xa", [P, TT * D])
        ht = sb("ht", [P, KT * T])
        z = sb("z", [P, TT * 4096])
        st = sb("st", [P, (NJ + 1) * 2 * PR])
        ypk = sb("ypk", [P, 2048])
        sml = sb("sml", [P, 2048])
        par = sb("par", [P, 1056])
        bcw = sb("bcw", [P, 2048])
        rw = sb("rw", [P, KT * (NG + NE)])
        wp = sb("wp", [P, G * SM])
        ident = sb("ident", [P, P])
        mask = sb("mask", [P, 2 * P])
        ang = sb("ang", [P, 4 * 96])
        ring_r = short("ring", DENSE_SLOTS * CHF)
        r45_r = short("r45", 2 * CHF)
        ht_r, z_r = short("ht", KT * T), short("z", TT * 4096)
        bcw_r = short("bcw", 2048)
        ypk_r, sml_r = short("ypk", 2048), short("sml", 2048)
        pb = [ctx.enter_context(nc.psum_tensor(f"pb{i}", [P, BLK], F32)) for i in range(8)]

        def slot(c):
            t, c = (ring, c) if c < DENSE_SLOTS else (s3, 0) if c == 3 else (r45, c - 4)
            return t[:, c * CHF:(c + 1) * CHF]

        x_t = xa[:].rearrange("p (t d) -> p t d", t=TT)
        h_t = z[:, 0:TT * D].rearrange("p (t d) -> p t d", t=TT)
        hT = ht[:].rearrange("p (k t) -> p k t", k=KT)
        z_t = z[:].rearrange("p (t c) -> p t c", t=TT)
        bp = xa[:, 0:2048].rearrange("p (c q i m) -> p c q i m", c=2, q=QP, i=L)
        tq = xa[:, 2048:4096].rearrange("p (i x) -> p i x", i=L)
        up = xa[:, 2048:4096].rearrange("p (g i m) -> p g i m", g=16, i=L)
        bt = r45[:, 0:2048].rearrange("p (q c x) -> p q c x", q=QP, c=2)
        cbd = r45[:, 2048:4096].rearrange("p (c q h m) -> p c q h m", c=2, q=PR, h=2)
        sbd = r45[:, 0:4096].rearrange("p (c h q j) -> p c h q j", c=2, h=2, q=PR)
        ut = r45[:, 4096:6144].rearrange("p (g f j) -> p g f j", g=16, f=4)
        tmp = r45[:, 6144:8192].rearrange("p (a x) -> p a x", a=2)
        braw = sml[:, 0:1024].rearrange("p (c g q m) -> p c g q m", c=2, g=4, q=8)
        ct = sml[:, 1024:2048].rearrange("p (c g q m) -> p c g q m", c=2, g=4, q=8)
        cn = ypk[:, 0:1024].rearrange("p (c g x) -> p c g x", c=2, g=4)
        yp = ypk[:].rearrange("p (i x) -> p i x", i=L)
        st_j = st[:].rearrange("p (j c q) -> p j c q", c=2, q=PR)
        yg = st[:, 0:2048].rearrange("p (t c) -> p t c", t=TT)
        yT = ypk[:].rearrange("p (k t) -> p k t", k=WK)
        oT = sml[:].rearrange("p (k t) -> p k t", k=WK)
        o = [0]

        def pv(n):
            o[0] += n
            return par[:, o[0] - n:o[0]]

        lam3 = pv(96)
        lr, li, ldt = lam3[:, 0:32], lam3[:, 32:64], lam3[:, 64:96]
        dt_, mag, nr, den, fr, fi, pt = pv(32), pv(32), pv(32), pv(32), pv(32), pv(32), pv(64)
        apw = pv(4 * 64).rearrange("p (k c q) -> p k c q", k=4, c=2)
        a8 = pv(128)
        w1c, w2c = pv(16), pv(16)
        ss = pv(8)
        lamv = pv(8)
        assert o[0] <= 1056
        p32 = ypk[0:32, 1408:1792]
        dt32 = ypk[0:32, 1792:1794]
        invf = sb("invf", [P, 32])
        posi = sb("posi", [P, TT], I32)
        posf = sb("posf", [P, TT])
        lamw = ypk[:, 1024:1344]
        subw = sb("subw", [P, P])
        qk = z_t[:, :, W:3 * W]
        qkT = r45[:, 0:4096].rearrange("p (h t) -> p h t", h=2 * H)
        rt = ypk[:].rearrange("p (a h d) -> p a h d", a=4, h=2 * H)
        sm_ = r45[:, 4096:5120].rearrange("p (c x) -> p c x", c=2)
        ex = r45[:, 5120:6144].rearrange("p (c x) -> p c x", c=2)
        am = r45[:, 6144:6656]
        aT = r45[:, 6656:7168]
        sc8 = r45[:, 7168:7232]
        oa = xa[:, 0:2048].rearrange("p (t c) -> p t c", t=TT)
        osq = xa[:, 2048:4096].rearrange("p (t c) -> p t c", t=TT)
        gs_t = s3[:].rearrange("p (t c) -> p t c", t=TT)
        ga_t = z_t[:, :, W:3 * W]

        HTL = DENSE_SLOTS * CHF - 2048

        def raw_piece(p):
            r = p % RAW
            o_ = (r if r < 4 else r + HIS) * PF
            return slice(o_, o_ + PF)

        def hi_piece(p):
            o_ = (4 + p % HIS) * PF
            return slice(o_, o_ + PF)

        def low_h(n):
            if n < 4:
                return bcw_r[:, n * BLK:(n + 1) * BLK], bcw[:, n * BLK:(n + 1) * BLK]
            o_ = HTL + (n - 4) * BLK
            return ring_r[:, o_:o_ + BLK], ring[:, o_:o_ + BLK]

        hT_lo = [low_h(kt // 2)[0][:, (kt % 2) * T:(kt % 2 + 1) * T] for kt in range(KT)]
        d_b = sml[:, 0:W]
        glu_bb = wp[:, 0:W]

        yT_hi = ypk_r[:].rearrange("p (k t) -> p k t", k=WK)
        oT_hi = sml_r[:].rearrange("p (k t) -> p k t", k=WK)
        mT_hi = ht_r[:].rearrange("p (k t) -> p k t", k=KT)

        def pieces(base, rows):
            v = [z_r[:, 4096 * i + base:4096 * i + base + rows * T].rearrange("p (k t) -> p k t", k=rows) for i in range(2)]
            return [v[k // rows][:, k % rows] for k in range(2 * rows)], [v[n // (rows // 2)][:, 2 * (n % (rows // 2)):2 * (n % (rows // 2)) + 2]
                                                                         for n in range(rows)]

        yT_lo, yT_lo2 = pieces(0, 4)
        oT_lo, oT_lo2 = pieces(3 * W, 4)
        mT_lo, mT_lo2 = pieces(W, 8)

        def hi_slot(hc):
            i = 2 + hc % 2 if hc < 6 else (hc + 2) % 4
            return slice(i * HF, (i + 1) * HF)

        def raw_half(hc):
            k = hc // 2
            o_ = (k % DENSE_SLOTS) * CHF + (hc % 2) * HF
            return slice(o_, o_ + HF)

        h2 = h_t
        gu = z[:, 4096:5120].rearrange("p (c f) -> p c f", c=2)
        ys = z[:, 5120:7168].rearrange("p (n d) -> p n d", n=4)
        xg = z[:, 7168:7680]
        aTe = z[:, 7680:7808].rearrange("p (k s) -> p k s", k=FK)
        sge = z[:, 7808:7936]
        lg = z[:, 7936:8008].rearrange("p (t e) -> p t e", t=TT)
        lt = yT[:, 0, 0:P]
        ones = yT[:, 0, P:2 * P]
        iota = yT[:, 1, 0:P].rearrange("p (a s) -> p a s", a=4)
        q32 = yT[:, 1, P:P + 32]
        thr = yT[:, 1, P + 32:P + 40]
        i48 = oT[0:1, :, :].rearrange("p k t -> p (k t)")[:, 0:MAXI * NE].rearrange("p (i e) -> p i e", i=MAXI)
        cmp48 = bcw[0:1, 0:MAXI * NE].rearrange("p (i e) -> p i e", i=MAXI)
        rs = st[:, 0:1600]
        xT = ht[:, 0:512].rearrange("p (j n s) -> p j n s", j=4, n=4)
        sel = ht[:, 512:576].rearrange("p (t s) -> p t s", t=TT)
        swr = ht[:, 576:832].rearrange("p (t a s) -> p t a s", t=TT, a=4)
        swt = ht[:, 832:1088]
        swa = ht[:, 1088:1344].rearrange("p (t a s) -> p t a s", t=TT, a=4)
        sela = ht[:, 1344:1408].rearrange("p (t s) -> p t s", t=TT)
        rem = ang[:, 0:4].rearrange("p (t k) -> p t k", t=TT)
        gw = ang[:, 4:8].rearrange("p (t k) -> p t k", t=TT)
        tabf = ang[0:1, 96:96 + 1 + MAXI]
        tab = ang[0:1, 160:160 + 1 + MAXI].bitcast(I32)
        rwv = rw[:].rearrange("p (k e) -> p k e", k=KT)

        S = {n: sem(n) for n in (
            "x_in norms_in lam_in dt_in b_in c_in consts_in rw_in ident_ok mask_ok st0_ok "
            "ss_done root_done h_done dve act pool pe_params "
            "v_ready v_free a_ready a_free chunk_used blk_ready blk_free out_free dt_spread "
            "dt_done mag_done arg_done sin_done lamx_in_done apow_done bp_ok bp_used bt_ok ct_ok cbd_ok "
            "uqkv_done up_ok uj_in ut_ok wp_ok s_used tq_zero tq_in tq_used ca_ok ca_used sbd_ok yp_ok yp_in "
            "gel_in gel_sig gelu_ok qk_rot qkT_ok nmx_ok ex_ok am_ok aT_ok aT_used o_ok osq_ok ort_ok oa_ok gates_ok "
            "glu_pre glu_sig y2_ok yT_ok oT_ok y2T_ok mrg_ok mT_ok x_again x2_ok scan cbd_zero sbd_zero "
            "lsum_ok lexp_ok mT_ps xfree ss2_done root2_done h2_ok h2T_ok lg_ps gex_in gex_ok pex_ok m_ok cnt_ps tab_ok iota_ok fw_in "
            "sel_ok xg_ps xg_sb xt_ps xt_sb gate_ps gate_sb up_ps up_sb sum_ps sig_ok swr_ok swt_ps swt_sb at_ok dn_ps dn_sb "
            "piece_used whi_ok wlo_ok hx_ok hl_ok d_in gb_in hi_ok lo_ok half_used alo_ok si_ok istep sc_ps sc_free item_chunk moe_ok fss_done froot_done out_ok out_in").split()}
        full = [sem(f"slot{i}_full") for i in range(SLOTS)]
        first_full = [sem(f"first_half{i}_full") for i in range(2)]
        w_full = [sem(f"piece{i}_full") for i in range(RAW)]

        block = ctx.enter_context(nc.Block())

        PE_A = (5, 7, 9, 11)
        PE_C = (17, 18, 19, 20)
        PE_QK = 21
        PE_ROUND = 22
        LO_A0 = 2 + 4 + 4 * NQ + NQ + 8 + 2 * 6

        def blocks_of(wap, kt_total):
            return wap.rearrange("(p k) n -> p k n", k=kt_total)

        win = blocks_of(a["w_in"][0], KT)
        glu = blocks_of(a["ssm_glu_w"][0], WK)
        wps = blocks_of(a["w_proj_ssm"][0], WK)
        wpa = blocks_of(a["w_proj_attn"][0], WK)
        wout = blocks_of(a["w_out"][0], KT)
        x_d = a["x"][0].rearrange("(t p) d -> p t d", p=P)
        out_d = out[0].rearrange("(t p) d -> p t d", p=P)

        def chunk3(c):
            return slot(c).rearrange("p (k n) -> p k n", k=CH)

        dense = []
        for n in range(2):
            dense.append(glu[:, :, n * BLK:(n + 1) * BLK])
        for n in range(4):
            dense.append(wps[:, :, n * BLK:(n + 1) * BLK])
            dense.append(wpa[:, :, n * BLK:(n + 1) * BLK])
        for n in range(4):
            for c in range(2):
                dense.append(wout[:, c * CH:(c + 1) * CH, n * BLK:(n + 1) * BLK])
        N_WIN = 32
        N_PIECE = N_WIN * CH // PK
        PPC = CH // PK
        N_DENSE = len(dense)
        N_HALF = 2 * len(dense)
        EXP_SLOT = (3, 0, 1, 5, 4, 2)
        FILLS = [len(range(s, N_DENSE, DENSE_SLOTS)) - (s == 0) for s in range(DENSE_SLOTS)] + [0, 0, 0]

        @block.sync
        def _(sp):
            for t in range(TT):
                sp.dma_start(x_t[:, t, :], x_d[:, t, :]).then_inc(S["x_in"], 16)

            for p in range(N_PIECE):
                if p >= RAW:
                    sp.wait_ge(S["piece_used"], p - RAW + 1)
                b, c = p // (2 * PPC), p % (2 * PPC)
                sp.dma_start(ring[:, raw_piece(p)].rearrange("p (k n) -> p k n", k=PK),
                             win[:, c * PK:(c + 1) * PK, b * BLK:(b + 1) * BLK]).then_inc(w_full[p % RAW], 16)
                if p == 4 * PPC + RAW + 1:
                    sp.wait_ge(S["blk_free"], 4)
                    sp.wait_ge(S["a_free"], 2)
                    sp.wait_ge(S["lsum_ok"], 1)
                    for f in range(4):
                        for t in range(TT):
                            sp.dma_start(yp[32 * f + 16 * t:32 * f + 16 * t + 16],
                                         z_t[:, t, f * 256:(f + 1) * 256]).then_inc(S["uj_in"], 16)
                for q in range(NQ):
                    if p == ((PE_A[3] + 1) if q == 0 else (PE_C[q - 1] + 1)) * PPC + RAW:
                        if q == 0:
                            sp.wait_ge(S["tq_zero"], 1)
                            sp.wait_ge(S["wp_ok"], NQ)
                            sp.wait_ge(S["bp_ok"], NQ)
                            sp.dma_start(d_b, a["ssm_d"][0].partition_broadcast(P)).then_inc(S["d_in"], 16)
                        else:
                            sp.wait_ge(S["tq_used"], q)
                        for i in range(L):
                            sp.dma_start(tq[0:SM * (i + 1), i, :],
                                         wp[SM * (L - 1 - i):P, q * 256:(q + 1) * 256]).then_inc(S["tq_in"], 16)
                if p == (PE_C[3] + 1) * PPC + RAW:
                    sp.wait_ge(S["yp_ok"], 1)
                    for f in range(4):
                        for t in range(TT):
                            sp.dma_start(yg[:, t, f * 256:(f + 1) * 256],
                                         yp[32 * f + 16 * t:32 * f + 16 * t + 16]).then_inc(S["yp_in"], 16)
                    sp.wait_ge(S["tq_in"], 16 * L * NQ)
                    sp.dma_start(glu_bb, a["ssm_glu_b"][0].partition_broadcast(P)).then_inc(S["gb_in"], 16)

            sp.wait_ge(S["piece_used"], N_PIECE)
            for k in range(N_DENSE):
                if k >= DENSE_SLOTS:
                    sp.wait_ge(S["chunk_used"], k - DENSE_SLOTS + 1)
                if k == 0:
                    for c in range(2):
                        sp.dma_start(chunk3(0)[:, c * HK:(c + 1) * HK], dense[0][:, c * HK:(c + 1) * HK]).then_inc(first_full[c], 16)
                else:
                    sp.dma_start(chunk3(k % DENSE_SLOTS), dense[k]).then_inc(full[k % DENSE_SLOTS], 16)
                if k == 10:
                    sp.wait_ge(S["xfree"], 1)
                    for t in range(TT):
                        sp.dma_start(x_t[:, t, :], x_d[:, t, :]).then_inc(S["x_again"], 16)

            def expert_chunks(e):
                for name in ("expert_w_gate", "expert_w_up"):
                    w = a[name][0, e].rearrange("e (p k) n -> p (e k) n", k=KT)
                    for c in range(2):
                        yield w[:, c * CH:(c + 1) * CH, :], "k"
                w = a["expert_w_down"][0, e].rearrange("e (p k) n -> p (e k) n", k=FK)
                for c in range(2):
                    yield w[:, 2 * c:2 * c + 2, :], "d"

            def fill(c, src, kind):
                s_ = EXP_SLOT[c]
                dst = chunk3(s_) if kind == "k" else slot(s_).rearrange("p (k n) -> p k n", k=2)
                sp.dma_start(dst, src).then_inc(full[s_], 16)

            for c, (src, kind) in enumerate(expert_chunks(bass.ds(0, 1))):
                if c == 0:
                    sp.wait_ge(S["mT_ps"], 1)
                elif c == 3:
                    sp.wait_ge(S["half_used"], N_HALF - 2)
                elif c == 4:
                    sp.wait_ge(S["half_used"], N_HALF)
                else:
                    sp.wait_ge(S["chunk_used"], N_DENSE - (3 - c if c < 3 else 0))
                fill(c, src, kind)
            sp.wait_ge(S["tab_ok"], 1)
            n_items = sp.value_load(tab[:, 0:1], min_val=1, max_val=MAXI)
            with sp.If(n_items > 1):
                with sp.Fori(1, n_items) as i:
                    e = sp.value_load(tab[:, bass.ds(i + 1, 1)], min_val=0, max_val=NE - 1)
                    for c, (src, kind) in enumerate(expert_chunks(bass.ds(e, 1))):
                        sp.wait_ge(S["item_chunk"], i * 6 + c - 5)
                        fill(c, src, kind)
            for t in range(TT):
                sp.wait_ge(S["out_ok"], t + 1)
                sp.dma_start(out_d[:, t, :], x_t[:, t, :]).then_inc(S["out_in"], 16)
            sp.wait_ge(S["out_in"], 16 * TT)

        @block.scalar
        def _(act):
            steps = Steps(act, S["act"])
            act.dma_start(w1c, a["norm1_w"][0].rearrange("(p k) -> p k", k=KT)).then_inc(S["norms_in"], 16)
            act.dma_start(w2c, a["norm2_w"][0].rearrange("(p k) -> p k", k=KT)).then_inc(S["norms_in"], 16)
            for n, name in enumerate(("ssm_lambda_re", "ssm_lambda_im")):
                src = a[name][0].rearrange("(g q r h) p -> q g r (h p)", g=4, q=NQ, h=2)
                for q in range(NQ):
                    act.dma_start(p32[q * 8:(q + 1) * 8, n * P:(n + 1) * P], src[q]).then_inc(S["lam_in"], 16)
            src = a["ssm_log_dt"][0].rearrange("(g q r h) -> q g r h", g=4, q=NQ, h=2)
            for q in range(NQ):
                act.dma_start(dt32[q * 8:(q + 1) * 8, :], src[q]).then_inc(S["dt_in"], 16)
            act.dma_start(invf[:], a["inv_freq"].partition_broadcast(P)).then_inc(S["consts_in"], 16)
            with nc.allow_non_contiguous_dma(reason="256 positions, one per partition"):
                act.dma_start(posi[:], a["positions"][0].rearrange("(t p) -> p t", p=P)).then_inc(S["consts_in"], 16)
            for n, name in enumerate(("q1", "k1", "q2", "k2")):
                act.dma_start(lamw[:, n * 64:(n + 1) * 64],
                              a[f"attn_lambda_{name}"][0].partition_broadcast(P)).then_inc(S["consts_in"], 16)
            act.dma_start(subw[:], a["attn_subln_w"][0].partition_broadcast(P)).then_inc(S["consts_in"], 16)
            act.wait_ge(S["x_in"], 32)
            for t in range(TT):
                act.activation(h_t[:, t, :], x_t[:, t, :], ACT.Square, accum_out=ss[:, t:t + 1]).then_inc(S["ss_done"], 1)
            act.wait_ge(S["root_done"], 1)
            act.activation(ss[:, 4:6], ss[:, 2:4], ACT.Sqrt).then_inc(S["ss_done"], 1)

            def high_w(p):
                if p >= N_PIECE:
                    return
                act.wait_ge(w_full[p % RAW], 16 * (p // RAW + 1))
                if p >= HIS:
                    act.wait_ge(S["piece_used"], p - HIS + 1)
                act.activation(ring_r[:, hi_piece(p)], ring[:, raw_piece(p)], ACT.Copy).then_inc(S["whi_ok"], 1)

            for p in range(HIS):
                high_w(p)
            for n in range(8):
                act.wait_ge(S["v_free"], n + 2)
                act.activation(ht_r[:, n * BLK:(n + 1) * BLK], low_h(n)[1], ACT.Copy).then_inc(S["hx_ok"], 1)
            act.wait_ge(S["pe_params"], 1)
            act.activation(dt_, ldt, ACT.Exp).then_inc(S["dt_done"], 1)
            act.wait_ge(S["arg_done"], 1)
            act.activation(mag, nr, ACT.Exp).then_inc(S["mag_done"], 1)
            act.wait_ge(S["lsum_ok"], 1)
            act.activation(lamv[:, 2:4], lamv[:, 0:2], ACT.Exp).then_inc(S["lexp_ok"], 1)
            act.wait_ge(S["arg_done"], 2)
            act.activation(ang[:, 192:288], ang[:, 96:192], ACT.Sin).then_inc(S["sin_done"], 1)
            act.activation(ang[:, 288:384], ang[:, 96:192], ACT.Sin, scale=0.5).then_inc(S["sin_done"], 1)

            aj = [0]

            def a_job(out_, cols, func=ACT.Copy):
                n = aj[0]
                aj[0] += 1
                act.wait_ge(S["a_ready"], n + 1)
                act.activation(out_, pb[6 + n % 2][:, 0:cols] if len(out_.shape) == 2 else out_x(out_, n, cols),
                               func).then_inc(S["a_free"], 1)

            def out_x(out_, n, cols):
                v = pb[6 + n % 2][:, 0:cols]
                if len(out_.shape) == 3:
                    return v.rearrange("p (a b) -> p a b", a=out_.shape[1])
                return v.rearrange("p (a b c) -> p a b c", a=out_.shape[1], b=out_.shape[2])

            for c in range(2):
                a_job(ct[:, c].rearrange("p g q m -> p (g q m)"), BLK)

            def block_out(b):
                for t in range(TT):
                    act.wait_ge(S["blk_ready"], 2 * b + t + 1)
                    if b < 8:
                        dst = z_t[:, t, b * BLK:(b + 1) * BLK]
                    elif b < 12:
                        dst = gs_t[:, t, (b - 8) * BLK:(b - 7) * BLK]
                    else:
                        dst = ga_t[:, t, (b - 12) * BLK:(b - 11) * BLK]
                    act.activation(dst, pb[2 * (b % 2) + t][:], ACT.Copy if b < 8 else ACT.Sigmoid).then_inc(S["blk_free"], 1)

            def u_out():
                for n in range(4):
                    a_job(ut[:, 4 * n:4 * n + 4].rearrange("p g f j -> p (g f j)"), BLK)

            def stage_a(q):
                for h in range(4):
                    if q and h == 0:
                        act.wait_ge(S["s_used"], q)
                    a_job(bt[:, 2 * h:2 * h + 2].rearrange("p q c x -> p (q c x)"), BLK)

            def stage_c(q):
                if q == 0:
                    act.wait_ge(S["qk_rot"], 1)
                n = aj[0]
                act.wait_ge(S["a_ready"], n + 1)
                aj[0] += 1
                act.activation(yp.rearrange("p i (g m) -> p g i m", g=16)[:, 4 * q:4 * q + 4],
                               pb[6 + n % 2][:].rearrange("p (g i m) -> p g i m", g=4, i=L),
                               ACT.Copy).then_inc(S["a_free"], 1)

            def exps(r):
                nh, K = (4, P) if r < 2 else (2, 2 * P)
                act.wait_ge(S["nmx_ok"], r + 1)
                if r:
                    act.wait_ge(S["am_ok"], r)
                for c in range(2):
                    for h in range(nh):
                        act.activation(ex[:, c, h * K:(h + 1) * K], sm_[:, c, h * K:(h + 1) * K], ACT.Exp,
                                       bias=sc8[:, 8 + c * 4 + h:9 + c * 4 + h], scale=SCALE,
                                       accum_out=sc8[:, 16 + c * 4 + h:17 + c * 4 + h]).then_inc(S["ex_ok"], 1)

            def high(hc):
                k = hc // 2
                if k == 0:
                    act.wait_ge(first_full[hc], 16)
                else:
                    act.wait_ge(full[k % DENSE_SLOTS], 16 * (k // DENSE_SLOTS + (k % DENSE_SLOTS > 0)))
                if 2 <= hc < 6:
                    act.wait_ge(S["half_used"], hc - 1)
                elif 6 <= hc < 8:
                    act.wait_ge(S["y2_ok"], 1)
                elif hc >= 8:
                    act.wait_ge(S["half_used"], hc - 3)
                act.activation(r45_r[:, hi_slot(hc)], ring[:, raw_half(hc)], ACT.Copy).then_inc(S["hi_ok"], 1)

            def round_out(r):
                nh = 4 if r < 2 else 2
                a_job(aT, BLK)
                t = 0 if r < 2 else 1
                h0 = 4 * r if r < 2 else 2 * (r - 2)
                a_job(oa[:, t, h0 * P:(h0 + nh) * P], nh * P)

            for c in range(N_WIN):
                r = c - PE_ROUND
                high_w(PPC * (c + 1))
                if 0 <= r < 6:
                    exps(r)
                for p in range(1, PPC):
                    high_w(PPC * (c + 1) + p)
                if c % 2:
                    block_out(c // 2)
                if c == PE_A[0]:
                    u_out()
                if c in PE_A:
                    stage_a(PE_A.index(c))
                if c in PE_C:
                    stage_c(PE_C.index(c))
                if c == PE_QK:
                    for n in range(8):
                        a_job(qkT[:, 2 * n:2 * n + 2].rearrange("p h t -> p (h t)"), BLK)
                if 0 <= r < 6:
                    round_out(r)
                if c == PE_ROUND + 6:
                    act.wait_ge(S["osq_ok"], 1)
                    act.activation(sc8[:, 40:56], sc8[:, 24:40], ACT.Sqrt).then_inc(S["ort_ok"], 1)
                if c == N_WIN - 2:
                    act.wait_ge(S["gel_in"], 1)
                    act.activation(r45[:, 2048:4096], r45[:, 0:2048], ACT.Sigmoid, scale=GELU_S).then_inc(S["gel_sig"], 1)
            for n in range(4):
                a_job(oT_hi[:, 2 * n:2 * n + 2].rearrange("p k t -> p (k t)"), BLK)
            for n in range(4):
                if n == 0:
                    act.wait_ge(S["yp_in"], 16 * 8)
                a_job(yT_hi[:, 2 * n:2 * n + 2].rearrange("p k t -> p (k t)"), BLK)
            for hc in range(5):
                high(hc)
            act.wait_ge(S["glu_pre"], 1)
            act.activation(r45[:, 0:2048], r45[:, 0:2048], ACT.Sigmoid).then_inc(S["glu_sig"], 1)
            high(5)
            for n in range(4):
                a_job(yT_hi[:, 2 * n:2 * n + 2].rearrange("p k t -> p (k t)"), BLK)
            for hc in range(6, 24):
                high(hc)
            for n in range(8):
                a_job(mT_hi[:, 2 * n:2 * n + 2].rearrange("p k t -> p (k t)"), BLK)
            for hc in range(24, N_HALF):
                high(hc)
            act.wait_ge(S["x2_ok"], 1)
            for t in range(TT):
                act.activation(h2[:, t, :], x_t[:, t, :], ACT.Square, accum_out=ss[:, t:t + 1]).then_inc(S["ss2_done"], 1)
            act.wait_ge(S["root2_done"], 1)
            act.activation(ss[:, 4:6], ss[:, 2:4], ACT.Sqrt).then_inc(S["ss2_done"], 1)
            act.wait_ge(S["gex_in"], 1)
            act.activation(rs[:, 64:74], rs[:, 48:58], ACT.Exp).then_inc(S["gex_ok"], 1)
            act.wait_ge(S["xg_ps"], 1)
            act.activation(xg, pb[0][:], ACT.Copy).then_inc(S["xg_sb"], 1)
            act.wait_ge(S["tab_ok"], 1)
            n_items = act.value_load(tab[:, 0:1], min_val=1, max_val=MAXI)
            act.sem_inc(S["gate_sb"], 1)
            with act.Fori(0, n_items) as i:
                act.wait_ge(S["gate_ps"], i + 1)
                act.activation(gu[:, 0], pb[2][:], ACT.Copy).then_inc(S["gate_sb"], 1)
                act.wait_ge(S["xt_ps"], i + 1)
                act.wait_ge(S["xg_ps"], i + 2)
                act.activation(xg, pb[0][:], ACT.Copy).then_inc(S["xg_sb"], 1)
                act.wait_ge(S["sum_ps"], i + 1)
                act.activation(sge, pb[4][:, 0:P], ACT.Sigmoid).then_inc(S["sig_ok"], 1)
                act.wait_ge(S["sc_ps"], i * 8 + 1)
                for n in range(4):
                    act.wait_ge(S["dn_ps"], i * 4 + n + 1)
                    act.activation(ys[:, n], pb[5 + n % 2][:], ACT.Copy).then_inc(S["dn_sb"], 1)
            act.wait_ge(S["moe_ok"], 1)
            for t in range(TT):
                act.activation(h2[:, t, :], x_t[:, t, :], ACT.Square, accum_out=ss[:, t:t + 1]).then_inc(S["fss_done"], 1)
            act.wait_ge(S["froot_done"], 1)
            act.activation(ss[:, 4:6], ss[:, 2:4], ACT.Sqrt).then_inc(S["fss_done"], 1)

        @block.gpsimd
        def _(pool):
            steps = Steps(pool, S["pool"])
            steps(pool.memset(ident[:], 0.0))
            pool.affine_select(out=ident[:], in_=ident[:], compare_op=ALU.not_equal, fill=1.0, base=0,
                               pattern=[[-1, P]], channel_multiplier=1).then_inc(S["ident_ok"], 1)
            for n, name in enumerate(("ssm_c_re", "ssm_c_im")):
                for g in range(4):
                    s_ = a[name][0, 16 * g:16 * g + 16].rearrange("(q h) m p -> h q m p", h=2)
                    for h in range(2):
                        pool.dma_start(cn[:, n, g, h * 64:(h + 1) * 64], s_[h]).then_inc(S["c_in"], 16)
            for n, name in enumerate(("ssm_b_re", "ssm_b_im")):
                pool.dma_start(braw[:, n].rearrange("p g q m -> p (g q) m"),
                              a[name][0].rearrange("(q h) p m -> (h p) q m", h=2)).then_inc(S["b_in"], 16)
            pool.dma_start(rwv[:, :, 0:NG], a["router_group_w"][0].rearrange("(p k) e -> p k e", k=KT)).then_inc(S["rw_in"], 16)
            pool.dma_start(rwv[:, :, NG:NG + NE], a["router_expert_w"][0].rearrange("(p k) e -> p k e", k=KT)).then_inc(S["rw_in"], 16)
            steps(pool.memset(mask[:], 0.0))
            pool.affine_select(out=mask[:, P:2 * P], in_=mask[:, P:2 * P], compare_op=ALU.is_ge, fill=NEG, base=0,
                               pattern=[[-1, P]], channel_multiplier=1).then_inc(S["mask_ok"], 1)
            pool.memset(r45[:, 2048:4096], 0.0).then_inc(S["cbd_zero"], 1)
            pool.memset(st_j[:, 0], 0.0).then_inc(S["st0_ok"], 1)

            def low_w(p):
                pool.wait_ge(S["whi_ok"], p + 1)
                pool.tensor_tensor(ring_r[:, raw_piece(p)], ring[:, raw_piece(p)], ring_r[:, hi_piece(p)].bitcast(F32),
                                   ALU.subtract).then_inc(S["wlo_ok"], 1)

            for p in range(N_PIECE):
                low_w(p)
                if p == PPC * (PE_A[0] + 1) - 1:
                    pool.wait_ge(S["uj_in"], 16 * 8)
                    pool.wait_ge(S["h_done"], 2)
                    pool.tensor_copy(up, yp.rearrange("p i (g m) -> p g i m", g=16)).then_inc(S["up_ok"], 1)
                if p == PPC * (PE_A[0] + 2) - 1:
                    pool.wait_ge(S["ut_ok"], 1)
                    pool.memset(xa[:, 2048:4096], 0.0).then_inc(S["tq_zero"], 1)
            pool.wait_ge(S["x2_ok"], 1)
            steps(pool.memset(yT[:, 0], 1.0))
            pool.affine_select(out=lt, in_=lt, compare_op=ALU.is_gt, fill=0.0, base=0,
                               pattern=[[1, P]], channel_multiplier=-1)
            pool.iota(iota, pattern=[[0, 4], [1, CAP]], base=0, channel_multiplier=0, allow_small_or_imprecise_dtypes=True)
            pool.iota(thr, pattern=[[CAP, 8]], base=0, channel_multiplier=0, allow_small_or_imprecise_dtypes=True)
            steps(pool.iota(i48, pattern=[[1, MAXI], [0, NE]], base=0, channel_multiplier=0, allow_small_or_imprecise_dtypes=True))
            pool.sem_inc(S["iota_ok"], 1)
            pool.wait_ge(S["tab_ok"], 1)
            pool.dma_start(bcw[:], a["final_norm_w"].partition_broadcast(P)).then_inc(S["fw_in"], 16)
            pool.wait_ge(S["fw_in"], 16)

        @block.vector
        def _(v):
            steps = Steps(v, S["dve"])
            vj = [0]

            def v_bank():
                n = vj[0]
                vj[0] += 1
                v.wait_ge(S["v_ready"], n + 1)
                return pb[4 + n % 2]

            v.wait_ge(S["dt_in"], 64)
            v.tensor_copy(p32[:, 2 * P:3 * P].rearrange("p (h s) -> p h s", h=2), bc(dt32, 2, 64)).then_inc(S["dt_spread"], 1)
            v.wait_ge(S["ss_done"], 2)
            v.tensor_scalar(ss[:, 2:4], ss[:, 0:2], 1.0 / D, NORM_EPS, ALU.mult, ALU.add).then_inc(S["root_done"], 1)
            v.wait_ge(S["ss_done"], 3)
            steps(v.reciprocal(ss[:, 6:8], ss[:, 4:6]))
            for t in range(TT):
                ins = v.tensor_scalar(h_t[:, t, :], x_t[:, t, :], ss[:, 6 + t:7 + t], None, ALU.mult)
                ins.then_inc(S["h_done"], 1) if t == 0 else ins.then_inc(S["h_done"], 1)
            bank = v_bank()
            v.tensor_copy(lam3, bank[:, 0:96]).then_inc(S["v_free"], 1)
            v.wait_ge(S["v_free"], 1)
            v.sem_inc(S["pe_params"], 1)
            v.wait_ge(S["norms_in"], 32)

            def low_hT(n):
                lo_, f = low_h(n)
                v.wait_ge(S["hx_ok"], n + 1)
                v.tensor_tensor(lo_, f, ht_r[:, n * BLK:(n + 1) * BLK].bitcast(F32), ALU.subtract).then_inc(S["hl_ok"], 1)

            for n in range(8):
                bank = v_bank()
                v.tensor_tensor(low_h(n)[1].rearrange("p (k t) -> p k t", k=2), bank[:].rearrange("p (k t) -> p k t", k=2),
                                bc(w1c[:, 2 * n:2 * n + 2], 2, T), ALU.mult).then_inc(S["v_free"], 1)
                if n:
                    low_hT(n - 1)
            low_hT(7)
            v.wait_ge(S["dt_done"], 1)
            steps(v.tensor_tensor(nr, lr, dt_, ALU.mult))
            v.sem_inc(S["arg_done"], 1)
            v.tensor_tensor(ang[:, 0:32], li, dt_, ALU.mult)
            v.wait_ge(S["consts_in"], 16 * 7)
            steps(v.tensor_copy(posf[:], posi[:]))
            for t in range(TT):
                steps(v.tensor_scalar(ang[:, 32 + 32 * t:64 + 32 * t], invf[:], posf[:, t:t + 1], None, ALU.mult))
            for n in range(2):
                steps(v.tensor_tensor(lamw[:, 256:320], lamw[:, n * 128:n * 128 + 64], lamw[:, n * 128 + 64:n * 128 + 128], ALU.mult))
                steps(v.tensor_reduce(lamv[:, n:n + 1], lamw[:, 256:320], AX.X, ALU.add))
            v.sem_inc(S["lsum_ok"], 1)
            kf, r_ = ang[:, 192:288], ang[:, 96:192]
            steps(v.tensor_scalar(kf, ang[:, 0:96], INV_2PI, ROUND, ALU.mult, ALU.add))
            steps(v.tensor_scalar(kf, kf, ROUND, None, ALU.subtract))
            steps(v.scalar_tensor_tensor(r_, kf, -C1, ang[:, 0:96], ALU.mult, ALU.add))
            steps(v.scalar_tensor_tensor(r_, kf, -C2, r_, ALU.mult, ALU.add))
            steps(v.scalar_tensor_tensor(r_, kf, -C3, r_, ALU.mult, ALU.add))
            steps(v.tensor_scalar(r_, r_, PI, -PI, ALU.min, ALU.max))
            v.sem_inc(S["arg_done"], 1)
            v.wait_ge(S["lexp_ok"], 1)
            steps(v.tensor_tensor(lamv[:, 4:5], lamv[:, 3:4], lamv[:, 2:3], ALU.subtract))
            steps(v.tensor_scalar(lamv[:, 5:6], lamv[:, 4:5], LAMBDA_INIT, None, ALU.subtract))
            v.wait_ge(S["sin_done"], 2)
            steps(v.tensor_tensor(ang[:, 0:96], ang[:, 288:384], ang[:, 288:384], ALU.mult))
            steps(v.tensor_scalar(ang[:, 0:96], ang[:, 0:96], -2.0, 1.0, ALU.mult, ALU.add))
            v.wait_ge(S["mag_done"], 1)
            A1 = apw[:, 0]
            v.tensor_tensor(A1[:, 0], mag, ang[:, 0:32], ALU.mult)
            steps(v.tensor_tensor(A1[:, 1], mag, ang[:, 192:224], ALU.mult))
            v.tensor_scalar(nr, A1[:, 0], 1.0, None, ALU.subtract)
            v.tensor_tensor(pt[:, 0:32], lr, lr, ALU.mult)
            steps(v.tensor_tensor(pt[:, 32:64], li, li, ALU.mult))
            steps(v.tensor_tensor(den, pt[:, 0:32], pt[:, 32:64], ALU.add))
            steps(v.reciprocal(den, den))
            v.tensor_tensor(pt[:, 0:32], nr, lr, ALU.mult)
            steps(v.tensor_tensor(pt[:, 32:64], A1[:, 1], li, ALU.mult))
            steps(v.tensor_tensor(fr, pt[:, 0:32], pt[:, 32:64], ALU.add))
            v.tensor_tensor(fr, fr, den, ALU.mult)
            v.tensor_tensor(pt[:, 0:32], A1[:, 1], lr, ALU.mult)
            steps(v.tensor_tensor(pt[:, 32:64], nr, li, ALU.mult))
            steps(v.tensor_tensor(fi, pt[:, 0:32], pt[:, 32:64], ALU.subtract))
            steps(v.tensor_tensor(fi, fi, den, ALU.mult))
            for k in range(3):
                Ak, An = apw[:, k], apw[:, k + 1]
                v.tensor_tensor(pt[:, 0:32], Ak[:, 0], Ak[:, 0], ALU.mult)
                v.tensor_tensor(pt[:, 32:64], Ak[:, 1], Ak[:, 1], ALU.mult)
                steps(v.tensor_tensor(An[:, 1], Ak[:, 0], Ak[:, 1], ALU.mult))
                v.tensor_tensor(An[:, 0], pt[:, 0:32], pt[:, 32:64], ALU.subtract)
                steps(v.tensor_scalar(An[:, 1], An[:, 1], 2.0, None, ALU.mult))
            v.tensor_copy(a8[:, 0:64].rearrange("p (c q) -> p c q", c=2), bc(apw[:, 3, 0], 1, 2))
            v.tensor_copy(a8[:, 64:96], apw[:, 3, 1])
            steps(v.tensor_scalar(a8[:, 96:128], apw[:, 3, 1], -1.0, None, ALU.mult))
            v.wait_ge(S["a_free"], 2)
            v.wait_ge(S["cbd_zero"], 1)
            for h in range(2):
                rows = slice(64 * h, 64 * h + 64)
                for c in range(2):
                    ins = v.tensor_scalar(cbd[rows, c, :, h, :], ct[rows, c].rearrange("p g q m -> p (g q) m"),
                                          1.0 - 2.0 * c, None, ALU.mult)
            steps(ins)
            v.sem_inc(S["cbd_ok"], 1)

            def quarter(t, q):
                return t[:, :, 2 * q:2 * q + 2, :]

            def cmul(o_re, o_im, i_re, i_im, m_re, m_im, t1, t2):
                v.tensor_tensor(t1, i_re, m_re, ALU.mult)
                steps(v.tensor_tensor(t2, i_im, m_im, ALU.mult))
                steps(v.tensor_tensor(o_re, t1, t2, ALU.subtract))
                v.tensor_tensor(t1, i_re, m_im, ALU.mult)
                steps(v.tensor_tensor(t2, i_im, m_re, ALU.mult))
                steps(v.tensor_tensor(o_im, t1, t2, ALU.add))

            def start_quarter(i, raw, m_re, m_im, q):
                def v4(x):
                    return x.rearrange("p (g r m) -> p g r m", g=4, r=2)

                def par_(x):
                    return bc(x[:, q * QP:(q + 1) * QP].rearrange("p (g r) -> p g r", g=4), 3, SM)

                t1, t2 = tmp[:, 0, 0:128], tmp[:, 1, 0:128]
                r_re, r_im = quarter(raw[:, 0], q), quarter(raw[:, 1], q)
                v.tensor_tensor(v4(t1), r_re, par_(m_re), ALU.mult)
                steps(v.tensor_tensor(v4(t2), r_im, par_(m_im), ALU.mult))
                t3 = t1.rearrange("p (q m) -> p q m", q=QP)
                t4 = t2.rearrange("p (q m) -> p q m", q=QP)
                steps(v.tensor_tensor(bp[:, 0, :, i, :], t3, t4, ALU.subtract))
                v.tensor_tensor(v4(t1), r_re, par_(m_im), ALU.mult)
                steps(v.tensor_tensor(v4(t2), r_im, par_(m_re), ALU.mult))
                steps(v.tensor_tensor(bp[:, 1, :, i, :], t3, t4, ALU.add))

            def raise_(dst, src, n, k, q):
                def x(t):
                    return t.rearrange("p q i m -> p q (i m)")
                sh = n * SM
                def w(t):
                    return t[:, 0:QP * sh].rearrange("p (q x) -> p q x", q=QP)
                cmul(x(bp[:, 0, :, dst:dst + n]), x(bp[:, 1, :, dst:dst + n]),
                     x(bp[:, 0, :, src:src + n]), x(bp[:, 1, :, src:src + n]),
                     bc(apw[:, k, 0, q * QP:(q + 1) * QP], 2, sh), bc(apw[:, k, 1, q * QP:(q + 1) * QP], 2, sh),
                     w(tmp[:, 0]), w(tmp[:, 1]))

            v.wait_ge(S["b_in"], 32)
            v.wait_ge(S["v_free"], 9)
            for q in range(NQ):
                if q:
                    v.wait_ge(S["bp_used"], q)
                start_quarter(7, braw, fr, fi, q)
                raise_(6, 7, 1, 0, q)
                raise_(4, 6, 2, 1, q)
                raise_(0, 4, 4, 2, q)
                v.sem_inc(S["bp_ok"], 1)
                bank = v_bank()
                ins = v.tensor_copy(wp[:, q * 256:(q + 1) * 256], bank[:, 0:256])
                ins.then_inc(S["v_free"], 1)
                v.wait_ge(S["v_free"], vj[0])
                v.sem_inc(S["wp_ok"], 1)
                for c in range(2):
                    bank = v_bank()
                    src = bank[:].rearrange("p (q h j) -> p q h j", q=QP, h=2)
                    for h in range(2):
                        rows = slice(64 * h, 64 * h + 64)
                        ins = v.tensor_copy(st_j[rows, 1:NJ + 1, c, q * QP:(q + 1) * QP].rearrange("p j q -> p q j"),
                                            src[rows, :, h, :])
                    ins.then_inc(S["v_free"], 1)
            v.wait_ge(S["v_free"], vj[0])
            v.wait_ge(S["st0_ok"], 1)
            t1 = tmp[:, 0, 0:64]
            t2 = tmp[:, 0, 64:128]
            SC, UN = 5, 8
            with v.Fori(0, NJ // UN) as ju:
                for k in range(UN):
                    def at(o_, n):
                        return st[:, bass.ds(ju * (64 * UN) + (64 * k + o_), n)]

                    def scanned(n):
                        v.wait_ge(S["scan"], ju * (SC * UN) + (SC * k + n))

                    sn, n_re, n_im = at(64, 64), at(64, 32), at(96, 32)
                    v.tensor_tensor(t1, at(0, 64), a8[:, 0:64], ALU.mult).then_inc(S["scan"], 1)
                    v.tensor_tensor(t2, at(0, 64), a8[:, 64:128], ALU.mult).then_inc(S["scan"], 1)
                    scanned(2)
                    v.tensor_tensor(sn, sn, t1, ALU.add).then_inc(S["scan"], 1)
                    scanned(3)
                    v.tensor_tensor(n_re, n_re, t2[:, 32:64], ALU.add).then_inc(S["scan"], 1)
                    v.tensor_tensor(n_im, n_im, t2[:, 0:32], ALU.add).then_inc(S["scan"], 1)
                    scanned(5)
            v.wait_ge(S["s_used"], NQ)
            steps(v.memset(r45[:, 0:4096], 0.0))
            for h in range(2):
                rows = slice(64 * h, 64 * h + 64)
                for c in range(2):
                    ins = v.tensor_scalar(sbd[rows, c, h], st_j[rows, 0:NJ, c, :].rearrange("p j q -> p q j"),
                                          1.0 - 2.0 * c, None, ALU.mult)
            steps(ins)
            v.sem_inc(S["sbd_ok"], 1)
            v.wait_ge(S["up_ok"], 1)
            for part in range(2):
                v.wait_ge(S["blk_free"], 8 + 4 * part)
                for t in range(TT):
                    src = z_t[:, t, (part + 1) * W:(part + 2) * W].rearrange("p (h a d) -> p h a d", a=2, d=32)
                    cos = bc(ang[:, 32 + 32 * t:64 + 32 * t], 1, 2 * H)
                    sin = bc(ang[:, 224 + 32 * t:256 + 32 * t], 1, 2 * H)
                    v.tensor_tensor(rt[:, 0], src[:, :, 0], cos, ALU.mult)
                    v.tensor_tensor(rt[:, 1], src[:, :, 1], sin, ALU.mult)
                    v.tensor_tensor(rt[:, 2], src[:, :, 1], cos, ALU.mult)
                    steps(v.tensor_tensor(rt[:, 3], src[:, :, 0], sin, ALU.mult))
                    v.tensor_tensor(src[:, :, 0], rt[:, 0], rt[:, 1], ALU.subtract)
                    steps(v.tensor_tensor(src[:, :, 1], rt[:, 2], rt[:, 3], ALU.add))
            v.sem_inc(S["qk_rot"], 1)
            v.wait_ge(S["bp_used"], NQ)
            for q in range(NQ):
                if q:
                    v.wait_ge(S["ca_used"], q)
                start_quarter(0, ct, apw[:, 0, 0], apw[:, 0, 1], q)
                raise_(1, 0, 1, 0, q)
                raise_(2, 0, 2, 1, q)
                raise_(4, 0, 4, 2, q)
                v.sem_inc(S["ca_ok"], 1)
            v.wait_ge(S["ca_used"], NQ)
            v.wait_ge(S["mask_ok"], 1)
            exps = [0, 8, 16, 20, 24, 28, 32]
            amw = [33 + 2 * r for r in range(7)]
            for r in range(6):
                nh, K = (4, P) if r < 2 else (2, 2 * P)
                mk = mask[:, P:2 * P] if r < 2 else mask[:]
                if r:
                    v.wait_ge(S["ex_ok"], exps[r])
                for c in range(2):
                    bank = v_bank()
                    v.tensor_tensor(sm_[:, c].rearrange("p (h k) -> p h k", h=nh),
                                    bank[:].rearrange("p (h k) -> p h k", h=nh), bc(mk, 1, nh), ALU.add).then_inc(S["v_free"], 1)
                v.wait_ge(S["v_free"], vj[0])
                steps(v.tensor_reduce(sc8[:, 0:8].rearrange("p (c h) -> p c h", c=2)[:, :, 0:nh],
                                      sm_[:].rearrange("p c (h k) -> p c h k", h=nh), AX.X, ALU.max))
                nm = sc8[:, 8:16].rearrange("p (c h) -> p c h", c=2)[:, :, 0:nh]
                steps(v.tensor_scalar(nm, sc8[:, 0:8].rearrange("p (c h) -> p c h", c=2)[:, :, 0:nh], -SCALE, None, ALU.mult))
                v.sem_inc(S["nmx_ok"], 1)
                v.wait_ge(S["ex_ok"], exps[r + 1])
                sv = sc8[:, 16:24].rearrange("p (c h) -> p c h", c=2)[:, :, 0:nh]
                steps(v.reciprocal(sv, sv))
                steps(v.tensor_scalar(sv[:, 1], sv[:, 1], lamv[:, 5:6], None, ALU.mult))
                e4 = ex[:].rearrange("p c (h k) -> p c h k", h=nh)
                am3 = am.rearrange("p (h k) -> p h k", h=nh)
                if r:
                    v.wait_ge(S["a_free"], amw[r])
                v.tensor_tensor(am3, e4[:, 0], bc(sv[:, 0], 2, K), ALU.mult)
                steps(v.tensor_tensor(e4[:, 1], e4[:, 1], bc(sv[:, 1], 2, K), ALU.mult))
                steps(v.tensor_tensor(am3, am3, e4[:, 1], ALU.add))
                v.sem_inc(S["am_ok"], 1)
            v.wait_ge(S["a_free"], amw[6] + 1)
            oa4 = oa.rearrange("p t (h e) -> p t h e", h=H)
            steps(v.tensor_tensor(osq, oa, oa, ALU.mult))
            for t in range(TT):
                steps(v.tensor_reduce(sc8[:, 24 + 8 * t:32 + 8 * t], osq[:, t].rearrange("p (h e) -> p h e", h=H), AX.X, ALU.add))
            steps(v.tensor_scalar(sc8[:, 24:40], sc8[:, 24:40], 1.0 / P, SUBLN_EPS, ALU.mult, ALU.add))
            v.sem_inc(S["osq_ok"], 1)
            steps(v.tensor_scalar(subw[:], subw[:], 1.0 - LAMBDA_INIT, None, ALU.mult))
            v.wait_ge(S["ort_ok"], 1)
            steps(v.reciprocal(sc8[:, 40:56], sc8[:, 40:56]))
            for t in range(TT):
                steps(v.tensor_tensor(oa4[:, t], oa4[:, t], bc(sc8[:, 40 + 8 * t:48 + 8 * t], 2, P), ALU.mult))
                steps(v.tensor_tensor(oa4[:, t], oa4[:, t], bc(subw[:], 1, H), ALU.mult))
            v.sem_inc(S["oa_ok"], 1)
            g0 = r45[:, 0:2048].rearrange("p (t c) -> p t c", t=TT)
            g1 = r45[:, 2048:4096].rearrange("p (t c) -> p t c", t=TT)
            v.wait_ge(S["yp_in"], 16 * 8)
            v.wait_ge(S["d_in"], 16)
            steps(v.tensor_tensor(g0, z_t[:, :, 0:W], bc(d_b, 1, TT), ALU.mult))
            steps(v.tensor_tensor(yg, yg, g0, ALU.add))
            steps(v.tensor_tensor(g0, yg, yg, ALU.mult))
            steps(v.tensor_scalar(g0, g0, GELU_C, 1.0, ALU.mult, ALU.add))
            steps(v.tensor_tensor(g0, g0, yg, ALU.mult))
            v.sem_inc(S["gel_in"], 1)
            v.wait_ge(S["gel_sig"], 1)
            steps(v.tensor_tensor(yg, yg, g1, ALU.mult))
            v.sem_inc(S["gelu_ok"], 1)
            lo = [0, 0]

            def low(n):
                for _ in range(n):
                    hc = lo[0]
                    lo[0] += 1
                    v.wait_ge(S["hi_ok"], hc + 1)
                    v.tensor_tensor(ring_r[:, raw_half(hc)], ring[:, raw_half(hc)], r45_r[:, hi_slot(hc)].bitcast(F32),
                                    ALU.subtract).then_inc(S["lo_ok"], 1)

            def low_x(hi, lo2, n_banks):
                for n in range(n_banks):
                    m = LO_A0 + lo[1]
                    lo[1] += 1
                    v.wait_ge(S["a_free"], m + 1)
                    v.tensor_tensor(lo2[n], pb[6 + m % 2][:].rearrange("p (k t) -> p k t", k=2),
                                    hi[:, 2 * n:2 * n + 2].bitcast(F32), ALU.subtract).then_inc(S["alo_ok"], 1)

            low_x(oT_hi, oT_lo2, 4)
            low_x(yT_hi, yT_lo2, 4)
            low(4)
            v.wait_ge(S["gb_in"], 16)
            for n in range(2):
                if n == 1:
                    low(1)
                for t in range(TT):
                    v.wait_ge(S["blk_ready"], 33 + 2 * n + t)
                    v.tensor_tensor(g0[:, t, n * BLK:(n + 1) * BLK], pb[2 * n + t][:],
                                    glu_bb[:, n * BLK:(n + 1) * BLK], ALU.add).then_inc(S["out_free"], 1)
            v.wait_ge(S["out_free"], 4)
            v.sem_inc(S["glu_pre"], 1)
            v.wait_ge(S["glu_sig"], 1)
            steps(v.tensor_tensor(yg, yg, g0, ALU.mult))
            v.sem_inc(S["y2_ok"], 1)
            low_x(yT_hi, yT_lo2, 4)
            low(1)
            for n in range(4):
                low(2)
                for t in range(TT):
                    gs = gs_t[:, t, n * BLK:(n + 1) * BLK]
                    v.wait_ge(S["blk_ready"], 37 + 4 * n + t)
                    steps(v.tensor_tensor(gs, gs, pb[t][:], ALU.mult))
                    v.sem_inc(S["out_free"], 1)
                low(2)
                for t in range(TT):
                    gs = gs_t[:, t, n * BLK:(n + 1) * BLK]
                    ga = ga_t[:, t, n * BLK:(n + 1) * BLK]
                    v.wait_ge(S["blk_ready"], 39 + 4 * n + t)
                    steps(v.tensor_tensor(ga, ga, pb[2 + t][:], ALU.mult))
                    v.sem_inc(S["out_free"], 1)
                    steps(v.tensor_tensor(gs, gs, ga, ALU.add))
            v.sem_inc(S["mrg_ok"], 1)
            low_x(mT_hi, mT_lo2, 8)
            v.wait_ge(S["x_again"], 32)
            for n in range(4):
                low(4 if n < 3 else 2)
                for t in range(TT):
                    v.wait_ge(S["blk_ready"], 53 + 2 * n + t)
                    xs = x_t[:, t, n * BLK:(n + 1) * BLK]
                    steps(v.tensor_tensor(xs, xs, pb[2 * (n % 2) + t][:], ALU.add))
                    v.sem_inc(S["out_free"], 1)
            v.sem_inc(S["x2_ok"], 1)
            v.wait_ge(S["ss2_done"], 2)
            steps(v.tensor_scalar(ss[:, 2:4], ss[:, 0:2], 1.0 / D, NORM_EPS, ALU.mult, ALU.add))
            v.sem_inc(S["root2_done"], 1)
            v.wait_ge(S["ss2_done"], 3)
            steps(v.reciprocal(ss[:, 6:8], ss[:, 4:6]))
            for t in range(TT):
                steps(v.tensor_scalar(h2[:, t, :], x_t[:, t, :], ss[:, 6 + t:7 + t], None, ALU.mult))
            v.sem_inc(S["h2_ok"], 1)
            for n in range(8):
                bank = v_bank()
                v.tensor_tensor(hT[:, 2 * n:2 * n + 2], bank[:].rearrange("p (k t) -> p k t", k=2),
                                bc(w2c[:, 2 * n:2 * n + 2], 2, T), ALU.mult).then_inc(S["v_free"], 1)
            v.wait_ge(S["v_free"], vj[0])
            v.sem_inc(S["h2T_ok"], 1)
            v.wait_ge(S["iota_ok"], 1)
            steps(v.tensor_reduce(q32, ident[:].rearrange("p (g s) -> p s g", g=4), AX.X, ALU.add))
            v.wait_ge(S["lg_ps"], 1)
            steps(v.tensor_copy(lg, pb[0][:, 0:128].rearrange("p (t e) -> p t e", t=TT)[:, :, 0:NG + NE]))
            g8 = rs[:, 0:16].rearrange("p (t e) -> p t e", t=TT)
            steps(v.memset(rs[:, 0:16], -3.0e38))
            steps(v.tensor_copy(g8[:, :, 0:NG], lg[:, :, 0:NG]))
            m8 = rs[:, 16:32].rearrange("p (t e) -> p t e", t=TT)
            x8 = rs[:, 32:48].bitcast(U32).rearrange("p (t e) -> p t e", t=TT)
            gidx = rs[:, 80:82]
            oh = rs[:, 84:92].rearrange("p (t g) -> p t g", t=TT)
            es = rs[:, 96:112].rearrange("p (t e) -> p t e", t=TT)
            pr = rs[:, 112:176].rearrange("p (t g e) -> p t g e", t=TT, g=NG)
            v8 = rs[:, 176:192].rearrange("p (t e) -> p t e", t=TT)
            y8 = rs[:, 192:208].bitcast(U32).rearrange("p (t e) -> p t e", t=TT)
            eid = rs[:, 208:212].rearrange("p (t k) -> p t k", t=TT)
            mk = rs[:, 212:340].rearrange("p (t k e) -> p t k e", t=TT, k=2)
            mm = rs[:, 340:404].rearrange("p (t e) -> p t e", t=TT)
            rk = rs[:, 404:500].rearrange("p (t e) -> p t e", t=3)
            nb = rs[:, 500:532]
            be = rs[:, 532:564]
            cm = rs[:, 564:820].rearrange("p (e j) -> p e j", j=8)
            pk = rs[:, 820:948].rearrange("p (t k e) -> p t k e", t=TT, k=2)
            for t in range(TT):
                steps(v.max(m8[:, t], g8[:, t]))
                steps(v.max_index(x8[:, t], m8[:, t], g8[:, t]))
            steps(v.tensor_copy(gidx, x8[:, :, 0]))
            for t in range(TT):
                steps(v.tensor_scalar(rs[:, 48 + 4 * t:52 + 4 * t], lg[:, t, 0:NG], m8[:, t, 0:1], None, ALU.subtract))
                steps(v.tensor_scalar(oh[:, t], iota[:, 0, 0:NG], gidx[:, t:t + 1], None, ALU.is_equal))
                steps(v.tensor_tensor(pr[:, t], lg[:, t, NG:NG + NE].rearrange("p (g e) -> p g e", g=NG), bc(oh[:, t], 2, EPG), ALU.mult))
                steps(v.tensor_reduce(es[:, t], pr[:, t].rearrange("p g e -> p e g"), AX.X, ALU.add))
                steps(v.max(v8[:, t], es[:, t]))
                steps(v.max_index(y8[:, t], v8[:, t], es[:, t]))
                steps(v.tensor_copy(eid[:, t], y8[:, t, 0:2]))
                steps(v.scalar_tensor_tensor(eid[:, t], gidx[:, t:t + 1].to_broadcast([P, 2]),
                                             float(EPG), eid[:, t], ALU.mult, ALU.add))
            steps(v.tensor_tensor(rs[:, 56:58], v8[:, :, 1], v8[:, :, 0], ALU.subtract))
            v.sem_inc(S["gex_in"], 1)
            for t in range(TT):
                for k in range(2):
                    steps(v.tensor_scalar(mk[:, t, k], iota[:, 0], eid[:, t, k:k + 1], None, ALU.is_equal))
            steps(v.tensor_tensor(mm, mk[:, :, 0], mk[:, :, 1], ALU.add))
            v.sem_inc(S["m_ok"], 1)
            v.wait_ge(S["gex_ok"], 1)
            steps(v.tensor_reduce(rs[:, 76:78], rs[:, 64:72].rearrange("p (t g) -> p t g", t=TT), AX.X, ALU.add))
            steps(v.tensor_scalar(rs[:, 78:80], rs[:, 72:74], 1.0, None, ALU.add))
            steps(v.tensor_tensor(rs[:, 76:78], rs[:, 76:78], rs[:, 78:80], ALU.mult))
            steps(v.reciprocal(gw[:, :, 0], rs[:, 76:78]))
            steps(v.tensor_tensor(gw[:, :, 1], gw[:, :, 0], rs[:, 72:74], ALU.mult))
            v.wait_ge(S["cnt_ps"], 1)
            steps(v.tensor_copy(rs[:, 404:500], pb[1][:, 0:96]))
            steps(v.tensor_tensor(cm, bc(rk[:, 2], 2, 8), bc(thr, 1, NE), ALU.is_gt))
            steps(v.tensor_reduce(nb, cm, AX.X, ALU.add))
            steps(v.tensor_scalar(nb[:, 0:1], nb[:, 0:1], 1.0, None, ALU.max))
            steps(v.tensor_tensor_scan(be, ones[:, 0:NE], nb, 0.0, ALU.mult, ALU.add))
            steps(v.tensor_tensor(cmp48, bc(be[0:1], 1, MAXI), i48, ALU.is_le))
            steps(v.tensor_reduce(tabf[:, 1:1 + MAXI], cmp48, AX.X, ALU.add))
            steps(v.tensor_copy(tabf[:, 0:1], be[0:1, NE - 1:NE]))
            steps(v.tensor_scalar(tabf[:, 1:1 + MAXI], tabf[:, 1:1 + MAXI], NE - 1.0, None, ALU.min))
            steps(v.tensor_copy(tab, tabf))
            v.sem_inc(S["tab_ok"], 1)
            steps(v.tensor_tensor(nb, be, nb, ALU.subtract))
            for t in range(TT):
                steps(v.scalar_tensor_tensor(rk[:, t], nb, float(CAP), rk[:, t], ALU.mult, ALU.add))
                steps(v.tensor_tensor(pk[:, t], mk[:, t], bc(rk[:, t], 1, 2), ALU.mult))
            for t in range(TT):
                steps(v.tensor_reduce(rem[:, t], pk[:, t], AX.X, ALU.add))
            istep = S["istep"]

            def selection():
                for t in range(TT):
                    v.tensor_scalar(sel[:, t], iota[:, 0], rem[:, t, 0:1], None, ALU.is_equal)
                    last = v.tensor_scalar(sela[:, t], iota[:, 0], rem[:, t, 1:2], None, ALU.is_equal)
                return last

            selection().then_inc(istep, 1)
            v.wait_ge(istep, 1)
            v.tensor_tensor(sel, sel, sela, ALU.add).then_inc(S["sel_ok"], 1)

            def xT_out():
                v.tensor_tensor(xT, pb[1][:].rearrange("p (j n s) -> p j n s", j=4, n=4),
                                bc(w2c.rearrange("p (n j) -> p j n", j=4), 3, CAP), ALU.mult).then_inc(S["xt_sb"], 1)

            v.wait_ge(S["xt_ps"], 1)
            xT_out()
            n_items = v.value_load(tab[:, 0:1], min_val=1, max_val=MAXI)
            v.sem_inc(S["up_sb"], 1)
            v.sem_inc(S["sc_free"], 1)
            with v.Fori(0, n_items) as i:
                v.wait_ge(S["swt_ps"], i + 1)
                v.wait_ge(S["sc_free"], i * 8 + 1)
                for t in range(TT):
                    v.tensor_scalar(swr[:, t], iota, rem[:, t, 0:1], gw[:, t, 0:1], ALU.is_equal, ALU.mult)
                    last = v.tensor_scalar(swa[:, t], iota, rem[:, t, 1:2], gw[:, t, 1:2], ALU.is_equal, ALU.mult)
                last.then_inc(istep, 1)
                v.wait_ge(istep, i * 3 + 2)
                v.tensor_tensor(swr, swr, swa, ALU.add).then_inc(S["swr_ok"], 1)
                v.tensor_scalar(rem, rem, float(CAP), None, ALU.subtract).then_inc(istep, 1)
                v.wait_ge(istep, i * 3 + 3)
                v.wait_ge(S["xg_ps"], i + 1)
                selection().then_inc(istep, 1)
                v.wait_ge(istep, i * 3 + 4)
                v.tensor_tensor(sel, sel, sela, ALU.add).then_inc(S["sel_ok"], 1)
                v.wait_ge(S["up_ps"], i + 1)
                v.tensor_copy(gu[:, 1], pb[3][:]).then_inc(S["up_sb"], 1)
                v.wait_ge(S["swt_ps"], i + 2)
                v.tensor_copy(swt, pb[5][:, 0:T]).then_inc(S["swt_sb"], 1)
                v.wait_ge(S["xt_ps"], i + 2)
                xT_out()
                v.wait_ge(S["sig_ok"], i + 1)
                aTf = aTe.rearrange("p k s -> p (k s)")
                v.tensor_tensor(sge, sge, pb[4][:, 0:P], ALU.mult).then_inc(S["si_ok"], 1)
                v.wait_ge(S["si_ok"], i + 1)
                v.tensor_tensor(aTf, sge, pb[4][:, P:2 * P], ALU.mult).then_inc(S["at_ok"], 1)
                for n in range(4):
                    for t in range(TT):
                        m = 2 * n + t
                        v.wait_ge(S["sc_ps"], i * 8 + m + 2)
                        xs = x_t[:, t, n * BLK:(n + 1) * BLK]
                        v.tensor_tensor(xs, xs, pb[(7, 1)[m % 2]][:], ALU.add).then_inc(S["sc_free"], 1)
            v.wait_ge(S["sc_free"], n_items * 8 + 1)
            v.sem_inc(S["moe_ok"], 1)
            v.wait_ge(S["fss_done"], 2)
            steps(v.tensor_scalar(ss[:, 2:4], ss[:, 0:2], 1.0 / D, NORM_EPS, ALU.mult, ALU.add))
            v.sem_inc(S["froot_done"], 1)
            v.wait_ge(S["fss_done"], 3)
            steps(v.reciprocal(ss[:, 6:8], ss[:, 4:6]))
            v.wait_ge(S["fw_in"], 16)
            for t in range(TT):
                v.scalar_tensor_tensor(x_t[:, t, :], x_t[:, t, :], ss[:, 6 + t:7 + t], bcw[:],
                                       ALU.mult, ALU.mult).then_inc(S["out_ok"], 1)

        @block.tensor
        def _(pe):
            vj, aj = [0], [0]

            def v_bank():
                n = vj[0]
                vj[0] += 1
                if n >= 2:
                    pe.wait_ge(S["v_free"], n - 1)
                return pb[4 + n % 2]

            def a_bank():
                n = aj[0]
                aj[0] += 1
                if n >= 2:
                    pe.wait_ge(S["a_free"], n - 1)
                return pb[6 + n % 2]

            pe.wait_ge(S["ident_ok"], 1)
            pe.wait_ge(S["lam_in"], 16 * 8)
            pe.wait_ge(S["dt_spread"], 1)
            bank = v_bank()
            for n in range(3):
                ins = pe.transpose(bank[:, 32 * n:32 * n + 32], p32[:, n * P:(n + 1) * P], ident[0:32, 0:32])
            ins.then_inc(S["v_ready"], 1)
            pe.wait_ge(S["h_done"], 2)
            hs = h_t.rearrange("p t (d k) -> p t d k", k=KT)
            for n in range(8):
                bank = v_bank()
                for k in range(2):
                    for t in range(TT):
                        ins = pe.transpose(bank[:, (2 * k + t) * P:(2 * k + t + 1) * P], hs[:, t, :, 2 * n + k], ident[:])
                ins.then_inc(S["v_ready"], 1)
            pe.wait_ge(S["c_in"], 16 * 16)
            for c in range(2):
                bank = a_bank()
                for g in range(4):
                    ins = pe.transpose(bank[:, g * P:(g + 1) * P], cn[:, c, g, :], ident[:])
                ins.then_inc(S["a_ready"], 1)

            def w_in_chunk(k):
                b, c = k // 2, k % 2
                b0 = 2 * (b % 2)
                if c == 0 and b >= 2:
                    pe.wait_ge(S["blk_free"], 2 * (b - 1))
                for p in range(PPC * k, PPC * (k + 1)):
                    pe.wait_ge(S["wlo_ok"], p + 1)
                    w_hi = ring_r[:, hi_piece(p)].rearrange("p (k n) -> p k n", k=PK)
                    w_lo = ring_r[:, raw_piece(p)].rearrange("p (k n) -> p k n", k=PK)
                    for kk in range(PK):
                        kt = PK * (p % (2 * PPC)) + kk
                        for t in range(TT):
                            x_hi = ht_r[:, kt * T + t * P:kt * T + (t + 1) * P]
                            x_lo = hT_lo[kt][:, t * P:(t + 1) * P]
                            for j, (x_, w_) in enumerate(((x_hi, w_hi), (x_hi, w_lo), (x_lo, w_hi))):
                                ins = pe.matmul(pb[b0 + t][:], x_, w_[:, kk, :], start=(kt == 0 and j == 0),
                                                stop=(kt == KT - 1 and j == 2))
                            if kt == KT - 1:
                                ins.then_inc(S["blk_ready"], 1)
                    if kt < KT - 1:
                        ins.then_inc(S["piece_used"], 1)
                if c == 1:
                    pe.wait_ge(S["blk_ready"], 2 * b + 2)
                    pe.sem_inc(S["piece_used"], 1)

            def u_turn():
                pe.wait_ge(S["up_ok"], 1)
                for n in range(4):
                    bank = a_bank()
                    for g in range(4):
                        ins = pe.transpose(bank[:, g * P:(g + 1) * P], up[:, 4 * n + g].rearrange("p i m -> p (i m)"), ident[:])
                    ins.then_inc(S["a_ready"], 1)
                pe.wait_ge(S["a_ready"], aj[0])
                pe.sem_inc(S["ut_ok"], 1)
                pe.wait_ge(S["cbd_ok"], 1)

            def stage_a(q):
                pe.wait_ge(S["bp_ok"], q + 1)
                for n in range(4):
                    bank = a_bank()
                    for r in range(2):
                        for c in range(2):
                            ins = pe.transpose(bank[:, (2 * r + c) * P:(2 * r + c + 1) * P],
                                               bp[:, c, 2 * n + r].rearrange("p i m -> p (i m)"), ident[:])
                    ins.then_inc(S["a_ready"], 1)
                bank = v_bank()
                for r in range(QP):
                    nat = (r // 2) * 8 + 2 * q + r % 2
                    for c in range(2):
                        ins = pe.matmul(bank[:, r * 32:(r + 1) * 32], bp[:, c, r].rearrange("p i m -> p (i m)"),
                                        cbd[:, c, nat].rearrange("p h m -> p (h m)"), start=(c == 0), stop=(c == 1))
                ins.then_inc(S["v_ready"], 1)
                pe.wait_ge(S["v_ready"], vj[0])
                pe.sem_inc(S["bp_used"], 1)
                pe.wait_ge(S["a_free"], aj[0])
                for c in range(2):
                    bank = v_bank()
                    for r in range(QP):
                        g0_ = 4 * q + 2 * (r % 2)
                        ins = pe.matmul(bank[:, r * 64:(r + 1) * 64].rearrange("p (h j) -> p h j", h=2), bt[:, r, c, :],
                                        ut[:, g0_:g0_ + 2, r // 2, :], start=True, stop=True)
                    ins.then_inc(S["v_ready"], 1)
                pe.wait_ge(S["v_ready"], vj[0])
                pe.sem_inc(S["s_used"], 1)

            def stage_c(q):
                pe.wait_ge(S["sbd_ok"], 1)
                pe.wait_ge(S["tq_in"], 16 * L * (q + 1))
                pe.wait_ge(S["ca_ok"], q + 1)
                bank = a_bank()
                for gq in range(4):
                    r2, h = gq // 2, gq % 2
                    for part in range(3):
                        for f in range(4):
                            dst = bank[32 * f:32 * f + 32, gq * P:(gq + 1) * P]
                            r = 2 * f + r2
                            if part == 0:
                                rhs = tq[:, :, r * 32 + h * SM:r * 32 + h * SM + SM]
                                ins = pe.matmul(dst.rearrange("p (i m) -> p i m", i=L), ut[:, 4 * q + gq, f, :], rhs,
                                                start=True, stop=False)
                            else:
                                ins = pe.matmul(dst, sbd[:, part - 1, h, q * QP + r, :],
                                                bp[:, part - 1, r].rearrange("p i m -> p (i m)"),
                                                start=False, stop=(part == 2))
                ins.then_inc(S["a_ready"], 1)
                pe.wait_ge(S["a_ready"], aj[0])
                pe.sem_inc(S["ca_used"], 1)
                pe.sem_inc(S["tq_used"], 1)
                if q == NQ - 1:
                    pe.wait_ge(S["a_free"], aj[0])
                    pe.sem_inc(S["yp_ok"], 1)

            def qk_turn():
                pe.wait_ge(S["qk_rot"], 1)
                for n in range(8):
                    bank = a_bank()
                    for k in range(2):
                        for t in range(TT):
                            hh = 2 * n + k
                            ins = pe.transpose(bank[:, (2 * k + t) * P:(2 * k + t + 1) * P], qk[:, t, hh * P:(hh + 1) * P], ident[:])
                    ins.then_inc(S["a_ready"], 1)
                pe.wait_ge(S["a_free"], aj[0])

            def scores(r):
                nh, K = (4, P) if r < 2 else (2, 2 * P)
                t = 0 if r < 2 else 1
                h0 = 4 * r if r < 2 else 2 * (r - 2)
                for c in range(2):
                    bank = v_bank()
                    rows = slice(64 * c, 64 * c + 64)
                    for h in range(nh):
                        ins = pe.matmul(bank[:, h * K:(h + 1) * K], qkT[rows, h0 + h, t * P:(t + 1) * P],
                                        qkT[rows, H + h0 + h, 0:K], start=True, stop=True)
                    ins.then_inc(S["v_ready"], 1)

            def round_(r):
                nh, K = (4, P) if r < 2 else (2, 2 * P)
                h0 = 4 * r if r < 2 else 2 * (r - 2)
                if r < 5:
                    scores(r + 1)
                pe.wait_ge(S["am_ok"], r + 1)
                bank = a_bank()
                for n in range(4):
                    ins = pe.transpose(bank[:, n * P:(n + 1) * P], am[:, n * P:(n + 1) * P], ident[:])
                ins.then_inc(S["a_ready"], 1)
                pe.wait_ge(S["a_free"], aj[0])
                bank = a_bank()
                nk = K // P
                for h in range(nh):
                    for k in range(nk):
                        ins = pe.matmul(bank[:, h * P:(h + 1) * P], aT[:, (h * nk + k) * P:(h * nk + k + 1) * P],
                                        z_t[:, k, 3 * W + (h0 + h) * P:3 * W + (h0 + h + 1) * P],
                                        start=(k == 0), stop=(k == nk - 1))
                ins.then_inc(S["a_ready"], 1)

            lo = [0]

            def turn(src, nk):
                sv = src.rearrange("p t (c k) -> p t c k", k=nk)
                for n in range(nk // 2):
                    bank = a_bank()
                    if lo[0] >= 2:
                        pe.wait_ge(S["alo_ok"], lo[0] - 1)
                    lo[0] += 1
                    for k in range(2):
                        for t in range(TT):
                            ins = pe.transpose(bank[:, (2 * k + t) * P:(2 * k + t + 1) * P], sv[:, t, :, 2 * n + k], ident[:])
                    ins.then_inc(S["a_ready"], 1)

            def half_product(hc, hi, low_, kt0, b0, first, last):
                pe.wait_ge(S["lo_ok"], hc + 1)
                w_hi = r45_r[:, hi_slot(hc)].rearrange("p (k n) -> p k n", k=HK)
                w_lo = ring_r[:, raw_half(hc)].rearrange("p (k n) -> p k n", k=HK)
                for kk in range(HK):
                    for t in range(TT):
                        x_hi = hi[:, kt0 + kk, t * P:(t + 1) * P]
                        x_lo = low_[kt0 + kk][:, t * P:(t + 1) * P]
                        for j, (x_, w_) in enumerate(((x_hi, w_hi), (x_hi, w_lo), (x_lo, w_hi))):
                            ins = pe.matmul(pb[b0 + t][:], x_, w_[:, kk, :], start=(first and kk == 0 and j == 0),
                                            stop=(last and kk == HK - 1 and j == 2))
                        if last and kk == HK - 1:
                            ins.then_inc(S["blk_ready"], 1)
                if not last:
                    ins.then_inc(S["half_used"], 1)

            pe.wait_ge(S["hl_ok"], 8)
            for c in range(N_WIN):
                w_in_chunk(c)
                if c == PE_A[0]:
                    u_turn()
                if c in PE_A:
                    stage_a(PE_A.index(c))
                if c in PE_C:
                    stage_c(PE_C.index(c))
                if c == PE_QK:
                    qk_turn()
                    scores(0)
                if 0 <= c - PE_ROUND < 6:
                    round_(c - PE_ROUND)
            pe.wait_ge(S["oa_ok"], 1)
            turn(oa, WK)
            pe.wait_ge(S["a_ready"], aj[0])
            pe.sem_inc(S["xfree"], 1)
            pe.wait_ge(S["gelu_ok"], 1)
            turn(yg, WK)
            assert aj[0] == LO_A0 + 8
            pe.wait_ge(S["alo_ok"], lo[0])
            hc = 0
            for n in range(2):
                pe.wait_ge(S["blk_free"], 30 + 2 * n)
                for c in range(2):
                    half_product(hc, yT_hi, yT_lo, c * HK, 2 * n, c == 0, c == 1)
                    hc += 1
                pe.wait_ge(S["blk_ready"], 32 + 2 * n + 2)
                pe.sem_inc(S["half_used"], 1)
                pe.sem_inc(S["chunk_used"], 1)
            pe.wait_ge(S["y2_ok"], 1)
            turn(yg, WK)
            pe.wait_ge(S["alo_ok"], lo[0])
            br = 36
            for n in range(4):
                for hi, low_, b0 in ((yT_hi, yT_lo, 0), (oT_hi, oT_lo, 2)):
                    pe.wait_ge(S["out_free"], 4 if n == 0 else 4 + 4 * (n - 1) + b0 + 2)
                    for c in range(2):
                        half_product(hc, hi, low_, c * HK, b0, c == 0, c == 1)
                        hc += 1
                    br += 2
                    pe.wait_ge(S["blk_ready"], br)
                    pe.sem_inc(S["half_used"], 1)
                    pe.sem_inc(S["chunk_used"], 1)
            pe.wait_ge(S["mrg_ok"], 1)
            turn(gs_t, KT)
            pe.wait_ge(S["a_ready"], aj[0])
            pe.sem_inc(S["mT_ps"], 1)
            pe.wait_ge(S["alo_ok"], lo[0])
            for n in range(4):
                b0 = 2 * (n % 2)
                pe.wait_ge(S["out_free"], 20 if n < 2 else 20 + 2 * (n - 1))
                for c in range(4):
                    half_product(hc, mT_hi, mT_lo, c * HK, b0, c == 0, c == 3)
                    hc += 1
                    if c == 1:
                        pe.wait_ge(S["half_used"], hc)
                        pe.sem_inc(S["chunk_used"], 1)
                pe.wait_ge(S["blk_ready"], 52 + 2 * n + 2)
                pe.sem_inc(S["half_used"], 1)
                pe.sem_inc(S["chunk_used"], 1)
            pe.wait_ge(S["h2_ok"], 1)
            for n in range(8):
                bank = v_bank()
                for kk in range(2):
                    for t in range(TT):
                        ins = pe.transpose(bank[:, (2 * kk + t) * P:(2 * kk + t + 1) * P], hs[:, t, :, 2 * n + kk], ident[:])
                ins.then_inc(S["v_ready"], 1)
            pe.wait_ge(S["h2T_ok"], 1)
            pe.wait_ge(S["rw_in"], 32)
            for t in range(TT):
                for kk in range(KT):
                    ins = pe.matmul(pb[0][:, 64 * t:64 * t + NG + NE], hT[:, kk, t * P:(t + 1) * P], rwv[:, kk, :],
                                    start=(kk == 0), stop=(kk == KT - 1))
            ins.then_inc(S["lg_ps"], 1)
            pe.wait_ge(S["m_ok"], 1)
            mmr = rs[:, 340:404].rearrange("p (t e) -> p t e", t=TT)
            pe.matmul(pb[1][:, 0:32], lt, mmr[:, 0], start=True, stop=True)
            pe.matmul(pb[1][:, 32:64], ones, mmr[:, 0], start=True, stop=False)
            pe.matmul(pb[1][:, 32:64], lt, mmr[:, 1], start=False, stop=True)
            pe.matmul(pb[1][:, 64:96], ones, mmr[:, 0], start=True, stop=False)
            pe.matmul(pb[1][:, 64:96], ones, mmr[:, 1], start=False, stop=True).then_inc(S["cnt_ps"], 1)

            h2k = h2.rearrange("p t (d k) -> p t k d", k=KT)

            def gather():
                for t in range(TT):
                    for n in range(4):
                        ins = pe.matmul(pb[0][32 * n:32 * n + 32, :].rearrange("p (j d) -> p j d", j=4), sel[:, t],
                                        h2k[:, t, 4 * n:4 * n + 4, :], start=(t == 0), stop=(t == TT - 1))
                ins.then_inc(S["xg_ps"], 1)

            def gather_turn():
                for j in range(4):
                    ins = pe.transpose(pb[1][:, j * P:(j + 1) * P], xg[:, j * P:(j + 1) * P], ident[:])
                ins.then_inc(S["xt_ps"], 1)

            pe.wait_ge(S["sel_ok"], 1)
            gather()
            pe.wait_ge(S["xg_sb"], 1)
            gather_turn()
            n_items = pe.value_load(tab[:, 0:1], min_val=1, max_val=MAXI)
            pe.sem_inc(S["swt_ps"], 1)
            pe.sem_inc(S["sc_ps"], 1)
            with pe.Fori(0, n_items) as i:
                pe.wait_ge(S["xt_sb"], i + 1)
                for part in range(2):
                    pe.wait_ge(S[("gate_sb", "up_sb")[part]], i + 1)
                    for c in range(2):
                        s_ = EXP_SLOT[2 * part + c]
                        pe.wait_ge(full[s_], i * 16 + 16 * (FILLS[s_] + 1))
                        wv = chunk3(s_)
                        for kk in range(CH):
                            kt = c * CH + kk
                            g_ = kt % 4
                            ins = pe.matmul(pb[2 + part][32 * g_:32 * g_ + 32, :], xT[:, kt % 4, kt // 4, :], wv[:, kk, :],
                                            start=(kt < 4), stop=(kt >= KT - 4))
                        ins.then_inc(S["item_chunk"], 1)
                    pe.wait_ge(S["item_chunk"], i * 6 + 2 * part + 2)
                    pe.sem_inc(S[("gate_ps", "up_ps")[part]], 1)
                pe.wait_ge(S["sel_ok"], i + 2)
                gather()
                pe.wait_ge(S["gate_sb"], i + 2)
                pe.wait_ge(S["up_sb"], i + 2)
                for part in range(2):
                    gv = gu[:, part].rearrange("p (f k) -> p f k", k=FK)
                    for k in range(FK):
                        ins = pe.matmul(pb[4][:, part * P + k * CAP:part * P + (k + 1) * CAP], gv[:, :, k], q32,
                                        start=True, stop=True)
                ins.then_inc(S["sum_ps"], 1)
                pe.wait_ge(S["swr_ok"], i + 1)
                for t in range(TT):
                    ins = pe.transpose(pb[5][:, t * P:(t + 1) * P], swr[:, t].rearrange("p a s -> p (a s)"), ident[:])
                ins.then_inc(S["swt_ps"], 1)
                pe.wait_ge(S["xg_sb"], i + 2)
                pe.wait_ge(S["sc_free"], i * 8 + 1)
                gather_turn()
                for c in (4, 5):
                    s_ = EXP_SLOT[c]
                    pe.wait_ge(full[s_], i * 16 + 16 * (FILLS[s_] + 1))
                pe.wait_ge(S["at_ok"], i + 1)
                for n in range(4):
                    if n >= 2:
                        pe.wait_ge(S["dn_sb"], i * 4 + n - 1)
                    for k in range(FK):
                        wv = slot(EXP_SLOT[4 + k // 2]).rearrange("p (k n) -> p k n", k=2)
                        ins = pe.matmul(pb[5 + n % 2][32 * k:32 * k + 32, :], aTe[:, k, :], wv[:, k % 2, n * BLK:(n + 1) * BLK],
                                        start=True, stop=True)
                    ins.then_inc(S["dn_ps"], 1)
                pe.wait_ge(S["dn_ps"], i * 4 + 4)
                pe.sem_inc(S["item_chunk"], 2)
                pe.wait_ge(S["swt_sb"], i + 1)
                pe.wait_ge(S["xt_sb"], i + 2)
                for n in range(4):
                    pe.wait_ge(S["dn_sb"], i * 4 + n + 1)
                    for t in range(TT):
                        m = 2 * n + t
                        if m >= 2:
                            pe.wait_ge(S["sc_free"], i * 8 + m)
                        pe.matmul(pb[(7, 1)[m % 2]][:], swt[:, t * P:(t + 1) * P], ys[:, n], start=True, stop=True).then_inc(S["sc_ps"], 1)


def kernel(**inputs):
    import numpy as np
    import concourse.bacc as bacc
    from concourse.bass_utils import run_bass_kernel_spmd

    nc = bacc.Bacc("TRN2", target_bir_lowering=False, num_devices=1)
    arrays, aps = {}, {}
    given = {k: np.ascontiguousarray(x) for k, x in inputs.items()}
    given["inv_freq"] = (1.0 / (np.float32(10000.0) ** (np.arange(0, HD, 2, dtype=np.float32) / np.float32(HD)))).astype(np.float32)
    for name, x in given.items():
        arrays[f"in_{name}"] = x
        aps[name] = nc.dram_tensor(f"in_{name}", x.shape, mybir.dt.from_np(x.dtype), kind="ExternalInput").ap()
    out = nc.dram_tensor("out_0", (1, T, D), F32, kind="ExternalOutput").ap()
    hybrid_block(nc, aps, out)
    r = run_bass_kernel_spmd(nc, [arrays], core_ids=[0])
    return r.results[0]["out_0"]
```

```python
from contextlib import ExitStack

import concourse.bass as bass
from concourse import mybir

F32 = mybir.dt.float32
F32R = mybir.dt.float32r
I32 = mybir.dt.int32
U32 = mybir.dt.uint32
ALU = mybir.AluOpType
ACT = mybir.ActivationFunctionType
AX = mybir.AxisListType

P = 128
D = 2048
T = 256
TT = T // P
KT = D // P
W = 1024
WK = W // P
BLK = 512
CH = 8
CHF = CH * BLK
HK = CH // 2
HF = HK * BLK
SLOTS = 6
DENSE_SLOTS = 3
PK = 2
PF = PK * BLK
RAW, HIS = 6, 4
G, SP_, SM = 64, 64, 16
PR = G // 2
L = 8
NJ = T // L
NQ = 4
QP = PR // NQ
H, HD = 8, 64
NG, EPG, NE = 4, 8, 32
F = 512
FK = F // P
CAP = 32
MAXI = 48
NORM_EPS, SUBLN_EPS = 1e-6, 1e-5
LAMBDA_INIT = 0.2
SCALE = HD ** -0.5
NEG = -1.0e30
ROUND = 12582912.0
INV_2PI = 0.15915494309189535
C1 = 6.28125
C2 = 0.0019350051879882812
C3 = 3.0199157663412e-07
PI = 3.1415925
GELU_C = 0.044715
GELU_S = 1.5957691216057308


def bc(ap, axis, n):
    a = ap.unsqueeze(axis)
    s = list(a.shape)
    s[axis] = n
    return a.to_broadcast(s)


class Steps:

    def __init__(self, eng, sem):
        self.eng, self.sem, self.n = eng, sem, 0

    def __call__(self, ins):
        ins.then_inc(self.sem, 1)
        self.n += 1
        self.eng.wait_ge(self.sem, self.n)


def hybrid_block(nc, a, out, upto=99, dbg=None):
    ctx = ExitStack()
    with ctx:
        place = {}

        def sb(name, shape, dt=F32):
            t = ctx.enter_context(nc.sbuf_tensor(name, shape, dt))
            place[name] = nc.sbuf_base - 4 * shape[1]
            return t

        def short(name, size):
            return nc.alloc_sbuf_tensor_at(name + "_r", [P, size], F32R, offset=place[name])

        def sem(name):
            return ctx.enter_context(nc.semaphore(name))

        ring = sb("ring", [P, DENSE_SLOTS * CHF])
        s3 = sb("s3", [P, CHF])
        r45 = sb("r45", [P, 2 * CHF])
        xa = sb("xa", [P, TT * D])
        ht = sb("ht", [P, KT * T])
        z = sb("z", [P, TT * 4096])
        st = sb("st", [P, (NJ + 1) * 2 * PR])
        ypk = sb("ypk", [P, 2048])
        sml = sb("sml", [P, 2048])
        par = sb("par", [P, 1056])
        bcw = sb("bcw", [P, 2048])
        rw = sb("rw", [P, KT * (NG + NE)])
        wp = sb("wp", [P, G * SM])
        ident = sb("ident", [P, P])
        mask = sb("mask", [P, 2 * P])
        ang = sb("ang", [P, 4 * 96])
        ring_r = short("ring", DENSE_SLOTS * CHF)
        r45_r = short("r45", 2 * CHF)
        ht_r, z_r = short("ht", KT * T), short("z", TT * 4096)
        bcw_r = short("bcw", 2048)
        ypk_r, sml_r = short("ypk", 2048), short("sml", 2048)
        pb = [ctx.enter_context(nc.psum_tensor(f"pb{i}", [P, BLK], F32)) for i in range(8)]

        def slot(c):
            t, c = (ring, c) if c < DENSE_SLOTS else (s3, 0) if c == 3 else (r45, c - 4)
            return t[:, c * CHF:(c + 1) * CHF]

        x_t = xa[:].rearrange("p (t d) -> p t d", t=TT)
        h_t = z[:, 0:TT * D].rearrange("p (t d) -> p t d", t=TT)
        hT = ht[:].rearrange("p (k t) -> p k t", k=KT)
        z_t = z[:].rearrange("p (t c) -> p t c", t=TT)
        bp = xa[:, 0:2048].rearrange("p (c q i m) -> p c q i m", c=2, q=QP, i=L)
        tq = xa[:, 2048:4096].rearrange("p (i x) -> p i x", i=L)
        up = xa[:, 2048:4096].rearrange("p (g i m) -> p g i m", g=16, i=L)
        bt = r45[:, 0:2048].rearrange("p (q c x) -> p q c x", q=QP, c=2)
        cbd = r45[:, 2048:4096].rearrange("p (c q h m) -> p c q h m", c=2, q=PR, h=2)
        sbd = r45[:, 0:4096].rearrange("p (c h q j) -> p c h q j", c=2, h=2, q=PR)
        ut = r45[:, 4096:6144].rearrange("p (g f j) -> p g f j", g=16, f=4)
        tmp = r45[:, 6144:8192].rearrange("p (a x) -> p a x", a=2)
        braw = sml[:, 0:1024].rearrange("p (c g q m) -> p c g q m", c=2, g=4, q=8)
        ct = sml[:, 1024:2048].rearrange("p (c g q m) -> p c g q m", c=2, g=4, q=8)
        cn = ypk[:, 0:1024].rearrange("p (c g x) -> p c g x", c=2, g=4)
        yp = ypk[:].rearrange("p (i x) -> p i x", i=L)
        st_j = st[:].rearrange("p (j c q) -> p j c q", c=2, q=PR)
        yg = st[:, 0:2048].rearrange("p (t c) -> p t c", t=TT)
        yT = ypk[:].rearrange("p (k t) -> p k t", k=WK)
        oT = sml[:].rearrange("p (k t) -> p k t", k=WK)
        o = [0]

        def pv(n):
            o[0] += n
            return par[:, o[0] - n:o[0]]

        lam3 = pv(96)
        lr, li, ldt = lam3[:, 0:32], lam3[:, 32:64], lam3[:, 64:96]
        dt_, mag, nr, den, fr, fi, pt = pv(32), pv(32), pv(32), pv(32), pv(32), pv(32), pv(64)
        apw = pv(4 * 64).rearrange("p (k c q) -> p k c q", k=4, c=2)
        a8 = pv(128)
        w1c, w2c = pv(16), pv(16)
        ss = pv(8)
        lamv = pv(8)
        assert o[0] <= 1056
        p32 = ypk[0:32, 1408:1792]
        dt32 = ypk[0:32, 1792:1794]
        invf = sb("invf", [P, 32])
        posi = sb("posi", [P, TT], I32)
        posf = sb("posf", [P, TT])
        lamw = ypk[:, 1024:1344]
        subw = sb("subw", [P, P])
        qk = z_t[:, :, W:3 * W]
        qkT = r45[:, 0:4096].rearrange("p (h t) -> p h t", h=2 * H)
        rt = ypk[:].rearrange("p (a h d) -> p a h d", a=4, h=2 * H)
        sm_ = r45[:, 4096:5120].rearrange("p (c x) -> p c x", c=2)
        ex = r45[:, 5120:6144].rearrange("p (c x) -> p c x", c=2)
        am = r45[:, 6144:6656]
        aT = r45[:, 6656:7168]
        sc8 = r45[:, 7168:7232]
        g0 = r45[:, 0:2048].rearrange("p (t c) -> p t c", t=TT)
        oa = xa[:, 0:2048].rearrange("p (t c) -> p t c", t=TT)
        osq = xa[:, 2048:4096].rearrange("p (t c) -> p t c", t=TT)
        gs_t = s3[:].rearrange("p (t c) -> p t c", t=TT)
        ga_t = z_t[:, :, W:3 * W]

        HTL = DENSE_SLOTS * CHF - 2048

        def raw_piece(p):
            r = p % RAW
            o_ = (r if r < 4 else r + HIS) * PF
            return slice(o_, o_ + PF)

        def hi_piece(p):
            o_ = (4 + p % HIS) * PF
            return slice(o_, o_ + PF)

        def low_h(n):
            if n < 4:
                return bcw_r[:, n * BLK:(n + 1) * BLK], bcw[:, n * BLK:(n + 1) * BLK]
            o_ = HTL + (n - 4) * BLK
            return ring_r[:, o_:o_ + BLK], ring[:, o_:o_ + BLK]

        hT_lo = [low_h(kt // 2)[0][:, (kt % 2) * T:(kt % 2 + 1) * T] for kt in range(KT)]
        d_b = sml[:, 0:W]
        glu_bb = wp[:, 0:W]

        yT_hi = ypk_r[:].rearrange("p (k t) -> p k t", k=WK)
        oT_hi = sml_r[:].rearrange("p (k t) -> p k t", k=WK)
        mT_hi = ht_r[:].rearrange("p (k t) -> p k t", k=KT)

        def pieces(base, rows):
            v = [z_r[:, 4096 * i + base:4096 * i + base + rows * T].rearrange("p (k t) -> p k t", k=rows) for i in range(2)]
            return [v[k // rows][:, k % rows] for k in range(2 * rows)], [v[n // (rows // 2)][:, 2 * (n % (rows // 2)):2 * (n % (rows // 2)) + 2]
                                                                         for n in range(rows)]

        yT_lo, yT_lo2 = pieces(0, 4)
        oT_lo, oT_lo2 = pieces(3 * W, 4)
        mT_l = z_r[:, 4096:8192].rearrange("p (k t) -> p k t", k=KT)
        mT_lo, mT_lo2 = [mT_l[:, k] for k in range(KT)], [mT_l[:, 2 * n:2 * n + 2] for n in range(8)]

        def hi_slot(hc):
            i = 2 + hc % 2 if hc < 6 else (hc + 2) % 4
            return slice(i * HF, (i + 1) * HF)

        def raw_half(hc):
            k = hc // 2
            o_ = (k % DENSE_SLOTS) * CHF + (hc % 2) * HF
            return slice(o_, o_ + HF)

        h2 = h_t
        h2T = [(sml, ypk)[n // 2][:, (n % 2) * W:(n % 2 + 1) * W].rearrange("p (k t) -> p k t", k=4) for n in range(4)]
        sq8 = st[:, 1600:1608].rearrange("p (t n) -> p t n", t=TT)
        gu = z[:, 4096:5120].rearrange("p (c f) -> p c f", c=2)
        ys = z[:, 5120:7168].rearrange("p (n d) -> p n d", n=4)
        xg = z[:, 7168:7680]
        aTe = z[:, 7680:7808].rearrange("p (k s) -> p k s", k=FK)
        sge = z[:, 7808:7936]
        lg = z[:, 7936:8000].rearrange("p (t e) -> p t e", t=TT)
        lt = wp[:, 0:P]
        ones = wp[:, P:2 * P]
        iota = wp[:, 2 * P:3 * P].rearrange("p (a s) -> p a s", a=4)
        q32 = wp[:, 3 * P:3 * P + 32]
        thr = wp[:, 3 * P + 32:3 * P + 40]
        pidx = wp[:, 3 * P + 40:3 * P + 42]
        rs = st[:, 0:1600]
        xT = ht[:, 0:512].rearrange("p (j n s) -> p j n s", j=4, n=4)
        sel = ht[:, 512:576].rearrange("p (t s) -> p t s", t=TT)
        swr = ht[:, 576:832].rearrange("p (t a s) -> p t a s", t=TT, a=4)
        swt = ht[:, 832:1088]
        swa = ht[:, 1088:1344].rearrange("p (t a s) -> p t a s", t=TT, a=4)
        sela = ht[:, 1344:1408].rearrange("p (t s) -> p t s", t=TT)
        rem = ang[:, 0:4].rearrange("p (t k) -> p t k", t=TT)
        gw = ang[:, 4:8].rearrange("p (t k) -> p t k", t=TT)
        tab4 = ang[0:1, 96:96 + 4 * MAXI].bitcast(I32)
        tab_e, tab_l, tab_new, tab_n = (tab4[:, MAXI * j:MAXI * (j + 1)] for j in range(4))
        rwv = rw[:].rearrange("p (k e) -> p k e", k=KT)

        S = {n: sem(n) for n in (
            "x_in norms_in lam_in dt_in b_in c_in consts_in rw_in ident_ok mask_ok st0_ok "
            "ss_done root_done rstd_ok dve act pool pe_params "
            "v_ready v_free a_ready a_free chunk_used blk_ready blk_free out_free dt_spread "
            "dt_done mag_done arg_done sin_done lamx_in_done apow_done bp_ok bp_used bt_ok ct_ok cbd_ok "
            "uqkv_done up_ok uj_in ut_ok wp_ok s_used tq_zero tq_in tq_used ca_ok ca_used sbd_ok yp_ok yp_in "
            "gel_in gel_sig gelu_ok qk_rot qkT_ok nmx_ok ex_ok am_ok aT_ok aT_used o_ok osq_ok ort_ok oa_ok gates_ok "
            "glu_pre glu_sig y2_ok yT_ok oT_ok y2T_ok mrg_ok mT_ok x_again scan cbd_zero sbd_zero "
            "lsum_ok lexp_ok mT_ps xfree ss2_done root2_done lg_ps gex_in gex_ok pex_ok m_ok cnt_ps tab_ok iota_ok acc_ok tabc_ok tab_ps fw_in "
            "sel_ok xg_ps xg_sb xt_ps xt_sb gate_ps gate_sb up_ps up_sb sum_ps sig_ok swr_ok swt_ps swt_sb at_ok dn_ps dn_sb "
            "piece_used whi_ok wlo_ok hx_ok hl_ok d_in gb_in hi_ok lo_ok half_used alo_ok si_ok istep sc_ps sc_free item_chunk moe_ok fss_done froot_done out_ok out_in").split()}
        full = [sem(f"slot{i}_full") for i in range(SLOTS)]
        first_full = [sem(f"first_half{i}_full") for i in range(2)]
        w_full = [sem(f"piece{i}_full") for i in range(RAW)]

        block = ctx.enter_context(nc.Block())

        PE_A = (5, 6, 7, 8)
        PE_C = (15, 16, 17, 18)
        PE_QK = 19
        PE_ROUND = 20
        LO_A0 = 2 + 4 + 4 * NQ + NQ + 8 + 2 * 6

        def blocks_of(wap, kt_total):
            return wap.rearrange("(p k) n -> p k n", k=kt_total)

        win = blocks_of(a["w_in"][0], KT)
        glu = blocks_of(a["ssm_glu_w"][0], WK)
        wps = blocks_of(a["w_proj_ssm"][0], WK)
        wpa = blocks_of(a["w_proj_attn"][0], WK)
        wout = blocks_of(a["w_out"][0], KT)
        x_d = a["x"][0].rearrange("(t p) d -> p t d", p=P)
        out_d = out[0].rearrange("(t p) d -> p t d", p=P)

        def chunk3(c):
            return slot(c).rearrange("p (k n) -> p k n", k=CH)

        dense = []
        for n in range(2):
            dense.append(glu[:, :, n * BLK:(n + 1) * BLK])
        for n in range(4):
            dense.append(wpa[:, :, n * BLK:(n + 1) * BLK])
            dense.append(wps[:, :, n * BLK:(n + 1) * BLK])
        for n in range(4):
            for c in range(2):
                dense.append(wout[:, c * CH:(c + 1) * CH, n * BLK:(n + 1) * BLK])
        N_WIN = 32
        N_PIECE = N_WIN * CH // PK
        PPC = CH // PK
        N_DENSE = len(dense)
        N_HALF = 2 * len(dense)
        EXP_SLOT = (3, 0, 1, 5, 4, 2)
        FILLS = [len(range(s, N_DENSE, DENSE_SLOTS)) - (s == 0) for s in range(DENSE_SLOTS)] + [0, 0, 0]

        @block.sync
        def _(sp):
            for t in range(TT):
                sp.dma_start(x_t[:, t, :], x_d[:, t, :]).then_inc(S["x_in"], 16)

            for p in range(N_PIECE):
                if p >= RAW:
                    sp.wait_ge(S["piece_used"], p - RAW + 1)
                b, c = p // (2 * PPC), p % (2 * PPC)
                sp.dma_start(ring[:, raw_piece(p)].rearrange("p (k n) -> p k n", k=PK),
                             win[:, c * PK:(c + 1) * PK, b * BLK:(b + 1) * BLK]).then_inc(w_full[p % RAW], 16)
                if p == RAW - 1:
                    for n, name in enumerate(("ssm_lambda_re", "ssm_lambda_im")):
                        src = a[name][0].rearrange("(g q r h) p -> q g r (h p)", g=4, q=NQ, h=2)
                        for q in range(NQ):
                            sp.dma_start(p32[q * 8:(q + 1) * 8, n * P:(n + 1) * P], src[q]).then_inc(S["lam_in"], 16)
                    src = a["ssm_log_dt"][0].rearrange("(g q r h) -> q g r h", g=4, q=NQ, h=2)
                    for q in range(NQ):
                        sp.dma_start(dt32[q * 8:(q + 1) * 8, :], src[q]).then_inc(S["dt_in"], 16)
                    sp.dma_start(invf[:], a["inv_freq"].partition_broadcast(P)).then_inc(S["consts_in"], 16)
                    with nc.allow_non_contiguous_dma(reason="256 positions, one per partition"):
                        sp.dma_start(posi[:], a["positions"][0].rearrange("(t p) -> p t", p=P)).then_inc(S["consts_in"], 16)
                    for n, name in enumerate(("q1", "k1", "q2", "k2")):
                        sp.dma_start(lamw[:, n * 64:(n + 1) * 64],
                                     a[f"attn_lambda_{name}"][0].partition_broadcast(P)).then_inc(S["consts_in"], 16)
                    sp.dma_start(subw[:], a["attn_subln_w"][0].partition_broadcast(P)).then_inc(S["consts_in"], 16)
                if p == RAW + 3:
                    for n, name in enumerate(("ssm_b_re", "ssm_b_im")):
                        sp.dma_start(braw[:, n].rearrange("p g q m -> p (g q) m"),
                                     a[name][0].rearrange("(q h) p m -> (h p) q m", h=2)).then_inc(S["b_in"], 16)
                if p == RAW + 9:
                    for n in range(4):
                        for name, dst in (("group", rwv[:, 4 * n:4 * n + 4, 0:NG]), ("expert", rwv[:, 4 * n:4 * n + 4, NG:NG + NE])):
                            sp.dma_start(dst, a[f"router_{name}_w"][0, n * BLK:(n + 1) * BLK].rearrange("(p j) e -> p j e", j=4)
                                         ).then_inc(S["rw_in"], 16)
                if p == 4 * PPC + RAW + 1:
                    sp.wait_ge(S["blk_free"], 4)
                    sp.wait_ge(S["a_free"], 2)
                    sp.wait_ge(S["lsum_ok"], 1)
                    for f in range(4):
                        for t in range(TT):
                            sp.dma_start(yp[32 * f + 16 * t:32 * f + 16 * t + 16],
                                         z_t[:, t, f * 256:(f + 1) * 256]).then_inc(S["uj_in"], 16)
                for q in range(NQ):
                    if p == ((PE_A[3] + 1) if q == 0 else (PE_C[q - 1] + 1)) * PPC + RAW:
                        if q == 0:
                            sp.wait_ge(S["tq_zero"], 1)
                            sp.wait_ge(S["wp_ok"], NQ)
                            sp.wait_ge(S["bp_ok"], NQ)
                            sp.dma_start(d_b, a["ssm_d"][0].partition_broadcast(P)).then_inc(S["d_in"], 16)
                        else:
                            sp.wait_ge(S["tq_used"], q)
                        for i in range(L):
                            sp.dma_start(tq[0:SM * (i + 1), i, :],
                                         wp[SM * (L - 1 - i):P, q * 256:(q + 1) * 256]).then_inc(S["tq_in"], 16)
                if p == (PE_C[3] + 1) * PPC + RAW:
                    sp.wait_ge(S["yp_ok"], 1)
                    for f in range(4):
                        for t in range(TT):
                            sp.dma_start(yg[:, t, f * 256:(f + 1) * 256],
                                         yp[32 * f + 16 * t:32 * f + 16 * t + 16]).then_inc(S["yp_in"], 16)
                    sp.wait_ge(S["tq_in"], 16 * L * NQ)
                    sp.dma_start(glu_bb, a["ssm_glu_b"][0].partition_broadcast(P)).then_inc(S["gb_in"], 16)

            sp.wait_ge(S["piece_used"], N_PIECE)
            for k in range(N_DENSE):
                if k >= DENSE_SLOTS:
                    sp.wait_ge(S["chunk_used"], k - DENSE_SLOTS + 1)
                if k == 0:
                    for c in range(2):
                        sp.dma_start(chunk3(0)[:, c * HK:(c + 1) * HK], dense[0][:, c * HK:(c + 1) * HK]).then_inc(first_full[c], 16)
                else:
                    sp.dma_start(chunk3(k % DENSE_SLOTS), dense[k]).then_inc(full[k % DENSE_SLOTS], 16)
                if k == 10:
                    sp.wait_ge(S["xfree"], 1)
                    for t in range(TT):
                        sp.dma_start(x_t[:, t, :], x_d[:, t, :]).then_inc(S["x_again"], 16)

            def expert_chunks(e):
                for name in ("expert_w_gate", "expert_w_up"):
                    w = a[name][0, e].rearrange("e (n p j) f -> p (e n) (j f)", n=4, j=4)
                    for c in range(2):
                        yield w[:, 2 * c:2 * c + 2, :], "k"
                w = a["expert_w_down"][0, e].rearrange("e (p k) n -> p (e k) n", k=FK)
                for c in range(2):
                    yield w[:, 2 * c:2 * c + 2, :], "d"

            def fill(c, src, kind):
                s_ = EXP_SLOT[c]
                dst = slot(s_).rearrange("p (k n) -> p k n", k=2)
                sp.dma_start(dst, src).then_inc(full[s_], 16)

            for c, (src, kind) in enumerate(expert_chunks(bass.ds(0, 1))):
                if c == 0:
                    sp.wait_ge(S["mT_ps"], 1)
                elif c == 3:
                    sp.wait_ge(S["half_used"], N_HALF - 2)
                elif c == 4:
                    sp.wait_ge(S["half_used"], N_HALF)
                else:
                    sp.wait_ge(S["chunk_used"], N_DENSE - (3 - c if c < 3 else 0))
                fill(c, src, kind)
            sp.wait_ge(S["tab_ok"], 1)
            n_items = sp.value_load(tab_n[:, 0:1], min_val=1, max_val=MAXI)
            with sp.If(n_items > 1):
                with sp.Fori(1, n_items) as i:
                    new = sp.value_load(tab_new[:, bass.ds(i, 1)], min_val=0, max_val=1)
                    with sp.If(new > 0):
                        e = sp.value_load(tab_e[:, bass.ds(i, 1)], min_val=0, max_val=NE - 1)
                        for c, (src, kind) in enumerate(expert_chunks(bass.ds(e, 1))):
                            sp.wait_ge(S["item_chunk"], i * 6 + c - 5)
                            fill(c, src, kind)
            for t in range(TT):
                sp.wait_ge(S["out_ok"], t + 1)
                sp.dma_start(out_d[:, t, :], x_t[:, t, :]).then_inc(S["out_in"], 16)
            sp.wait_ge(S["out_in"], 16 * TT)

        @block.scalar
        def _(act):
            steps = Steps(act, S["act"])
            act.dma_start(w1c, a["norm1_w"][0].rearrange("(p k) -> p k", k=KT)).then_inc(S["norms_in"], 16)
            act.dma_start(w2c.rearrange("p (n j) -> p n j", n=4), a["norm2_w"][0].rearrange("(n p j) -> p n j", n=4, j=4)).then_inc(S["norms_in"], 16)
            act.wait_ge(S["x_in"], 32)
            for t in range(TT):
                act.activation(h_t[:, t, :], x_t[:, t, :], ACT.Square, accum_out=ss[:, t:t + 1]).then_inc(S["ss_done"], 1)

            def high_w(p):
                if p >= N_PIECE:
                    return
                act.wait_ge(w_full[p % RAW], 16 * (p // RAW + 1))
                if p >= HIS:
                    act.wait_ge(S["piece_used"], p - HIS + 1)
                act.activation(ring_r[:, hi_piece(p)], ring[:, raw_piece(p)], ACT.Copy).then_inc(S["whi_ok"], 1)

            for n in range(8):
                act.wait_ge(S["v_free"], n + 1)
                act.activation(ht_r[:, n * BLK:(n + 1) * BLK], low_h(n)[1], ACT.Copy).then_inc(S["hx_ok"], 1)
                if n < HIS:
                    high_w(n)
            act.wait_ge(S["root_done"], 1)
            act.activation(ss[:, 4:6], ss[:, 2:4], ACT.Sqrt).then_inc(S["ss_done"], 1)
            aj = [0]

            def a_job(out_, cols, func=ACT.Copy):
                n = aj[0]
                aj[0] += 1
                act.wait_ge(S["a_ready"], n + 1)
                act.activation(out_, pb[6 + n % 2][:, 0:cols] if len(out_.shape) == 2 else out_x(out_, n, cols),
                               func).then_inc(S["a_free"], 1)

            def out_x(out_, n, cols):
                v = pb[6 + n % 2][:, 0:cols]
                if len(out_.shape) == 3:
                    return v.rearrange("p (a b) -> p a b", a=out_.shape[1])
                return v.rearrange("p (a b c) -> p a b c", a=out_.shape[1], b=out_.shape[2])

            def parameters():
                act.wait_ge(S["pe_params"], 1)
                act.activation(dt_, ldt, ACT.Exp).then_inc(S["dt_done"], 1)
                act.wait_ge(S["arg_done"], 1)
                act.activation(mag, nr, ACT.Exp).then_inc(S["mag_done"], 1)
                act.wait_ge(S["lsum_ok"], 1)
                act.activation(lamv[:, 2:4], lamv[:, 0:2], ACT.Exp).then_inc(S["lexp_ok"], 1)
                act.wait_ge(S["arg_done"], 2)
                act.activation(ang[:, 192:288], ang[:, 96:192], ACT.Sin).then_inc(S["sin_done"], 1)
                act.activation(ang[:, 288:384], ang[:, 96:192], ACT.Sin, scale=0.5).then_inc(S["sin_done"], 1)
                for c in range(2):
                    a_job(ct[:, c].rearrange("p g q m -> p (g q m)"), BLK)

            def block_out(b):
                if b == 0:
                    act.wait_ge(S["rstd_ok"], 1)
                for t in range(TT):
                    act.wait_ge(S["blk_ready"], 2 * b + t + 1)
                    if b < 8:
                        dst = z_t[:, t, b * BLK:(b + 1) * BLK]
                    elif b < 12:
                        dst = gs_t[:, t, (b - 8) * BLK:(b - 7) * BLK]
                    else:
                        dst = ga_t[:, t, (b - 12) * BLK:(b - 11) * BLK]
                    act.activation(dst, pb[2 * (b % 2) + t][:], ACT.Copy if b < 8 else ACT.Sigmoid,
                                   scale=ss[:, 6 + t:7 + t]).then_inc(S["blk_free"], 1)

            def u_out():
                for n in range(4):
                    a_job(ut[:, 4 * n:4 * n + 4].rearrange("p g f j -> p (g f j)"), BLK)

            def stage_a(q):
                for h in range(4):
                    if q and h == 0:
                        act.wait_ge(S["s_used"], q)
                    a_job(bt[:, 2 * h:2 * h + 2].rearrange("p q c x -> p (q c x)"), BLK)

            def stage_c(q):
                if q == 0:
                    act.wait_ge(S["qk_rot"], 1)
                n = aj[0]
                act.wait_ge(S["a_ready"], n + 1)
                aj[0] += 1
                act.activation(yp.rearrange("p i (g m) -> p g i m", g=16)[:, 4 * q:4 * q + 4],
                               pb[6 + n % 2][:].rearrange("p (g i m) -> p g i m", g=4, i=L),
                               ACT.Copy).then_inc(S["a_free"], 1)

            def exps(r):
                nh, K = (4, P) if r < 2 else (2, 2 * P)
                act.wait_ge(S["nmx_ok"], r + 1)
                if r:
                    act.wait_ge(S["am_ok"], r)
                for c in range(2):
                    for h in range(nh):
                        act.activation(ex[:, c, h * K:(h + 1) * K], sm_[:, c, h * K:(h + 1) * K], ACT.Exp,
                                       bias=sc8[:, 8 + c * 4 + h:9 + c * 4 + h], scale=SCALE,
                                       accum_out=sc8[:, 16 + c * 4 + h:17 + c * 4 + h]).then_inc(S["ex_ok"], 1)

            def high(hc):
                k = hc // 2
                if k == 0:
                    act.wait_ge(first_full[hc], 16)
                else:
                    act.wait_ge(full[k % DENSE_SLOTS], 16 * (k // DENSE_SLOTS + (k % DENSE_SLOTS > 0)))
                if 2 <= hc < 6:
                    act.wait_ge(S["half_used"], hc - 1)
                elif 6 <= hc < 8:
                    act.wait_ge(S["y2_ok"], 1)
                elif hc >= 8:
                    act.wait_ge(S["half_used"], hc - 3)
                act.activation(r45_r[:, hi_slot(hc)], ring[:, raw_half(hc)], ACT.Copy).then_inc(S["hi_ok"], 1)

            def round_out(r):
                nh = 4 if r < 2 else 2
                a_job(aT, BLK)
                t = 0 if r < 2 else 1
                h0 = 4 * r if r < 2 else 2 * (r - 2)
                a_job(oa[:, t, h0 * P:(h0 + nh) * P], nh * P)

            for c in range(N_WIN):
                r = c - PE_ROUND
                high_w(PPC * (c + 1))
                if 0 <= r < 6:
                    exps(r)
                for p in range(1, PPC):
                    high_w(PPC * (c + 1) + p)
                if c % 2:
                    block_out(c // 2)
                if c == 0:
                    parameters()
                if c == PE_A[0]:
                    u_out()
                if c in PE_A:
                    stage_a(PE_A.index(c))
                if c in PE_C:
                    stage_c(PE_C.index(c))
                if c == PE_QK:
                    for n in range(8):
                        a_job(qkT[:, 2 * n:2 * n + 2].rearrange("p h t -> p (h t)"), BLK)
                if 0 <= r < 6:
                    round_out(r)
                if c == PE_ROUND + 6:
                    act.wait_ge(S["osq_ok"], 1)
                    act.activation(sc8[:, 40:56], sc8[:, 24:40], ACT.Sqrt).then_inc(S["ort_ok"], 1)
                if c == N_WIN - 2:
                    act.wait_ge(S["gel_in"], 1)
                    act.activation(r45[:, 2048:4096], r45[:, 0:2048], ACT.Sigmoid, scale=GELU_S).then_inc(S["gel_sig"], 1)
            for n in range(4):
                a_job(oT_hi[:, 2 * n:2 * n + 2].rearrange("p k t -> p (k t)"), BLK)
            for n in range(4):
                if n == 0:
                    act.wait_ge(S["yp_in"], 16 * 8)
                a_job(yT_hi[:, 2 * n:2 * n + 2].rearrange("p k t -> p (k t)"), BLK)
            for hc in range(5):
                high(hc)
            for n in range(2):
                if n == 1:
                    high(5)
                act.wait_ge(S["glu_pre"], n + 1)
                act.activation(g0[:, :, n * BLK:(n + 1) * BLK], g0[:, :, n * BLK:(n + 1) * BLK], ACT.Sigmoid).then_inc(S["glu_sig"], 1)
            for hc in (6, 7, 8):
                high(hc)
            for n in range(4):
                a_job(yT_hi[:, 2 * n:2 * n + 2].rearrange("p k t -> p (k t)"), BLK)
            for hc in range(9, 24):
                high(hc)
            for n in range(8):
                a_job(mT_hi[:, 2 * n:2 * n + 2].rearrange("p k t -> p (k t)"), BLK)
            for hc in range(24, N_HALF):
                high(hc)
            for n in range(4):
                for t in range(TT):
                    act.wait_ge(S["out_free"], 21 + 2 * n + t)
                    m = 2 * n + t
                    if m >= 4:
                        act.wait_ge(S["ss2_done"], m - 3)
                    act.activation(bcw[:, m % 4 * BLK:(m % 4 + 1) * BLK], h2[:, t, n * BLK:(n + 1) * BLK], ACT.Square,
                                   accum_out=sq8[:, t, n:n + 1]).then_inc(S["ss2_done"], 1)
            act.wait_ge(S["root2_done"], 1)
            act.activation(ss[:, 4:6], ss[:, 2:4], ACT.Sqrt).then_inc(S["ss2_done"], 1)
            act.wait_ge(S["gex_in"], 1)
            act.activation(rs[:, 64:74], rs[:, 48:58], ACT.Exp).then_inc(S["gex_ok"], 1)
            act.wait_ge(S["xg_ps"], 1)
            act.activation(xg, pb[0][:], ACT.Copy).then_inc(S["xg_sb"], 1)
            act.wait_ge(S["tab_ok"], 1)
            n_items = act.value_load(tab_n[:, 0:1], min_val=1, max_val=MAXI)
            act.sem_inc(S["gate_sb"], 1)
            with act.Fori(0, n_items) as i:
                act.wait_ge(S["gate_ps"], i + 1)
                act.activation(gu[:, 0], pb[2][:], ACT.Copy).then_inc(S["gate_sb"], 1)
                act.wait_ge(S["xt_ps"], i + 1)
                act.wait_ge(S["xg_ps"], i + 2)
                act.activation(xg, pb[0][:], ACT.Copy).then_inc(S["xg_sb"], 1)
                act.wait_ge(S["sum_ps"], i + 1)
                act.activation(sge, pb[4][:, 0:P], ACT.Sigmoid).then_inc(S["sig_ok"], 1)
                act.wait_ge(S["sc_ps"], i * 8 + 1)
                for n in range(4):
                    act.wait_ge(S["dn_ps"], i * 4 + n + 1)
                    act.activation(ys[:, n], pb[5 + n % 2][:], ACT.Copy).then_inc(S["dn_sb"], 1)
            act.wait_ge(S["moe_ok"], 1)
            for t in range(TT):
                act.activation(h2[:, t, :], x_t[:, t, :], ACT.Square, accum_out=ss[:, t:t + 1]).then_inc(S["fss_done"], 1)
            act.wait_ge(S["froot_done"], 1)
            act.activation(ss[:, 4:6], ss[:, 2:4], ACT.Sqrt).then_inc(S["fss_done"], 1)

        @block.gpsimd
        def _(pool):
            steps = Steps(pool, S["pool"])
            steps(pool.memset(ident[:], 0.0))
            pool.affine_select(out=ident[:], in_=ident[:], compare_op=ALU.not_equal, fill=1.0, base=0,
                               pattern=[[-1, P]], channel_multiplier=1).then_inc(S["ident_ok"], 1)
            for n, name in enumerate(("ssm_c_re", "ssm_c_im")):
                for g in range(4):
                    s_ = a[name][0, 16 * g:16 * g + 16].rearrange("(q h) m p -> h q m p", h=2)
                    for h in range(2):
                        pool.dma_start(cn[:, n, g, h * 64:(h + 1) * 64], s_[h]).then_inc(S["c_in"], 16)
            steps(pool.memset(mask[:], 0.0))
            pool.affine_select(out=mask[:, P:2 * P], in_=mask[:, P:2 * P], compare_op=ALU.is_ge, fill=NEG, base=0,
                               pattern=[[-1, P]], channel_multiplier=1).then_inc(S["mask_ok"], 1)
            pool.memset(r45[:, 2048:4096], 0.0).then_inc(S["cbd_zero"], 1)
            pool.memset(st_j[:, 0], 0.0).then_inc(S["st0_ok"], 1)

            def low_w(p):
                pool.wait_ge(S["whi_ok"], p + 1)
                pool.tensor_tensor(ring_r[:, raw_piece(p)], ring[:, raw_piece(p)], ring_r[:, hi_piece(p)].bitcast(F32),
                                   ALU.subtract).then_inc(S["wlo_ok"], 1)

            for p in range(N_PIECE):
                low_w(p)
                if p == PPC * (PE_A[0] + 1) - 1:
                    pool.wait_ge(S["uj_in"], 16 * 8)
                    pool.wait_ge(S["v_free"], 8)
                    pool.wait_ge(S["ss_done"], 2)
                    pool.tensor_copy(up, yp.rearrange("p i (g m) -> p g i m", g=16)).then_inc(S["up_ok"], 1)
                if p == PPC * (PE_A[0] + 2) - 1:
                    pool.wait_ge(S["ut_ok"], 1)
                    pool.memset(xa[:, 2048:4096], 0.0).then_inc(S["tq_zero"], 1)
            pool.wait_ge(S["y2_ok"], 1)
            steps(pool.memset(wp[:, 0:2 * P], 1.0))
            pool.affine_select(out=lt, in_=lt, compare_op=ALU.is_gt, fill=0.0, base=0,
                               pattern=[[1, P]], channel_multiplier=-1)
            pool.iota(iota, pattern=[[0, 4], [1, CAP]], base=0, channel_multiplier=0, allow_small_or_imprecise_dtypes=True)
            pool.iota(thr, pattern=[[CAP, 8]], base=0, channel_multiplier=0, allow_small_or_imprecise_dtypes=True)
            steps(pool.iota(pidx, pattern=[[-1, 2]], base=0, channel_multiplier=1, allow_small_or_imprecise_dtypes=True))
            pool.sem_inc(S["iota_ok"], 1)
            for n in range(4):
                for t in range(TT):
                    pool.wait_ge(S["out_free"], 21 + 2 * n + t)
                    pool.tensor_copy(x_t[:, t, n * BLK:(n + 1) * BLK], h2[:, t, n * BLK:(n + 1) * BLK]).then_inc(S["acc_ok"], 1)
            pool.wait_ge(S["tab_ok"], 1)
            pool.dma_start(bcw[:], a["final_norm_w"].partition_broadcast(P)).then_inc(S["fw_in"], 16)
            pool.wait_ge(S["fw_in"], 16)

        @block.vector
        def _(v):
            steps = Steps(v, S["dve"])
            vj = [0]

            def v_bank():
                n = vj[0]
                vj[0] += 1
                v.wait_ge(S["v_ready"], n + 1)
                return pb[4 + n % 2]

            v.wait_ge(S["norms_in"], 32)

            def low_hT(n):
                lo_, f = low_h(n)
                v.wait_ge(S["hx_ok"], n + 1)
                v.tensor_tensor(lo_, f, ht_r[:, n * BLK:(n + 1) * BLK].bitcast(F32), ALU.subtract).then_inc(S["hl_ok"], 1)

            for n in range(8):
                bank = v_bank()
                v.tensor_tensor(low_h(n)[1].rearrange("p (k t) -> p k t", k=2), bank[:].rearrange("p (k t) -> p k t", k=2),
                                bc(w1c[:, 2 * n:2 * n + 2], 2, T), ALU.mult).then_inc(S["v_free"], 1)
                if n:
                    low_hT(n - 1)
            low_hT(7)
            v.wait_ge(S["ss_done"], 2)
            v.tensor_scalar(ss[:, 2:4], ss[:, 0:2], 1.0 / D, NORM_EPS, ALU.mult, ALU.add).then_inc(S["root_done"], 1)
            v.wait_ge(S["dt_in"], 64)
            v.tensor_copy(p32[:, 2 * P:3 * P].rearrange("p (h s) -> p h s", h=2), bc(dt32, 2, 64)).then_inc(S["dt_spread"], 1)
            v.wait_ge(S["ss_done"], 3)
            v.reciprocal(ss[:, 6:8], ss[:, 4:6]).then_inc(S["rstd_ok"], 1)
            bank = v_bank()
            v.tensor_copy(lam3, bank[:, 0:96]).then_inc(S["v_free"], 1)
            v.wait_ge(S["v_free"], 9)
            v.sem_inc(S["pe_params"], 1)
            v.wait_ge(S["dt_done"], 1)
            steps(v.tensor_tensor(nr, lr, dt_, ALU.mult))
            v.sem_inc(S["arg_done"], 1)
            v.tensor_tensor(ang[:, 0:32], li, dt_, ALU.mult)
            v.wait_ge(S["consts_in"], 16 * 7)
            steps(v.tensor_copy(posf[:], posi[:]))
            for t in range(TT):
                steps(v.tensor_scalar(ang[:, 32 + 32 * t:64 + 32 * t], invf[:], posf[:, t:t + 1], None, ALU.mult))
            for n in range(2):
                steps(v.tensor_tensor(lamw[:, 256:320], lamw[:, n * 128:n * 128 + 64], lamw[:, n * 128 + 64:n * 128 + 128], ALU.mult))
                steps(v.tensor_reduce(lamv[:, n:n + 1], lamw[:, 256:320], AX.X, ALU.add))
            v.sem_inc(S["lsum_ok"], 1)
            kf, r_ = ang[:, 192:288], ang[:, 96:192]
            steps(v.tensor_scalar(kf, ang[:, 0:96], INV_2PI, ROUND, ALU.mult, ALU.add))
            steps(v.tensor_scalar(kf, kf, ROUND, None, ALU.subtract))
            steps(v.scalar_tensor_tensor(r_, kf, -C1, ang[:, 0:96], ALU.mult, ALU.add))
            steps(v.scalar_tensor_tensor(r_, kf, -C2, r_, ALU.mult, ALU.add))
            steps(v.scalar_tensor_tensor(r_, kf, -C3, r_, ALU.mult, ALU.add))
            steps(v.tensor_scalar(r_, r_, PI, -PI, ALU.min, ALU.max))
            v.sem_inc(S["arg_done"], 1)
            v.wait_ge(S["lexp_ok"], 1)
            steps(v.tensor_tensor(lamv[:, 4:5], lamv[:, 3:4], lamv[:, 2:3], ALU.subtract))
            steps(v.tensor_scalar(lamv[:, 5:6], lamv[:, 4:5], LAMBDA_INIT, None, ALU.subtract))
            v.wait_ge(S["sin_done"], 2)
            steps(v.tensor_tensor(ang[:, 0:96], ang[:, 288:384], ang[:, 288:384], ALU.mult))
            steps(v.tensor_scalar(ang[:, 0:96], ang[:, 0:96], -2.0, 1.0, ALU.mult, ALU.add))
            v.wait_ge(S["mag_done"], 1)
            A1 = apw[:, 0]
            v.tensor_tensor(A1[:, 0], mag, ang[:, 0:32], ALU.mult)
            steps(v.tensor_tensor(A1[:, 1], mag, ang[:, 192:224], ALU.mult))
            v.tensor_scalar(nr, A1[:, 0], 1.0, None, ALU.subtract)
            v.tensor_tensor(pt[:, 0:32], lr, lr, ALU.mult)
            steps(v.tensor_tensor(pt[:, 32:64], li, li, ALU.mult))
            steps(v.tensor_tensor(den, pt[:, 0:32], pt[:, 32:64], ALU.add))
            steps(v.reciprocal(den, den))
            v.tensor_tensor(pt[:, 0:32], nr, lr, ALU.mult)
            steps(v.tensor_tensor(pt[:, 32:64], A1[:, 1], li, ALU.mult))
            steps(v.tensor_tensor(fr, pt[:, 0:32], pt[:, 32:64], ALU.add))
            v.tensor_tensor(fr, fr, den, ALU.mult)
            v.tensor_tensor(pt[:, 0:32], A1[:, 1], lr, ALU.mult)
            steps(v.tensor_tensor(pt[:, 32:64], nr, li, ALU.mult))
            steps(v.tensor_tensor(fi, pt[:, 0:32], pt[:, 32:64], ALU.subtract))
            steps(v.tensor_tensor(fi, fi, den, ALU.mult))
            for k in range(3):
                Ak, An = apw[:, k], apw[:, k + 1]
                v.tensor_tensor(pt[:, 0:32], Ak[:, 0], Ak[:, 0], ALU.mult)
                v.tensor_tensor(pt[:, 32:64], Ak[:, 1], Ak[:, 1], ALU.mult)
                steps(v.tensor_tensor(An[:, 1], Ak[:, 0], Ak[:, 1], ALU.mult))
                v.tensor_tensor(An[:, 0], pt[:, 0:32], pt[:, 32:64], ALU.subtract)
                steps(v.tensor_scalar(An[:, 1], An[:, 1], 2.0, None, ALU.mult))
            v.tensor_copy(a8[:, 0:64].rearrange("p (c q) -> p c q", c=2), bc(apw[:, 3, 0], 1, 2))
            v.tensor_copy(a8[:, 64:96], apw[:, 3, 1])
            steps(v.tensor_scalar(a8[:, 96:128], apw[:, 3, 1], -1.0, None, ALU.mult))
            v.wait_ge(S["a_free"], 2)
            v.wait_ge(S["cbd_zero"], 1)
            for h in range(2):
                rows = slice(64 * h, 64 * h + 64)
                for c in range(2):
                    ins = v.tensor_scalar(cbd[rows, c, :, h, :], ct[rows, c].rearrange("p g q m -> p (g q) m"),
                                          1.0 - 2.0 * c, None, ALU.mult)
            steps(ins)
            v.sem_inc(S["cbd_ok"], 1)

            def quarter(t, q):
                return t[:, :, 2 * q:2 * q + 2, :]

            def cmul(o_re, o_im, i_re, i_im, m_re, m_im, t1, t2):
                v.tensor_tensor(t1, i_re, m_re, ALU.mult)
                steps(v.tensor_tensor(t2, i_im, m_im, ALU.mult))
                steps(v.tensor_tensor(o_re, t1, t2, ALU.subtract))
                v.tensor_tensor(t1, i_re, m_im, ALU.mult)
                steps(v.tensor_tensor(t2, i_im, m_re, ALU.mult))
                steps(v.tensor_tensor(o_im, t1, t2, ALU.add))

            def start_quarter(i, raw, m_re, m_im, q):
                def v4(x):
                    return x.rearrange("p (g r m) -> p g r m", g=4, r=2)

                def par_(x):
                    return bc(x[:, q * QP:(q + 1) * QP].rearrange("p (g r) -> p g r", g=4), 3, SM)

                t1, t2 = tmp[:, 0, 0:128], tmp[:, 1, 0:128]
                r_re, r_im = quarter(raw[:, 0], q), quarter(raw[:, 1], q)
                v.tensor_tensor(v4(t1), r_re, par_(m_re), ALU.mult)
                steps(v.tensor_tensor(v4(t2), r_im, par_(m_im), ALU.mult))
                t3 = t1.rearrange("p (q m) -> p q m", q=QP)
                t4 = t2.rearrange("p (q m) -> p q m", q=QP)
                steps(v.tensor_tensor(bp[:, 0, :, i, :], t3, t4, ALU.subtract))
                v.tensor_tensor(v4(t1), r_re, par_(m_im), ALU.mult)
                steps(v.tensor_tensor(v4(t2), r_im, par_(m_re), ALU.mult))
                steps(v.tensor_tensor(bp[:, 1, :, i, :], t3, t4, ALU.add))

            def raise_(dst, src, n, k, q):
                def x(t):
                    return t.rearrange("p q i m -> p q (i m)")
                sh = n * SM
                def w(t):
                    return t[:, 0:QP * sh].rearrange("p (q x) -> p q x", q=QP)
                cmul(x(bp[:, 0, :, dst:dst + n]), x(bp[:, 1, :, dst:dst + n]),
                     x(bp[:, 0, :, src:src + n]), x(bp[:, 1, :, src:src + n]),
                     bc(apw[:, k, 0, q * QP:(q + 1) * QP], 2, sh), bc(apw[:, k, 1, q * QP:(q + 1) * QP], 2, sh),
                     w(tmp[:, 0]), w(tmp[:, 1]))

            v.wait_ge(S["b_in"], 32)
            v.wait_ge(S["v_free"], 9)
            for q in range(NQ):
                if q:
                    v.wait_ge(S["bp_used"], q)
                start_quarter(7, braw, fr, fi, q)
                raise_(6, 7, 1, 0, q)
                raise_(4, 6, 2, 1, q)
                raise_(0, 4, 4, 2, q)
                v.sem_inc(S["bp_ok"], 1)
                bank = v_bank()
                ins = v.tensor_copy(wp[:, q * 256:(q + 1) * 256], bank[:, 0:256])
                ins.then_inc(S["v_free"], 1)
                v.wait_ge(S["v_free"], vj[0])
                v.sem_inc(S["wp_ok"], 1)
                for c in range(2):
                    bank = v_bank()
                    src = bank[:].rearrange("p (q h j) -> p q h j", q=QP, h=2)
                    for h in range(2):
                        rows = slice(64 * h, 64 * h + 64)
                        ins = v.tensor_copy(st_j[rows, 1:NJ + 1, c, q * QP:(q + 1) * QP].rearrange("p j q -> p q j"),
                                            src[rows, :, h, :])
                    ins.then_inc(S["v_free"], 1)
            v.wait_ge(S["v_free"], vj[0])
            v.wait_ge(S["st0_ok"], 1)
            t1 = tmp[:, 0, 0:64]
            t2 = tmp[:, 0, 64:128]
            SC, UN = 5, 8
            with v.Fori(0, NJ // UN) as ju:
                for k in range(UN):
                    def at(o_, n):
                        return st[:, bass.ds(ju * (64 * UN) + (64 * k + o_), n)]

                    def scanned(n):
                        v.wait_ge(S["scan"], ju * (SC * UN) + (SC * k + n))

                    sn, n_re, n_im = at(64, 64), at(64, 32), at(96, 32)
                    v.tensor_tensor(t1, at(0, 64), a8[:, 0:64], ALU.mult).then_inc(S["scan"], 1)
                    v.tensor_tensor(t2, at(0, 64), a8[:, 64:128], ALU.mult).then_inc(S["scan"], 1)
                    scanned(2)
                    v.tensor_tensor(sn, sn, t1, ALU.add).then_inc(S["scan"], 1)
                    scanned(3)
                    v.tensor_tensor(n_re, n_re, t2[:, 32:64], ALU.add).then_inc(S["scan"], 1)
                    v.tensor_tensor(n_im, n_im, t2[:, 0:32], ALU.add).then_inc(S["scan"], 1)
                    scanned(5)
            v.wait_ge(S["s_used"], NQ)
            steps(v.memset(r45[:, 0:4096], 0.0))
            for h in range(2):
                rows = slice(64 * h, 64 * h + 64)
                for c in range(2):
                    ins = v.tensor_scalar(sbd[rows, c, h], st_j[rows, 0:NJ, c, :].rearrange("p j q -> p q j"),
                                          1.0 - 2.0 * c, None, ALU.mult)
            steps(ins)
            v.sem_inc(S["sbd_ok"], 1)
            v.wait_ge(S["up_ok"], 1)
            for part in range(2):
                v.wait_ge(S["blk_free"], 8 + 4 * part)
                for t in range(TT):
                    src = z_t[:, t, (part + 1) * W:(part + 2) * W].rearrange("p (h a d) -> p h a d", a=2, d=32)
                    cos = bc(ang[:, 32 + 32 * t:64 + 32 * t], 1, 2 * H)
                    sin = bc(ang[:, 224 + 32 * t:256 + 32 * t], 1, 2 * H)
                    v.tensor_tensor(rt[:, 0], src[:, :, 0], cos, ALU.mult)
                    v.tensor_tensor(rt[:, 1], src[:, :, 1], sin, ALU.mult)
                    v.tensor_tensor(rt[:, 2], src[:, :, 1], cos, ALU.mult)
                    steps(v.tensor_tensor(rt[:, 3], src[:, :, 0], sin, ALU.mult))
                    v.tensor_tensor(src[:, :, 0], rt[:, 0], rt[:, 1], ALU.subtract)
                    steps(v.tensor_tensor(src[:, :, 1], rt[:, 2], rt[:, 3], ALU.add))
            v.sem_inc(S["qk_rot"], 1)
            v.wait_ge(S["bp_used"], NQ)
            for q in range(NQ):
                if q:
                    v.wait_ge(S["ca_used"], q)
                start_quarter(0, ct, apw[:, 0, 0], apw[:, 0, 1], q)
                raise_(1, 0, 1, 0, q)
                raise_(2, 0, 2, 1, q)
                raise_(4, 0, 4, 2, q)
                v.sem_inc(S["ca_ok"], 1)
            v.wait_ge(S["ca_used"], NQ)
            v.wait_ge(S["mask_ok"], 1)
            exps = [0, 8, 16, 20, 24, 28, 32]
            amw = [33 + 2 * r for r in range(7)]
            for r in range(6):
                nh, K = (4, P) if r < 2 else (2, 2 * P)
                mk = mask[:, P:2 * P] if r < 2 else mask[:]
                if r:
                    v.wait_ge(S["ex_ok"], exps[r])
                for c in range(2):
                    bank = v_bank()
                    v.tensor_tensor(sm_[:, c].rearrange("p (h k) -> p h k", h=nh),
                                    bank[:].rearrange("p (h k) -> p h k", h=nh), bc(mk, 1, nh), ALU.add).then_inc(S["v_free"], 1)
                v.wait_ge(S["v_free"], vj[0])
                steps(v.tensor_reduce(sc8[:, 0:8].rearrange("p (c h) -> p c h", c=2)[:, :, 0:nh],
                                      sm_[:].rearrange("p c (h k) -> p c h k", h=nh), AX.X, ALU.max))
                nm = sc8[:, 8:16].rearrange("p (c h) -> p c h", c=2)[:, :, 0:nh]
                steps(v.tensor_scalar(nm, sc8[:, 0:8].rearrange("p (c h) -> p c h", c=2)[:, :, 0:nh], -SCALE, None, ALU.mult))
                v.sem_inc(S["nmx_ok"], 1)
                v.wait_ge(S["ex_ok"], exps[r + 1])
                sv = sc8[:, 16:24].rearrange("p (c h) -> p c h", c=2)[:, :, 0:nh]
                steps(v.reciprocal(sv, sv))
                steps(v.tensor_scalar(sv[:, 1], sv[:, 1], lamv[:, 5:6], None, ALU.mult))
                e4 = ex[:].rearrange("p c (h k) -> p c h k", h=nh)
                am3 = am.rearrange("p (h k) -> p h k", h=nh)
                if r:
                    v.wait_ge(S["a_free"], amw[r])
                v.tensor_tensor(am3, e4[:, 0], bc(sv[:, 0], 2, K), ALU.mult)
                steps(v.tensor_tensor(e4[:, 1], e4[:, 1], bc(sv[:, 1], 2, K), ALU.mult))
                steps(v.tensor_tensor(am3, am3, e4[:, 1], ALU.add))
                v.sem_inc(S["am_ok"], 1)
            v.wait_ge(S["a_free"], amw[6] + 1)
            oa4 = oa.rearrange("p t (h e) -> p t h e", h=H)
            steps(v.tensor_tensor(osq, oa, oa, ALU.mult))
            for t in range(TT):
                steps(v.tensor_reduce(sc8[:, 24 + 8 * t:32 + 8 * t], osq[:, t].rearrange("p (h e) -> p h e", h=H), AX.X, ALU.add))
            steps(v.tensor_scalar(sc8[:, 24:40], sc8[:, 24:40], 1.0 / P, SUBLN_EPS, ALU.mult, ALU.add))
            v.sem_inc(S["osq_ok"], 1)
            steps(v.tensor_scalar(subw[:], subw[:], 1.0 - LAMBDA_INIT, None, ALU.mult))
            v.wait_ge(S["ort_ok"], 1)
            steps(v.reciprocal(sc8[:, 40:56], sc8[:, 40:56]))
            for t in range(TT):
                steps(v.tensor_tensor(oa4[:, t], oa4[:, t], bc(sc8[:, 40 + 8 * t:48 + 8 * t], 2, P), ALU.mult))
                steps(v.tensor_tensor(oa4[:, t], oa4[:, t], bc(subw[:], 1, H), ALU.mult))
            v.sem_inc(S["oa_ok"], 1)
            g1 = r45[:, 2048:4096].rearrange("p (t c) -> p t c", t=TT)
            v.wait_ge(S["yp_in"], 16 * 8)
            v.wait_ge(S["d_in"], 16)
            steps(v.tensor_tensor(g0, z_t[:, :, 0:W], bc(d_b, 1, TT), ALU.mult))
            steps(v.tensor_tensor(yg, yg, g0, ALU.add))
            steps(v.tensor_tensor(g0, yg, yg, ALU.mult))
            steps(v.tensor_scalar(g0, g0, GELU_C, 1.0, ALU.mult, ALU.add))
            steps(v.tensor_tensor(g0, g0, yg, ALU.mult))
            v.sem_inc(S["gel_in"], 1)
            v.wait_ge(S["gel_sig"], 1)
            steps(v.tensor_tensor(yg, yg, g1, ALU.mult))
            v.sem_inc(S["gelu_ok"], 1)
            lo = [0, 0]

            def low(n):
                for _ in range(n):
                    hc = lo[0]
                    lo[0] += 1
                    v.wait_ge(S["hi_ok"], hc + 1)
                    v.tensor_tensor(ring_r[:, raw_half(hc)], ring[:, raw_half(hc)], r45_r[:, hi_slot(hc)].bitcast(F32),
                                    ALU.subtract).then_inc(S["lo_ok"], 1)

            def low_x(hi, lo2, n_banks):
                for n in range(n_banks):
                    m = LO_A0 + lo[1]
                    lo[1] += 1
                    v.wait_ge(S["a_free"], m + 1)
                    v.tensor_tensor(lo2[n], pb[6 + m % 2][:].rearrange("p (k t) -> p k t", k=2),
                                    hi[:, 2 * n:2 * n + 2].bitcast(F32), ALU.subtract).then_inc(S["alo_ok"], 1)

            low_x(oT_hi, oT_lo2, 4)
            low_x(yT_hi, yT_lo2, 4)
            low(4)
            v.wait_ge(S["gb_in"], 16)
            for n in range(2):
                if n == 1:
                    low(1)
                for t in range(TT):
                    v.wait_ge(S["blk_ready"], 33 + 2 * n + t)
                    v.tensor_tensor(g0[:, t, n * BLK:(n + 1) * BLK], pb[2 * n + t][:],
                                    glu_bb[:, n * BLK:(n + 1) * BLK], ALU.add).then_inc(S["out_free"], 1)
                v.wait_ge(S["out_free"], 2 * n + 2)
                v.sem_inc(S["glu_pre"], 1)
            low(1)
            for n in range(2):
                v.wait_ge(S["glu_sig"], n + 1)
                ins = v.tensor_tensor(yg[:, :, n * BLK:(n + 1) * BLK], yg[:, :, n * BLK:(n + 1) * BLK],
                                      g0[:, :, n * BLK:(n + 1) * BLK], ALU.mult)
            steps(ins)
            v.sem_inc(S["y2_ok"], 1)
            low(2)
            low_x(yT_hi, yT_lo2, 4)
            for n in range(4):
                cols = slice(n * BLK, (n + 1) * BLK)
                for t in range(TT):
                    v.wait_ge(S["blk_ready"], 37 + 4 * n + t)
                    v.tensor_tensor(ga_t[:, t, cols], ga_t[:, t, cols], pb[t][:], ALU.mult).then_inc(S["out_free"], 1)
                low(2)
                for t in range(TT):
                    v.wait_ge(S["blk_ready"], 39 + 4 * n + t)
                    v.tensor_tensor(gs_t[:, t, cols], gs_t[:, t, cols], pb[2 + t][:], ALU.mult).then_inc(S["out_free"], 1)
                v.wait_ge(S["out_free"], 8 + 4 * n)
                for t in range(TT):
                    ins = v.tensor_tensor(gs_t[:, t, cols], gs_t[:, t, cols], ga_t[:, t, cols], ALU.add)
                steps(ins)
                if n < 3:
                    low(2)
            v.sem_inc(S["mrg_ok"], 1)
            low_x(mT_hi, mT_lo2, 8)
            g8 = rs[:, 0:16].rearrange("p (t e) -> p t e", t=TT)
            v.wait_ge(S["iota_ok"], 1)
            v.tensor_reduce(q32, ident[:].rearrange("p (g s) -> p s g", g=4), AX.X, ALU.add)
            steps(v.memset(rs[:, 0:16], -3.0e38))

            def h2T_out(n):
                for i in range(2):
                    bank = v_bank()
                    v.tensor_tensor(h2T[n][:, 2 * i:2 * i + 2], bank[:].rearrange("p (k t) -> p k t", k=2),
                                    bc(w2c[:, 4 * n + 2 * i:4 * n + 2 * i + 2], 2, T), ALU.mult).then_inc(S["v_free"], 1)

            v.wait_ge(S["x_again"], 32)
            for n in range(4):
                low(4 if n < 3 else 2)
                for t in range(TT):
                    v.wait_ge(S["blk_ready"], 53 + 2 * n + t)
                    cols = slice(n * BLK, (n + 1) * BLK)
                    v.tensor_tensor(h2[:, t, cols], x_t[:, t, cols], pb[2 * (n % 2) + t][:], ALU.add).then_inc(S["out_free"], 1)
                if n:
                    h2T_out(n - 1)
            v.wait_ge(S["ss2_done"], 8)
            steps(v.tensor_reduce(ss[:, 0:2], sq8, AX.X, ALU.add))
            steps(v.tensor_scalar(ss[:, 2:4], ss[:, 0:2], 1.0 / D, NORM_EPS, ALU.mult, ALU.add))
            v.sem_inc(S["root2_done"], 1)
            h2T_out(3)
            v.wait_ge(S["ss2_done"], 9)
            steps(v.reciprocal(ss[:, 6:8], ss[:, 4:6]))
            rstd = ss[:, 6:8]
            m8 = rs[:, 16:32].rearrange("p (t e) -> p t e", t=TT)
            x8 = rs[:, 32:48].bitcast(U32).rearrange("p (t e) -> p t e", t=TT)
            gidx = rs[:, 80:82]
            oh = rs[:, 84:92].rearrange("p (t g) -> p t g", t=TT)
            es = rs[:, 96:112].rearrange("p (t e) -> p t e", t=TT)
            pr = rs[:, 112:176].rearrange("p (t g e) -> p t g e", t=TT, g=NG)
            v8 = rs[:, 176:192].rearrange("p (t e) -> p t e", t=TT)
            y8 = rs[:, 192:208].bitcast(U32).rearrange("p (t e) -> p t e", t=TT)
            eid = rs[:, 208:212].rearrange("p (t k) -> p t k", t=TT)
            mk = rs[:, 212:340].rearrange("p (t k e) -> p t k e", t=TT, k=2)
            mm = rs[:, 340:404].rearrange("p (t e) -> p t e", t=TT)
            rk = rs[:, 404:532].rearrange("p (a e) -> p a e", a=4)
            cnt = rs[:, 532:564]
            nb = rs[:, 564:596]
            be = rs[:, 596:628]
            bs = rs[:, 628:660]
            cm = rs[:, 660:916].rearrange("p (e j) -> p e j", j=8)
            pk = rs[:, 916:1044].rearrange("p (t k e) -> p t k e", t=TT, k=2)
            bsm = rs[:, 1044:1076]
            cmp3 = rs[:, 1076:1172].rearrange("p (j e) -> p j e", j=3)
            cols4 = rs[:, 1172:1176]
            lgc = rs[:, 1176:1178]
            v.wait_ge(S["lg_ps"], 1)
            for t in range(TT):
                v.tensor_scalar(g8[:, t, 0:NG], pb[6 + t][:, 0:NG], rstd[:, t:t + 1], None, ALU.mult)
            for t in range(TT):
                ins = v.tensor_scalar(lg[:, t], pb[6 + t][:, NG:NG + NE], rstd[:, t:t + 1], None, ALU.mult)
            steps(ins)
            for t in range(TT):
                ins = v.max(m8[:, t], g8[:, t])
            steps(ins)
            for t in range(TT):
                ins = v.max_index(x8[:, t], m8[:, t], g8[:, t])
            steps(ins)
            steps(v.tensor_copy(gidx, x8[:, :, 0]))
            for t in range(TT):
                v.tensor_scalar(rs[:, 48 + 4 * t:52 + 4 * t], g8[:, t, 0:NG], m8[:, t, 0:1], None, ALU.subtract)
                ins = v.tensor_scalar(oh[:, t], iota[:, 0, 0:NG], gidx[:, t:t + 1], None, ALU.is_equal)
            steps(ins)
            for t in range(TT):
                ins = v.tensor_tensor(pr[:, t], lg[:, t].rearrange("p (g e) -> p g e", g=NG), bc(oh[:, t], 2, EPG), ALU.mult)
            steps(ins)
            for t in range(TT):
                ins = v.tensor_reduce(es[:, t], pr[:, t].rearrange("p g e -> p e g"), AX.X, ALU.add)
            steps(ins)
            for t in range(TT):
                ins = v.max(v8[:, t], es[:, t])
            steps(ins)
            for t in range(TT):
                ins = v.max_index(y8[:, t], v8[:, t], es[:, t])
            steps(ins)
            v.tensor_tensor(rs[:, 56:58], v8[:, :, 1], v8[:, :, 0], ALU.subtract)
            steps(v.tensor_copy(eid, y8[:, :, 0:2]))
            v.sem_inc(S["gex_in"], 1)
            steps(v.scalar_tensor_tensor(eid, bc(gidx, 2, 2), float(EPG), eid, ALU.mult, ALU.add))
            for t in range(TT):
                for k in range(2):
                    ins = v.tensor_scalar(mk[:, t, k], iota[:, 0], eid[:, t, k:k + 1], None, ALU.is_equal)
            steps(ins)
            steps(v.tensor_tensor(mm, mk[:, :, 0], mk[:, :, 1], ALU.add))
            v.sem_inc(S["m_ok"], 1)
            v.wait_ge(S["gex_ok"], 1)
            v.tensor_reduce(rs[:, 76:78], rs[:, 64:72].rearrange("p (t g) -> p t g", t=TT), AX.X, ALU.add)
            steps(v.tensor_scalar(rs[:, 78:80], rs[:, 72:74], 1.0, None, ALU.add))
            steps(v.tensor_tensor(rs[:, 76:78], rs[:, 76:78], rs[:, 78:80], ALU.mult))
            steps(v.reciprocal(gw[:, :, 0], rs[:, 76:78]))
            v.wait_ge(S["cnt_ps"], 1)
            steps(v.tensor_copy(rs[:, 404:532], pb[1][:, 0:128]))
            v.tensor_tensor(gw[:, :, 1], gw[:, :, 0], rs[:, 72:74], ALU.mult)
            v.tensor_tensor(rk[:, 1], rk[:, 1], rk[:, 2], ALU.add)
            steps(v.tensor_tensor(cnt, rk[:, 2], rk[:, 3], ALU.add))
            steps(v.tensor_tensor(cm, bc(cnt, 2, 8), bc(thr, 1, NE), ALU.is_gt))
            steps(v.tensor_reduce(nb, cm, AX.X, ALU.add))
            steps(v.tensor_scalar(nb[:, 0:1], nb[:, 0:1], 1.0, None, ALU.max))
            steps(v.tensor_tensor_scan(be, ones[:, 0:NE], nb, 0.0, ALU.mult, ALU.add))
            steps(v.tensor_tensor(bs, be, nb, ALU.subtract))
            steps(v.scalar_tensor_tensor(rk[:, 0:2], bc(bs, 1, 2), float(CAP), rk[:, 0:2], ALU.mult, ALU.add))
            for t in range(TT):
                ins = v.tensor_tensor(pk[:, t], mk[:, t], bc(rk[:, t], 1, 2), ALU.mult)
            steps(ins)
            steps(v.tensor_reduce(rem, pk, AX.X, ALU.add))
            istep = S["istep"]

            def selection():
                for t in range(TT):
                    v.tensor_scalar(sel[:, t], iota[:, 0], rem[:, t, 0:1], rstd[:, t:t + 1], ALU.is_equal, ALU.mult)
                    last = v.tensor_scalar(sela[:, t], iota[:, 0], rem[:, t, 1:2], rstd[:, t:t + 1], ALU.is_equal, ALU.mult)
                return last

            selection().then_inc(istep, 1)
            v.wait_ge(istep, 1)
            v.tensor_tensor(sel, sel, sela, ALU.add).then_inc(S["sel_ok"], 1)
            steps(v.tensor_scalar(bsm, nb, 0.0, 1000.0, ALU.is_equal, ALU.mult))
            steps(v.tensor_tensor(bsm, bsm, bs, ALU.add))
            v.tensor_scalar(cmp3[:, 0], be, pidx[:, 0:1], None, ALU.is_le)
            v.tensor_scalar(cmp3[:, 1], bsm, pidx[:, 0:1], None, ALU.is_le)
            steps(v.tensor_scalar(cmp3[:, 2], bsm, pidx[:, 1:2], None, ALU.is_le))
            steps(v.tensor_reduce(cols4[:, 0:3], cmp3, AX.X, ALU.add))
            v.tensor_copy(cols4[:, 3:4], be[:, NE - 1:NE])
            steps(v.tensor_tensor(cols4[:, 2:3], cols4[:, 1:2], cols4[:, 2:3], ALU.subtract))
            v.sem_inc(S["tabc_ok"], 1)
            v.wait_ge(S["tab_ps"], 1)
            steps(v.tensor_copy(tab4, pb[4][0:1, 0:4 * MAXI]))
            v.sem_inc(S["tab_ok"], 1)

            def xT_out():
                v.tensor_tensor(xT, pb[1][:].rearrange("p (j n s) -> p j n s", j=4, n=4),
                                bc(w2c.rearrange("p (n j) -> p j n", j=4), 3, CAP), ALU.mult).then_inc(S["xt_sb"], 1)

            v.wait_ge(S["xt_ps"], 1)
            xT_out()
            n_items = v.value_load(tab_n[:, 0:1], min_val=1, max_val=MAXI)
            v.sem_inc(S["up_sb"], 1)
            v.sem_inc(S["sc_free"], 1)
            v.wait_ge(S["acc_ok"], 8)
            with v.Fori(0, n_items) as i:
                v.wait_ge(S["swt_ps"], i + 1)
                v.wait_ge(S["sc_free"], i * 8 + 1)
                for t in range(TT):
                    v.tensor_scalar(swr[:, t], iota, rem[:, t, 0:1], gw[:, t, 0:1], ALU.is_equal, ALU.mult)
                    last = v.tensor_scalar(swa[:, t], iota, rem[:, t, 1:2], gw[:, t, 1:2], ALU.is_equal, ALU.mult)
                last.then_inc(istep, 1)
                v.wait_ge(istep, i * 3 + 2)
                v.tensor_tensor(swr, swr, swa, ALU.add).then_inc(S["swr_ok"], 1)
                v.tensor_scalar(rem, rem, float(CAP), None, ALU.subtract).then_inc(istep, 1)
                v.wait_ge(istep, i * 3 + 3)
                v.wait_ge(S["xg_ps"], i + 1)
                selection().then_inc(istep, 1)
                v.wait_ge(istep, i * 3 + 4)
                v.tensor_tensor(sel, sel, sela, ALU.add).then_inc(S["sel_ok"], 1)
                v.wait_ge(S["up_ps"], i + 1)
                v.tensor_copy(gu[:, 1], pb[3][:]).then_inc(S["up_sb"], 1)
                v.wait_ge(S["swt_ps"], i + 2)
                v.tensor_copy(swt, pb[5][:, 0:T]).then_inc(S["swt_sb"], 1)
                v.wait_ge(S["xt_ps"], i + 2)
                xT_out()
                v.wait_ge(S["sig_ok"], i + 1)
                aTf = aTe.rearrange("p k s -> p (k s)")
                v.tensor_tensor(sge, sge, pb[4][:, 0:P], ALU.mult).then_inc(S["si_ok"], 1)
                v.wait_ge(S["si_ok"], i + 1)
                v.tensor_tensor(aTf, sge, pb[4][:, P:2 * P], ALU.mult).then_inc(S["at_ok"], 1)
                for n in range(4):
                    for t in range(TT):
                        m = 2 * n + t
                        v.wait_ge(S["sc_ps"], i * 8 + m + 2)
                        xs = x_t[:, t, n * BLK:(n + 1) * BLK]
                        v.tensor_tensor(xs, xs, pb[(7, 1)[m % 2]][:], ALU.add).then_inc(S["sc_free"], 1)
            v.wait_ge(S["sc_free"], n_items * 8 + 1)
            v.sem_inc(S["moe_ok"], 1)
            v.wait_ge(S["fss_done"], 2)
            steps(v.tensor_scalar(ss[:, 2:4], ss[:, 0:2], 1.0 / D, NORM_EPS, ALU.mult, ALU.add))
            v.sem_inc(S["froot_done"], 1)
            v.wait_ge(S["fss_done"], 3)
            steps(v.reciprocal(ss[:, 6:8], ss[:, 4:6]))
            v.wait_ge(S["fw_in"], 16)
            for t in range(TT):
                v.scalar_tensor_tensor(x_t[:, t, :], x_t[:, t, :], ss[:, 6 + t:7 + t], bcw[:],
                                       ALU.mult, ALU.mult).then_inc(S["out_ok"], 1)

        @block.tensor
        def _(pe):
            vj, aj = [0], [0]

            def v_bank():
                n = vj[0]
                vj[0] += 1
                if n >= 2:
                    pe.wait_ge(S["v_free"], n - 1)
                return pb[4 + n % 2]

            def a_bank():
                n = aj[0]
                aj[0] += 1
                if n >= 2:
                    pe.wait_ge(S["a_free"], n - 1)
                return pb[6 + n % 2]

            pe.wait_ge(S["ident_ok"], 1)
            pe.wait_ge(S["x_in"], 32)
            xs = x_t.rearrange("p t (d k) -> p t d k", k=KT)
            for n in range(8):
                bank = v_bank()
                for k in range(2):
                    for t in range(TT):
                        ins = pe.transpose(bank[:, (2 * k + t) * P:(2 * k + t + 1) * P], xs[:, t, :, 2 * n + k], ident[:])
                ins.then_inc(S["v_ready"], 1)

            def parameters():
                pe.wait_ge(S["lam_in"], 16 * 8)
                pe.wait_ge(S["dt_spread"], 1)
                bank = v_bank()
                for n in range(3):
                    ins = pe.transpose(bank[:, 32 * n:32 * n + 32], p32[:, n * P:(n + 1) * P], ident[0:32, 0:32])
                ins.then_inc(S["v_ready"], 1)
                pe.wait_ge(S["c_in"], 16 * 16)
                for c in range(2):
                    bank = a_bank()
                    for g in range(4):
                        ins = pe.transpose(bank[:, g * P:(g + 1) * P], cn[:, c, g, :], ident[:])
                    ins.then_inc(S["a_ready"], 1)

            def w_in_chunk(k):
                b, c = k // 2, k % 2
                b0 = 2 * (b % 2)
                if c == 0 and b >= 2:
                    pe.wait_ge(S["blk_free"], 2 * (b - 1))
                for p in range(PPC * k, PPC * (k + 1)):
                    pe.wait_ge(S["wlo_ok"], p + 1)
                    w_hi = ring_r[:, hi_piece(p)].rearrange("p (k n) -> p k n", k=PK)
                    w_lo = ring_r[:, raw_piece(p)].rearrange("p (k n) -> p k n", k=PK)
                    for kk in range(PK):
                        kt = PK * (p % (2 * PPC)) + kk
                        for t in range(TT):
                            x_hi = ht_r[:, kt * T + t * P:kt * T + (t + 1) * P]
                            x_lo = hT_lo[kt][:, t * P:(t + 1) * P]
                            for j, (x_, w_) in enumerate(((x_hi, w_hi), (x_hi, w_lo), (x_lo, w_hi))):
                                ins = pe.matmul(pb[b0 + t][:], x_, w_[:, kk, :], start=(kt == 0 and j == 0),
                                                stop=(kt == KT - 1 and j == 2))
                            if kt == KT - 1:
                                ins.then_inc(S["blk_ready"], 1)
                    if kt < KT - 1:
                        ins.then_inc(S["piece_used"], 1)
                if c == 1:
                    pe.wait_ge(S["blk_ready"], 2 * b + 2)
                    pe.sem_inc(S["piece_used"], 1)

            def u_turn():
                pe.wait_ge(S["up_ok"], 1)
                for n in range(4):
                    bank = a_bank()
                    for g in range(4):
                        ins = pe.transpose(bank[:, g * P:(g + 1) * P], up[:, 4 * n + g].rearrange("p i m -> p (i m)"), ident[:])
                    ins.then_inc(S["a_ready"], 1)
                pe.wait_ge(S["a_ready"], aj[0])
                pe.sem_inc(S["ut_ok"], 1)
                pe.wait_ge(S["cbd_ok"], 1)

            def stage_a(q):
                pe.wait_ge(S["bp_ok"], q + 1)
                for n in range(4):
                    bank = a_bank()
                    for r in range(2):
                        for c in range(2):
                            ins = pe.transpose(bank[:, (2 * r + c) * P:(2 * r + c + 1) * P],
                                               bp[:, c, 2 * n + r].rearrange("p i m -> p (i m)"), ident[:])
                    ins.then_inc(S["a_ready"], 1)
                bank = v_bank()
                for r in range(QP):
                    nat = (r // 2) * 8 + 2 * q + r % 2
                    for c in range(2):
                        ins = pe.matmul(bank[:, r * 32:(r + 1) * 32], bp[:, c, r].rearrange("p i m -> p (i m)"),
                                        cbd[:, c, nat].rearrange("p h m -> p (h m)"), start=(c == 0), stop=(c == 1))
                ins.then_inc(S["v_ready"], 1)
                pe.wait_ge(S["v_ready"], vj[0])
                pe.sem_inc(S["bp_used"], 1)
                pe.wait_ge(S["a_free"], aj[0])
                for c in range(2):
                    bank = v_bank()
                    for r in range(QP):
                        g0_ = 4 * q + 2 * (r % 2)
                        ins = pe.matmul(bank[:, r * 64:(r + 1) * 64].rearrange("p (h j) -> p h j", h=2), bt[:, r, c, :],
                                        ut[:, g0_:g0_ + 2, r // 2, :], start=True, stop=True)
                    ins.then_inc(S["v_ready"], 1)
                pe.wait_ge(S["v_ready"], vj[0])
                pe.sem_inc(S["s_used"], 1)

            def stage_c(q):
                pe.wait_ge(S["sbd_ok"], 1)
                pe.wait_ge(S["tq_in"], 16 * L * (q + 1))
                pe.wait_ge(S["ca_ok"], q + 1)
                bank = a_bank()
                for gq in range(4):
                    r2, h = gq // 2, gq % 2
                    for part in range(3):
                        for f in range(4):
                            dst = bank[32 * f:32 * f + 32, gq * P:(gq + 1) * P]
                            r = 2 * f + r2
                            if part == 0:
                                rhs = tq[:, :, r * 32 + h * SM:r * 32 + h * SM + SM]
                                ins = pe.matmul(dst.rearrange("p (i m) -> p i m", i=L), ut[:, 4 * q + gq, f, :], rhs,
                                                start=True, stop=False)
                            else:
                                ins = pe.matmul(dst, sbd[:, part - 1, h, q * QP + r, :],
                                                bp[:, part - 1, r].rearrange("p i m -> p (i m)"),
                                                start=False, stop=(part == 2))
                ins.then_inc(S["a_ready"], 1)
                pe.wait_ge(S["a_ready"], aj[0])
                pe.sem_inc(S["ca_used"], 1)
                pe.sem_inc(S["tq_used"], 1)
                if q == NQ - 1:
                    pe.wait_ge(S["a_free"], aj[0])
                    pe.sem_inc(S["yp_ok"], 1)

            def qk_turn():
                pe.wait_ge(S["qk_rot"], 1)
                for n in range(8):
                    bank = a_bank()
                    for k in range(2):
                        for t in range(TT):
                            hh = 2 * n + k
                            ins = pe.transpose(bank[:, (2 * k + t) * P:(2 * k + t + 1) * P], qk[:, t, hh * P:(hh + 1) * P], ident[:])
                    ins.then_inc(S["a_ready"], 1)
                pe.wait_ge(S["a_free"], aj[0])

            def scores(r):
                nh, K = (4, P) if r < 2 else (2, 2 * P)
                t = 0 if r < 2 else 1
                h0 = 4 * r if r < 2 else 2 * (r - 2)
                for c in range(2):
                    bank = v_bank()
                    rows = slice(64 * c, 64 * c + 64)
                    for h in range(nh):
                        ins = pe.matmul(bank[:, h * K:(h + 1) * K], qkT[rows, h0 + h, t * P:(t + 1) * P],
                                        qkT[rows, H + h0 + h, 0:K], start=True, stop=True)
                    ins.then_inc(S["v_ready"], 1)

            def round_(r):
                nh, K = (4, P) if r < 2 else (2, 2 * P)
                h0 = 4 * r if r < 2 else 2 * (r - 2)
                if r < 5:
                    scores(r + 1)
                pe.wait_ge(S["am_ok"], r + 1)
                bank = a_bank()
                for n in range(4):
                    ins = pe.transpose(bank[:, n * P:(n + 1) * P], am[:, n * P:(n + 1) * P], ident[:])
                ins.then_inc(S["a_ready"], 1)
                pe.wait_ge(S["a_free"], aj[0])
                bank = a_bank()
                nk = K // P
                for h in range(nh):
                    for k in range(nk):
                        ins = pe.matmul(bank[:, h * P:(h + 1) * P], aT[:, (h * nk + k) * P:(h * nk + k + 1) * P],
                                        z_t[:, k, 3 * W + (h0 + h) * P:3 * W + (h0 + h + 1) * P],
                                        start=(k == 0), stop=(k == nk - 1))
                ins.then_inc(S["a_ready"], 1)

            lo = [0]

            def turn(src, nk):
                sv = src.rearrange("p t (c k) -> p t c k", k=nk)
                for n in range(nk // 2):
                    bank = a_bank()
                    if lo[0] >= 2:
                        pe.wait_ge(S["alo_ok"], lo[0] - 1)
                    lo[0] += 1
                    for k in range(2):
                        for t in range(TT):
                            ins = pe.transpose(bank[:, (2 * k + t) * P:(2 * k + t + 1) * P], sv[:, t, :, 2 * n + k], ident[:])
                    ins.then_inc(S["a_ready"], 1)

            def half_product(hc, hi, low_, kt0, b0, first, last):
                pe.wait_ge(S["lo_ok"], hc + 1)
                w_hi = r45_r[:, hi_slot(hc)].rearrange("p (k n) -> p k n", k=HK)
                w_lo = ring_r[:, raw_half(hc)].rearrange("p (k n) -> p k n", k=HK)
                for kk in range(HK):
                    for t in range(TT):
                        x_hi = hi[:, kt0 + kk, t * P:(t + 1) * P]
                        x_lo = low_[kt0 + kk][:, t * P:(t + 1) * P]
                        for j, (x_, w_) in enumerate(((x_hi, w_hi), (x_hi, w_lo), (x_lo, w_hi))):
                            ins = pe.matmul(pb[b0 + t][:], x_, w_[:, kk, :], start=(first and kk == 0 and j == 0),
                                            stop=(last and kk == HK - 1 and j == 2))
                        if last and kk == HK - 1:
                            ins.then_inc(S["blk_ready"], 1)
                if not last:
                    ins.then_inc(S["half_used"], 1)

            pe.wait_ge(S["hl_ok"], 8)
            for c in range(N_WIN):
                w_in_chunk(c)
                if c == 0:
                    parameters()
                if c == PE_A[0]:
                    u_turn()
                if c in PE_A:
                    stage_a(PE_A.index(c))
                if c in PE_C:
                    stage_c(PE_C.index(c))
                if c == PE_QK:
                    qk_turn()
                    scores(0)
                if 0 <= c - PE_ROUND < 6:
                    round_(c - PE_ROUND)
            pe.wait_ge(S["oa_ok"], 1)
            turn(oa, WK)
            pe.wait_ge(S["a_ready"], aj[0])
            pe.sem_inc(S["xfree"], 1)
            pe.wait_ge(S["gelu_ok"], 1)
            turn(yg, WK)
            assert aj[0] == LO_A0 + 8
            pe.wait_ge(S["alo_ok"], lo[0])
            hc = 0
            for n in range(2):
                pe.wait_ge(S["blk_free"], 30 + 2 * n)
                for c in range(2):
                    half_product(hc, yT_hi, yT_lo, c * HK, 2 * n, c == 0, c == 1)
                    hc += 1
                pe.wait_ge(S["blk_ready"], 32 + 2 * n + 2)
                pe.sem_inc(S["half_used"], 1)
                pe.sem_inc(S["chunk_used"], 1)
            br = 36
            for n in range(4):
                for hi, low_, b0 in ((oT_hi, oT_lo, 0), (yT_hi, yT_lo, 2)):
                    pe.wait_ge(S["out_free"], 4 * n + b0 + 2)
                    if n == 0 and b0 == 2:
                        pe.wait_ge(S["y2_ok"], 1)
                        turn(yg, WK)
                        pe.wait_ge(S["alo_ok"], lo[0])
                    for c in range(2):
                        half_product(hc, hi, low_, c * HK, b0, c == 0, c == 1)
                        hc += 1
                    br += 2
                    pe.wait_ge(S["blk_ready"], br)
                    pe.sem_inc(S["half_used"], 1)
                    pe.sem_inc(S["chunk_used"], 1)
            pe.wait_ge(S["mrg_ok"], 1)
            turn(gs_t, KT)
            pe.wait_ge(S["a_ready"], aj[0])
            pe.sem_inc(S["mT_ps"], 1)
            pe.wait_ge(S["alo_ok"], lo[0])
            turned = {}

            def h2_turn(n):
                pe.wait_ge(S["out_free"], 22 + 2 * n)
                for i in range(2):
                    bank = v_bank()
                    for k in range(2):
                        for t in range(TT):
                            ins = pe.transpose(bank[:, (2 * k + t) * P:(2 * k + t + 1) * P], h2b[n][:, t, 2 * i + k, :], ident[:])
                    ins.then_inc(S["v_ready"], 1)
                turned[n] = vj[0]

            def logits(n):
                pe.wait_ge(S["v_free"], turned[n])
                if n == 0:
                    pe.wait_ge(S["rw_in"], 16 * 8)
                for k in range(4):
                    for t in range(TT):
                        ins = pe.matmul(pb[6 + t][:, 0:NG + NE], h2T[n][:, k, t * P:(t + 1) * P], rwv[:, 4 * n + k, :],
                                        start=(n == 0 and k == 0), stop=(n == 3 and k == 3))
                if n == 3:
                    ins.then_inc(S["lg_ps"], 1)

            h2b = [h2[:, :, n * BLK:(n + 1) * BLK].rearrange("p t (d j) -> p t j d", j=4) for n in range(4)]
            for n in range(4):
                b0 = 2 * (n % 2)
                pe.wait_ge(S["out_free"], 20 if n < 2 else 20 + 2 * (n - 1))
                for c in range(4):
                    half_product(hc, mT_hi, mT_lo, c * HK, b0, c == 0, c == 3)
                    hc += 1
                    if c == 1:
                        pe.wait_ge(S["half_used"], hc)
                        pe.sem_inc(S["chunk_used"], 1)
                pe.wait_ge(S["blk_ready"], 52 + 2 * n + 2)
                pe.sem_inc(S["half_used"], 1)
                pe.sem_inc(S["chunk_used"], 1)
                if n >= 1:
                    h2_turn(n - 1)
                if n >= 2:
                    logits(n - 2)
            h2_turn(3)
            logits(2)
            logits(3)
            pe.wait_ge(S["m_ok"], 1)
            mmr = rs[:, 340:404]
            pe.matmul(pb[1][:, 0:64], lt, mmr, start=True, stop=True)
            pe.matmul(pb[1][:, 64:128], ones, mmr, start=True, stop=True).then_inc(S["cnt_ps"], 1)

            def gather():
                for t in range(TT):
                    for n in range(4):
                        ins = pe.matmul(pb[0][32 * n:32 * n + 32, :].rearrange("p (j d) -> p j d", j=4), sel[:, t],
                                        h2b[n][:, t], start=(t == 0), stop=(t == TT - 1))
                ins.then_inc(S["xg_ps"], 1)

            def gather_turn():
                for j in range(4):
                    ins = pe.transpose(pb[1][:, j * P:(j + 1) * P], xg[:, j * P:(j + 1) * P], ident[:])
                ins.then_inc(S["xt_ps"], 1)

            pe.wait_ge(S["sel_ok"], 1)
            gather()
            pe.wait_ge(S["tabc_ok"], 1)
            for j in range(4):
                ins = pe.transpose(pb[4][0:1, MAXI * j:MAXI * (j + 1)], rs[0:MAXI, 1172 + j:1173 + j], ident[0:MAXI, 0:MAXI])
            ins.then_inc(S["tab_ps"], 1)
            pe.wait_ge(S["xg_sb"], 1)
            gather_turn()
            pe.wait_ge(S["tab_ok"], 1)
            n_items = pe.value_load(tab_n[:, 0:1], min_val=1, max_val=MAXI)
            pe.sem_inc(S["swt_ps"], 1)
            pe.sem_inc(S["sc_ps"], 1)
            with pe.Fori(0, n_items) as i:
                loads = pe.value_load(tab_l[:, bass.ds(i, 1)], min_val=1, max_val=NE)
                pe.wait_ge(S["xt_sb"], i + 1)
                for part in range(2):
                    pe.wait_ge(S[("gate_sb", "up_sb")[part]], i + 1)
                    for c in range(2):
                        s_ = EXP_SLOT[2 * part + c]
                        pe.wait_ge(full[s_], loads * 16 + 16 * FILLS[s_])
                        wv = chunk3(s_)
                        for kk in range(CH):
                            kt = c * CH + kk
                            g_ = kt % 4
                            ins = pe.matmul(pb[2 + part][32 * g_:32 * g_ + 32, :], xT[:, kt % 4, kt // 4, :], wv[:, kk, :],
                                            start=(kt < 4), stop=(kt >= KT - 4))
                        ins.then_inc(S["item_chunk"], 1)
                    pe.wait_ge(S["item_chunk"], i * 6 + 2 * part + 2)
                    pe.sem_inc(S[("gate_ps", "up_ps")[part]], 1)
                pe.wait_ge(S["sel_ok"], i + 2)
                gather()
                pe.wait_ge(S["gate_sb"], i + 2)
                pe.wait_ge(S["up_sb"], i + 2)
                for part in range(2):
                    gv = gu[:, part].rearrange("p (f k) -> p f k", k=FK)
                    for k in range(FK):
                        ins = pe.matmul(pb[4][:, part * P + k * CAP:part * P + (k + 1) * CAP], gv[:, :, k], q32,
                                        start=True, stop=True)
                ins.then_inc(S["sum_ps"], 1)
                pe.wait_ge(S["swr_ok"], i + 1)
                for t in range(TT):
                    ins = pe.transpose(pb[5][:, t * P:(t + 1) * P], swr[:, t].rearrange("p a s -> p (a s)"), ident[:])
                ins.then_inc(S["swt_ps"], 1)
                pe.wait_ge(S["xg_sb"], i + 2)
                pe.wait_ge(S["sc_free"], i * 8 + 1)
                gather_turn()
                for c in (4, 5):
                    s_ = EXP_SLOT[c]
                    pe.wait_ge(full[s_], loads * 16 + 16 * FILLS[s_])
                pe.wait_ge(S["at_ok"], i + 1)
                for n in range(4):
                    if n >= 2:
                        pe.wait_ge(S["dn_sb"], i * 4 + n - 1)
                    for k in range(FK):
                        wv = slot(EXP_SLOT[4 + k // 2]).rearrange("p (k n) -> p k n", k=2)
                        ins = pe.matmul(pb[5 + n % 2][32 * k:32 * k + 32, :], aTe[:, k, :], wv[:, k % 2, n * BLK:(n + 1) * BLK],
                                        start=True, stop=True)
                    ins.then_inc(S["dn_ps"], 1)
                pe.wait_ge(S["dn_ps"], i * 4 + 4)
                pe.sem_inc(S["item_chunk"], 2)
                pe.wait_ge(S["swt_sb"], i + 1)
                pe.wait_ge(S["xt_sb"], i + 2)
                for n in range(4):
                    pe.wait_ge(S["dn_sb"], i * 4 + n + 1)
                    for t in range(TT):
                        m = 2 * n + t
                        if m >= 2:
                            pe.wait_ge(S["sc_free"], i * 8 + m)
                        pe.matmul(pb[(7, 1)[m % 2]][:], swt[:, t * P:(t + 1) * P], ys[:, n], start=True, stop=True).then_inc(S["sc_ps"], 1)


def kernel(**inputs):
    import numpy as np
    import concourse.bacc as bacc
    from concourse.bass_utils import run_bass_kernel_spmd

    nc = bacc.Bacc("TRN2", target_bir_lowering=False, num_devices=1)
    arrays, aps = {}, {}
    given = {k: np.ascontiguousarray(x) for k, x in inputs.items()}
    given["inv_freq"] = (1.0 / (np.float32(10000.0) ** (np.arange(0, HD, 2, dtype=np.float32) / np.float32(HD)))).astype(np.float32)
    for name, x in given.items():
        arrays[f"in_{name}"] = x
        aps[name] = nc.dram_tensor(f"in_{name}", x.shape, mybir.dt.from_np(x.dtype), kind="ExternalInput").ap()
    out = nc.dram_tensor("out_0", (1, T, D), F32, kind="ExternalOutput").ap()
    hybrid_block(nc, aps, out)
    r = run_bass_kernel_spmd(nc, [arrays], core_ids=[0])
    return r.results[0]["out_0"]
```
